# Optimizing a Trainium2 kernel written in Bass

```python
import math
import jax, jax.numpy as jnp
from jax import lax
import numpy as np

D_MODEL = 1024
BATCH = 1
SEQ = 256
DEPTH = 2

CHUNK = 64
MEM_LEN = 256
N_MIXERS = 2
N_A = (DEPTH + 1) // 2
N_B = DEPTH // 2

D_LRU = D_MODEL // 2
LRU_BLOCKS = 8
LRU_BLK = D_LRU // LRU_BLOCKS
CONV_WIDTH = 4
LRU_C = 8.0

FOX_HEADS = 8
FOX_HD = 64
FOX_WIDTH = FOX_HEADS * FOX_HD
Q_BLOCK = 128

XA_HEADS = 4
XA_HD = 128
XA_WIDTH = XA_HEADS * XA_HD

D_FF = 4 * D_MODEL
EPS = 1e-6
NEG_INF = -1e30


def rms_norm(x, g):
    xf = x.astype(jnp.float32)
    y = xf * lax.rsqrt(jnp.mean(xf * xf, axis=-1, keepdims=True) + EPS)
    return (y * g.astype(jnp.float32)).astype(x.dtype)

def _lin_combine(left, right):
    a1, b1 = left
    a2, b2 = right
    return a1 * a2, a2 * b1 + b2

def rglru_group(h, w_in, conv_w, conv_b, w_r, b_r, w_i, b_i, lam):
    B, S, _ = h.shape
    proj = h @ w_in
    u, gate, xq = jnp.split(proj, [D_LRU, 2 * D_LRU], axis=-1)
    u = lax.conv_general_dilated(
        u, conv_w[:, None, :].astype(u.dtype), window_strides=(1,),
        padding=[(CONV_WIDTH - 1, 0)], dimension_numbers=("NWC", "WIO", "NWC"),
        feature_group_count=D_LRU) + conv_b
    ub = u.reshape(B, S, LRU_BLOCKS, LRU_BLK)
    r = jax.nn.sigmoid(jnp.einsum("bsnc,ncd->bsnd", ub, w_r).reshape(B, S, D_LRU) + b_r)
    i = jax.nn.sigmoid(jnp.einsum("bsnc,ncd->bsnd", ub, w_i).reshape(B, S, D_LRU) + b_i)
    log_a = -LRU_C * r.astype(jnp.float32) * jax.nn.softplus(-lam.astype(jnp.float32))
    a = jnp.exp(log_a)
    b = jnp.sqrt(-jnp.expm1(2.0 * log_a)) * (i.astype(jnp.float32) * u.astype(jnp.float32))
    _, hs = lax.associative_scan(_lin_combine, (a, b), axis=1)
    y = hs.astype(h.dtype) * jax.nn.gelu(gate, approximate=True)
    return y, xq

def fox_group(h, w_in, b_f, q_gain, k_gain):
    B, S, _ = h.shape
    n_qb = S // Q_BLOCK
    proj = h @ w_in
    q, k, v, f_logit, xq = jnp.split(
        proj, [FOX_WIDTH, 2 * FOX_WIDTH, 3 * FOX_WIDTH, 3 * FOX_WIDTH + FOX_HEADS], axis=-1)
    q = rms_norm(q.reshape(B, S, FOX_HEADS, FOX_HD), q_gain)
    k = rms_norm(k.reshape(B, S, FOX_HEADS, FOX_HD), k_gain)
    v = v.reshape(B, S, FOX_HEADS, FOX_HD)
    log_f = jax.nn.log_sigmoid(f_logit.astype(jnp.float32) + b_f.astype(jnp.float32))
    c = jnp.cumsum(log_f, axis=1).transpose(0, 2, 1)
    kh = k.transpose(0, 2, 1, 3)
    vh = v.transpose(0, 2, 1, 3)
    q_blocks = q.reshape(B, n_qb, Q_BLOCK, FOX_HEADS, FOX_HD).transpose(1, 0, 3, 2, 4)
    c_blocks = c.reshape(B, FOX_HEADS, n_qb, Q_BLOCK).transpose(2, 0, 1, 3)
    q_pos = jnp.arange(S, dtype=jnp.int32).reshape(n_qb, Q_BLOCK)
    k_pos = jnp.arange(S, dtype=jnp.int32)
    scale = 1.0 / math.sqrt(FOX_HD)

    def one_block(args):
        qb, cb, pos = args
        s = jnp.einsum("bhqd,bhkd->bhqk", qb, kh).astype(jnp.float32) * scale
        s = s + cb[..., :, None] - c[:, :, None, :]
        s = jnp.where(pos[:, None] >= k_pos[None, :], s, NEG_INF)
        p = jax.nn.softmax(s, axis=-1)
        return jnp.einsum("bhqk,bhkd->bhqd", p.astype(vh.dtype), vh)

    o = lax.map(one_block, (q_blocks, c_blocks, q_pos))
    o = o.transpose(1, 0, 3, 2, 4).reshape(B, S, FOX_WIDTH)
    return o, xq

def memory_group(xq, mem, g_mem, w_kv, q_gain, k_gain):
    B, S, _ = xq.shape
    M = mem.shape[1]
    kv = rms_norm(mem, g_mem) @ w_kv
    k, v = jnp.split(kv, [XA_WIDTH], axis=-1)
    q = rms_norm(xq.reshape(B, S, XA_HEADS, XA_HD), q_gain)
    k = rms_norm(k.reshape(B, M, XA_HEADS, XA_HD), k_gain)
    v = v.reshape(B, M, XA_HEADS, XA_HD)
    s = jnp.einsum("bshd,bmhd->bhsm", q, k).astype(jnp.float32) * (1.0 / math.sqrt(XA_HD))
    p = jax.nn.softmax(s, axis=-1)
    o = jnp.einsum("bhsm,bmhd->bshd", p.astype(v.dtype), v)
    return o.reshape(B, S, XA_WIDTH)

def sqrelu_mlp(h, w1, w2):
    return jnp.square(jax.nn.relu(h @ w1)) @ w2

def first_inputs(seed: int = 0) -> dict:
    key = jax.random.key(seed)
    ks = jax.random.split(key, 32)
    f32 = jnp.float32

    def nrm(k, shape, fan_in):
        return jax.random.normal(k, shape, f32) * (fan_in ** -0.5)

    def gain(k, shape):
        return 1.0 + 0.05 * jax.random.normal(k, shape, f32)

    def small(k, shape):
        return 0.02 * jax.random.normal(k, shape, f32)

    x = jax.random.normal(ks[0], (BATCH, SEQ, D_MODEL), f32)
    mem = jax.random.normal(ks[1], (BATCH, MEM_LEN, D_MODEL), f32)
    a_c = jax.random.uniform(ks[2], (N_A, D_LRU), f32, 0.9, 0.999)
    s_lam = a_c ** (1.0 / LRU_C)
    lru_lambda = jnp.log(s_lam) - jnp.log1p(-s_lam)
    return {
        "x": x,
        "mem": mem,
        "norm_mix": gain(ks[3], (DEPTH, D_MODEL)),
        "norm_mem": gain(ks[4], (DEPTH, D_MODEL)),
        "w_mem_kv": nrm(ks[5], (DEPTH, D_MODEL, 2 * XA_WIDTH), D_MODEL),
        "xa_q_gain": gain(ks[6], (DEPTH, XA_HD)),
        "xa_k_gain": gain(ks[7], (DEPTH, XA_HD)),
        "w_out": nrm(ks[8], (DEPTH, D_LRU + XA_WIDTH, D_MODEL), D_LRU + XA_WIDTH),
        "norm_mlp": gain(ks[9], (DEPTH, D_MODEL)),
        "w_mlp_in": nrm(ks[10], (DEPTH, D_MODEL, D_FF), D_MODEL),
        "w_mlp_out": nrm(ks[11], (DEPTH, D_FF, D_MODEL), D_FF),
        "w_in_a": nrm(ks[12], (N_A, D_MODEL, 2 * D_LRU + XA_WIDTH), D_MODEL),
        "conv_w": nrm(ks[13], (N_A, CONV_WIDTH, D_LRU), CONV_WIDTH),
        "conv_b": small(ks[14], (N_A, D_LRU)),
        "w_rgate": nrm(ks[15], (N_A, LRU_BLOCKS, LRU_BLK, LRU_BLK), LRU_BLK),
        "b_rgate": small(ks[16], (N_A, D_LRU)),
        "w_igate": nrm(ks[17], (N_A, LRU_BLOCKS, LRU_BLK, LRU_BLK), LRU_BLK),
        "b_igate": small(ks[18], (N_A, D_LRU)),
        "lru_lambda": lru_lambda,
        "w_in_b": nrm(ks[19], (N_B, D_MODEL, 3 * FOX_WIDTH + FOX_HEADS + XA_WIDTH), D_MODEL),
        "b_forget": jax.random.uniform(ks[20], (N_B, FOX_HEADS), f32, 1.0, 6.0),
        "fox_q_gain": gain(ks[21], (N_B, FOX_HD)),
        "fox_k_gain": gain(ks[22], (N_B, FOX_HD)),
    }

def first_block(x, mem, norm_mix, norm_mem, w_mem_kv, xa_q_gain, xa_k_gain, w_out,
              norm_mlp, w_mlp_in, w_mlp_out, w_in_a, conv_w, conv_b, w_rgate, b_rgate,
              w_igate, b_igate, lru_lambda, w_in_b, b_forget, fox_q_gain, fox_k_gain):
    for layer in range(DEPTH):
        h = rms_norm(x, norm_mix[layer])
        j = layer // N_MIXERS
        if layer % N_MIXERS == 0:
            y_mix, xq = rglru_group(h, w_in_a[j], conv_w[j], conv_b[j], w_rgate[j], b_rgate[j],
                                    w_igate[j], b_igate[j], lru_lambda[j])
        else:
            y_mix, xq = fox_group(h, w_in_b[j], b_forget[j], fox_q_gain[j], fox_k_gain[j])
        y_mem = memory_group(xq, mem, norm_mem[layer], w_mem_kv[layer],
                             xa_q_gain[layer], xa_k_gain[layer])
        x = x + jnp.concatenate([y_mix, y_mem], axis=-1) @ w_out[layer]
        x = x + sqrelu_mlp(rms_norm(x, norm_mlp[layer]), w_mlp_in[layer], w_mlp_out[layer])
    return x


HG_HEADS = 4
HG_DIM = 128
HG_WIDTH = HG_HEADS * HG_DIM
HG_CHUNK = 64
NSA_HEADS = 8
NSA_KV_HEADS = 2
NSA_GROUP = NSA_HEADS // NSA_KV_HEADS
NSA_DIM = 64
NSA_WIDTH = NSA_HEADS * NSA_DIM
NSA_KV_WIDTH = NSA_KV_HEADS * NSA_DIM
CMP_LEN = 32
CMP_STRIDE = 16
CMP_HIDDEN = 256
SLC_LEN = 64
SLC_TOP = 16
SLC_QBLOCK = 32
WINDOW = 512
SWA_QBLOCK = 128
N_BRANCH = 3
MIX_WIDTH = HG_WIDTH + NSA_WIDTH
D_FF_2 = ((8 * D_MODEL + 3 * 256 - 1) // (3 * 256)) * 256
ROPE_THETA = 10000.0
RMS_EPS = 1e-6
NEG = -1e30
FORCED_SCORE = 1e9
IN_SPLITS = (HG_WIDTH, HG_WIDTH, HG_WIDTH, HG_WIDTH, NSA_WIDTH,
             NSA_KV_WIDTH, NSA_KV_WIDTH, NSA_KV_WIDTH, NSA_KV_WIDTH, NSA_KV_WIDTH, NSA_KV_WIDTH,
             NSA_HEADS * N_BRANCH)
IN_WIDTH = sum(IN_SPLITS)
IN_SPLIT_POINTS = tuple(int(v) for v in np.cumsum(IN_SPLITS)[:-1])


def rms_norm_2(x, gain):
    xf = x.astype(jnp.float32)
    y = xf * lax.rsqrt(jnp.mean(xf * xf, axis=-1, keepdims=True) + RMS_EPS)
    return (y * gain.astype(jnp.float32)).astype(x.dtype)

def rope(x, pos):
    half = x.shape[-1] // 2
    freqs = ROPE_THETA ** (-jnp.arange(half, dtype=jnp.float32) / half)
    ang = pos.astype(jnp.float32)[:, None] * freqs[None, :]
    cos = jnp.cos(ang)[:, None, :]
    sin = jnp.sin(ang)[:, None, :]
    xf = x.astype(jnp.float32)
    x1, x2 = xf[..., :half], xf[..., half:]
    return jnp.concatenate([x1 * cos - x2 * sin, x1 * sin + x2 * cos], axis=-1).astype(x.dtype)

def hgrn2_mixer(q, f_logit, i, g, lower_bound, g_norm):
    B, T, _ = q.shape
    dt = q.dtype
    n_chunk = T // HG_CHUNK
    lb = lower_bound.astype(jnp.float32)
    f = lb + (1.0 - lb) * jax.nn.sigmoid(f_logit.astype(jnp.float32))
    log_f = jnp.log(f)
    k = 1.0 - f
    qf = jax.nn.silu(q.astype(jnp.float32))
    v = i.astype(jnp.float32)

    def to_chunks(a):
        return a.reshape(B, n_chunk, HG_CHUNK, HG_HEADS, HG_DIM).transpose(1, 0, 3, 2, 4)

    causal = jnp.tril(jnp.ones((HG_CHUNK, HG_CHUNK), dtype=bool))[:, :, None]

    def step(S, xs):
        qc, kc, vc, lfc = xs
        b = jnp.cumsum(lfc, axis=2)
        diff = b[:, :, :, None, :] - b[:, :, None, :, :]
        decay = jnp.exp(jnp.where(causal, diff, -jnp.inf))
        A = jnp.einsum('bhtd,bhsd,bhtsd->bhts', qc, kc, decay)
        o = (jnp.einsum('bhts,bhsv->bhtv', A, vc)
             + jnp.einsum('bhtd,bhdv->bhtv', qc * jnp.exp(b), S))
        b_last = b[:, :, -1:, :]
        S = (jnp.exp(b_last[:, :, 0, :])[..., None] * S
             + jnp.einsum('bhsd,bhsv->bhdv', kc * jnp.exp(b_last - b), vc))
        return S, o

    S0 = jnp.zeros((B, HG_HEADS, HG_DIM, HG_DIM), jnp.float32)
    _, o = lax.scan(step, S0, (to_chunks(qf), to_chunks(k), to_chunks(v), to_chunks(log_f)))
    o = o.transpose(1, 0, 3, 2, 4).reshape(B, T, HG_HEADS, HG_DIM)
    o = rms_norm_2(o, g_norm) * jax.nn.silu(g.astype(jnp.float32).reshape(B, T, HG_HEADS, HG_DIM))
    return o.reshape(B, T, HG_WIDTH).astype(dt)

def compress(a, pe, w1, w2):
    B, T, G, d = a.shape
    R = CMP_LEN // CMP_STRIDE
    n_cmp = (T - CMP_LEN) // CMP_STRIDE + 1
    seg = a.reshape(B, T // CMP_STRIDE, CMP_STRIDE, G, d)
    blocks = jnp.concatenate([seg[:, r:r + n_cmp] for r in range(R)], axis=2)
    blocks = blocks + pe[None, None, :, None, :]
    flat = blocks.transpose(0, 1, 3, 2, 4).reshape(B, n_cmp, G, CMP_LEN * d)
    return jax.nn.silu(flat @ w1) @ w2

def cmp_to_slc_matrix(T):
    n_cmp = (T - CMP_LEN) // CMP_STRIDE + 1
    n_slc = T // SLC_LEN
    c_start = np.arange(n_cmp) * CMP_STRIDE
    c_end = c_start + CMP_LEN - 1
    s_start = np.arange(n_slc) * SLC_LEN
    s_end = s_start + SLC_LEN - 1
    M = (c_start[:, None] <= s_end[None, :]) & (c_end[:, None] >= s_start[None, :])
    return jnp.asarray(M.astype(np.float32))

def nsa_mixer(q, k_cmp, v_cmp, k_slc, v_slc, k_swa, v_swa, gate_logit, q_gain, k_gain,
              pe_k, w1_k, w2_k, pe_v, w1_v, w2_v):
    B, T, _ = q.shape
    dt = q.dtype
    H, G, Hg, d = NSA_HEADS, NSA_KV_HEADS, NSA_GROUP, NSA_DIM
    pos = jnp.arange(T)
    scale = d ** -0.5
    qr = rope(rms_norm_2(q.reshape(B, T, H, d), q_gain), pos)
    qg = qr.reshape(B, T, G, Hg, d)

    def kv_heads(a):
        return a.reshape(B, T, G, d)

    kc = compress(kv_heads(k_cmp), pe_k, w1_k, w2_k)
    vc = compress(kv_heads(v_cmp), pe_v, w1_v, w2_v)
    n_cmp = kc.shape[1]
    cmp_end = jnp.arange(n_cmp) * CMP_STRIDE + CMP_LEN - 1
    kc = rope(rms_norm_2(kc, k_gain[0]), cmp_end)
    s = jnp.einsum('btghd,bngd->bghtn', qg, kc).astype(jnp.float32) * scale
    m_cmp = cmp_end[None, :] <= pos[:, None]
    p_cmp = jax.nn.softmax(jnp.where(m_cmp, s, NEG), axis=-1) * m_cmp
    o_cmp = jnp.einsum('bghtn,bngd->btghd', p_cmp.astype(dt), vc)

    n_slc = T // SLC_LEN
    imp = jnp.einsum('bghtn,nj->bgtj', p_cmp, cmp_to_slc_matrix(T))
    blk = jnp.arange(n_slc)
    cur = pos // SLC_LEN
    forced = (blk[None, :] == 0) | (blk[None, :] == cur[:, None]) | (blk[None, :] == cur[:, None] - 1)
    causal_blk = blk[None, :] <= cur[:, None]
    score = jnp.where(forced, FORCED_SCORE, jnp.where(causal_blk, imp, NEG))
    top = min(SLC_TOP, n_slc)
    _, idx = lax.top_k(score, top)

    ks = rope(rms_norm_2(kv_heads(k_slc), k_gain[1]), pos)
    kb = ks.reshape(B, n_slc, SLC_LEN, G, d).transpose(0, 3, 1, 2, 4)
    vb = kv_heads(v_slc).reshape(B, n_slc, SLC_LEN, G, d).transpose(0, 3, 1, 2, 4)
    nq = T // SLC_QBLOCK
    q_blocks = qg.reshape(B, nq, SLC_QBLOCK, G, Hg, d).transpose(1, 0, 3, 4, 2, 5)
    idx_blocks = idx.reshape(B, G, nq, SLC_QBLOCK, top).transpose(2, 0, 1, 3, 4)
    t_blocks = pos.reshape(nq, SLC_QBLOCK)
    bi = jnp.arange(B)[:, None, None, None]
    gi = jnp.arange(G)[None, :, None, None]
    tok = jnp.arange(SLC_LEN)

    def slc_block(xs):
        qb, ib, tb = xs
        kg = kb[bi, gi, ib]
        vg = vb[bi, gi, ib]
        sb = jnp.einsum('bghqd,bgqnsd->bghqns', qb, kg).astype(jnp.float32) * scale
        kpos = ib[..., None] * SLC_LEN + tok
        mb = (kpos <= tb[None, None, :, None, None])[:, :, None]
        sb = jnp.where(mb, sb, NEG)
        pb = jax.nn.softmax(sb.reshape(B, G, Hg, SLC_QBLOCK, -1), axis=-1).reshape(sb.shape)
        return jnp.einsum('bghqns,bgqnsd->bghqd', pb.astype(dt), vg)

    o_slc = lax.map(slc_block, (q_blocks, idx_blocks, t_blocks))
    o_slc = o_slc.transpose(1, 0, 4, 2, 3, 5).reshape(B, T, G, Hg, d)

    kw = rope(rms_norm_2(kv_heads(k_swa), k_gain[2]), pos)
    vw = kv_heads(v_swa)
    kpad = jnp.pad(kw, ((0, 0), (WINDOW, 0), (0, 0), (0, 0)))
    vpad = jnp.pad(vw, ((0, 0), (WINDOW, 0), (0, 0), (0, 0)))
    nw = T // SWA_QBLOCK
    span = WINDOW + SWA_QBLOCK
    qw_blocks = qg.reshape(B, nw, SWA_QBLOCK, G, Hg, d).transpose(1, 0, 3, 4, 2, 5)

    def swa_block(xs):
        qb, n = xs
        start = n * SWA_QBLOCK
        kblk = lax.dynamic_slice_in_dim(kpad, start, span, axis=1)
        vblk = lax.dynamic_slice_in_dim(vpad, start, span, axis=1)
        tq = start + jnp.arange(SWA_QBLOCK)
        tk = start - WINDOW + jnp.arange(span)
        mw = (tk[None, :] <= tq[:, None]) & (tk[None, :] > tq[:, None] - WINDOW) & (tk[None, :] >= 0)
        sw = jnp.einsum('bghqd,bkgd->bghqk', qb, kblk).astype(jnp.float32) * scale
        pw = jax.nn.softmax(jnp.where(mw, sw, NEG), axis=-1)
        return jnp.einsum('bghqk,bkgd->bghqd', pw.astype(dt), vblk)

    o_swa = lax.map(swa_block, (qw_blocks, jnp.arange(nw)))
    o_swa = o_swa.transpose(1, 0, 4, 2, 3, 5).reshape(B, T, G, Hg, d)

    gate = jax.nn.sigmoid(gate_logit.astype(jnp.float32)).reshape(B, T, G, Hg, N_BRANCH)
    o = (gate[..., 0:1] * o_cmp.astype(jnp.float32)
         + gate[..., 1:2] * o_slc.astype(jnp.float32)
         + gate[..., 2:3] * o_swa.astype(jnp.float32))
    return o.reshape(B, T, NSA_WIDTH).astype(dt)

def second_inputs(seed: int = 0) -> dict:
    key = jax.random.key(seed)
    ks = jax.random.split(key, 20)

    def dense(k, shape, fan_in):
        return jax.random.normal(k, shape, jnp.float32) * fan_in ** -0.5

    def gain(k, shape):
        return 1.0 + 0.05 * jax.random.normal(k, shape, jnp.float32)

    return {
        'x': jax.random.normal(ks[0], (BATCH, SEQ, D_MODEL), jnp.float32),
        'w_in': dense(ks[1], (DEPTH, D_MODEL, IN_WIDTH), D_MODEL),
        'w_out': dense(ks[2], (DEPTH, MIX_WIDTH, D_MODEL), MIX_WIDTH),
        'hg_lb_logits': 0.1 * jax.random.normal(ks[3], (DEPTH, HG_WIDTH), jnp.float32),
        'hg_gnorm': gain(ks[4], (DEPTH, HG_DIM)),
        'q_gain': gain(ks[5], (DEPTH, NSA_DIM)),
        'k_gain': gain(ks[6], (DEPTH, N_BRANCH, NSA_DIM)),
        'cmp_pe_k': 0.1 * jax.random.normal(ks[7], (DEPTH, CMP_LEN, NSA_DIM), jnp.float32),
        'cmp_w1_k': dense(ks[8], (DEPTH, CMP_LEN * NSA_DIM, CMP_HIDDEN), CMP_LEN * NSA_DIM),
        'cmp_w2_k': dense(ks[9], (DEPTH, CMP_HIDDEN, NSA_DIM), CMP_HIDDEN),
        'cmp_pe_v': 0.1 * jax.random.normal(ks[10], (DEPTH, CMP_LEN, NSA_DIM), jnp.float32),
        'cmp_w1_v': dense(ks[11], (DEPTH, CMP_LEN * NSA_DIM, CMP_HIDDEN), CMP_LEN * NSA_DIM),
        'cmp_w2_v': dense(ks[12], (DEPTH, CMP_HIDDEN, NSA_DIM), CMP_HIDDEN),
        'w_ffn_in': dense(ks[13], (DEPTH, D_MODEL, 2 * D_FF_2), D_MODEL),
        'w_ffn_out': dense(ks[14], (DEPTH, D_FF_2, D_MODEL), D_FF_2),
        'norm_mix': gain(ks[15], (DEPTH, D_MODEL)),
        'norm_ffn': gain(ks[16], (DEPTH, D_MODEL)),
    }

def second_block(x, w_in, w_out, hg_lb_logits, hg_gnorm, q_gain, k_gain,
              cmp_pe_k, cmp_w1_k, cmp_w2_k, cmp_pe_v, cmp_w1_v, cmp_w2_v,
              w_ffn_in, w_ffn_out, norm_mix, norm_ffn):
    lb = jnp.cumsum(jax.nn.softmax(hg_lb_logits.astype(jnp.float32), axis=0), axis=0)
    lb = lb - lb[0:1]
    h = x
    for l in range(DEPTH):
        xn = rms_norm_2(h, norm_mix[l])
        proj = xn @ w_in[l]
        (hq, hf, hi, hg, nq, kc, vc, ksl, vsl, ksw, vsw, ngate) = jnp.split(proj, IN_SPLIT_POINTS, axis=-1)
        o_hg = hgrn2_mixer(hq, hf, hi, hg, lb[l], hg_gnorm[l])
        o_nsa = nsa_mixer(nq, kc, vc, ksl, vsl, ksw, vsw, ngate, q_gain[l], k_gain[l],
                          cmp_pe_k[l], cmp_w1_k[l], cmp_w2_k[l], cmp_pe_v[l], cmp_w1_v[l], cmp_w2_v[l])
        mix = jnp.concatenate([o_hg, o_nsa], axis=-1)
        h = h + mix @ w_out[l]
        xn = rms_norm_2(h, norm_ffn[l])
        gu = xn @ w_ffn_in[l]
        g_ff, u_ff = gu[..., :D_FF_2], gu[..., D_FF_2:]
        h = h + (jax.nn.silu(g_ff) * u_ff) @ w_ffn_out[l]
    return h


def setup_inputs(seed=0):
    out = dict(first_inputs(seed))
    for name, value in second_inputs(seed + 1).items():
        if name != "x":
            out[name + "_2"] = value
    return out


def reference(
    x, mem, norm_mix, norm_mem, w_mem_kv, xa_q_gain, xa_k_gain, w_out, norm_mlp, w_mlp_in,
    w_mlp_out, w_in_a, conv_w, conv_b, w_rgate, b_rgate, w_igate, b_igate, lru_lambda, w_in_b,
    b_forget, fox_q_gain, fox_k_gain, w_in_2, w_out_2, hg_lb_logits_2, hg_gnorm_2, q_gain_2,
    k_gain_2, cmp_pe_k_2, cmp_w1_k_2, cmp_w2_k_2, cmp_pe_v_2, cmp_w1_v_2, cmp_w2_v_2,
    w_ffn_in_2, w_ffn_out_2, norm_mix_2, norm_ffn_2,
):
    x = first_block(
        x, mem, norm_mix, norm_mem, w_mem_kv, xa_q_gain, xa_k_gain, w_out, norm_mlp, w_mlp_in,
        w_mlp_out, w_in_a, conv_w, conv_b, w_rgate, b_rgate, w_igate, b_igate, lru_lambda,
        w_in_b, b_forget, fox_q_gain, fox_k_gain,
    )
    return second_block(
        x, w_in_2, w_out_2, hg_lb_logits_2, hg_gnorm_2, q_gain_2, k_gain_2, cmp_pe_k_2,
        cmp_w1_k_2, cmp_w2_k_2, cmp_pe_v_2, cmp_w1_v_2, cmp_w2_v_2, w_ffn_in_2, w_ffn_out_2,
        norm_mix_2, norm_ffn_2,
    )


_drawn_inputs = setup_inputs


def setup_inputs(seed=0):
    import zlib

    import numpy as np

    out = dict(_drawn_inputs(seed))
    spreads = {}
    factors = {'norm_mem': 7.459,
     'xa_q_gain': 8.0,
     'xa_k_gain': 8.0,
     'b_rgate': 31.944,
     'b_igate': 26.403,
     'fox_q_gain': 8.0,
     'fox_k_gain': 8.0,
     'hg_lb_logits_2': 28.389,
     'hg_gnorm_2': 12.535,
     'q_gain_2': 8.0,
     'k_gain_2': 8.0,
     'cmp_pe_k_2': 8.0,
     'cmp_pe_v_2': 12.547,
     'b_forget': 30.8,
     'norm_ffn_2': 6.295}
    for name, (base, spread) in spreads.items():
        noise = np.random.default_rng([zlib.crc32(name.encode()), seed]).standard_normal(out[name].shape)
        drawn = base * np.exp(spread * noise) if base else spread * noise
        out[name] = __import__('jax').numpy.asarray(drawn.astype(out[name].dtype))
    for name, factor in factors.items():
        out[name] = (out[name] * factor).astype(out[name].dtype)
    return out
```

```python
from contextlib import ExitStack

import concourse.bass as bass
import numpy as np
from concourse import mybir

ACT = mybir.ActivationFunctionType
ALU = mybir.AluOpType
AX = mybir.AxisListType
F32 = mybir.dt.float32
F32R = mybir.dt.float32r
U32 = mybir.dt.uint32

P = 128
T = 256
TT = T // P
D = 1024
KT = D // P
EPS = 1e-6
NEG = -1e30
BLK = 512
UNIT = 1024
NRAW = 8
NSPLIT = 4
AHEAD = NSPLIT - 1
NSLOT = 12
SLOT = 1040
MLP_BLOCKS = 4 * D // BLK
D_FF2 = 2816
FFN_HALF = BLK // 2
FFN_BLOCKS = D_FF2 // FFN_HALF
NCMP = (T - 32) // 16 + 1
LEVELS = 8
NSMALL = 1130

CONST = {}
_at = 0
for _n, _w in (("ident", 128), ("mask", 256), ("tri", 128), ("ones", 128), ("cos", 64), ("sin", 64), ("ccos", 32),
               ("csin", 32), ("cadd", 2 * NCMP), ("cmul", 2 * NCMP), ("hmask", 7 * 64), ("bd", 8)):
    CONST[_n] = (_at, _w)
    _at += _w
NCONST = _at
ROWG = {}
_at = 0
for _n, _w in (("xaq0", 128), ("xak0", 128), ("xaq1", 128), ("xak1", 128), ("foxq", 64), ("foxk", 64), ("bf", 8),
               ("gn2", 128), ("q2", 64), ("k2", 192), ("gn3", 128), ("q3", 64), ("k3", 192)):
    ROWG[_n] = (_at, _w)
    _at += _w
NROWG = _at
COLG = {}
_at = 0
for _n, _w in (("cw", 16), ("cb", 4), ("br", 4), ("bi", 4), ("lam", 4), ("lb", 8), ("pe2", 32), ("pe3", 32)):
    COLG[_n] = (_at, _w)
    _at += _w
NCOLG = _at


def bc(ap, axis, n):
    v = ap.unsqueeze(axis)
    shape = list(v.shape)
    shape[axis] = n
    return v.broadcast_to(shape)


class Fill:

    def __init__(self, bank, turn):
        self.bank, self.turn, self.pos = bank, turn, None


def program(nc, a):
    ctx = ExitStack()
    with ctx:
        def sb(name, shape, dt=F32):
            return ctx.enter_context(nc.sbuf_tensor(name, shape, dt))

        def sem(name):
            return ctx.enter_context(nc.semaphore(name))

        x = sb("x", [P, TT, D])
        xn = sb("xn", [P, TT, D])
        XT = (sb("XT_hi", [P, KT, T], F32R), sb("XT_lo", [P, KT, T], F32R))
        MX = (sb("MX_hi", [P, KT, T], F32R), sb("MX_lo", [P, KT, T], F32R))
        HT = (sb("HT_hi", [P, 2, 4, T], F32R), sb("HT_lo", [P, 2, 4, T], F32R))
        raw = sb("raw", [P, NRAW, UNIT])
        whi = sb("whi", [P, NSPLIT, UNIT], F32R)
        wlo = sb("wlo", [P, NSPLIT, UNIT], F32R)
        gain = sb("gain", [P, 2, D])
        hrow = sb("hrow", [P, TT, BLK])
        scr = sb("scr", [P, NSLOT * SLOT])
        const = sb("const", [P, NCONST])
        rowg = sb("rowg", [P, NROWG])
        colg = sb("colg", [P, NCOLG])
        w2c = sb("w2c", [P, 2, 2, 2, 64])
        powc = sb("powc", [P, 16])
        small = sb("small", [P, NSMALL])
        PS = [ctx.enter_context(nc.psum_tensor(f"ps{i}", [P, BLK], F32)) for i in range(8)]

        def slot(i, w):
            return scr[:, i * SLOT:i * SLOT + w]

        def cst(name, lo=0, w=None):
            at, full = CONST[name]
            return const[:, at + lo:at + lo + (full if w is None else w)]

        def rg(name, lo=0, w=None):
            at, full = ROWG[name]
            return rowg[:, at + lo:at + lo + (full if w is None else w)]

        def cg(name, lo=0, w=None):
            at, full = COLG[name]
            return colg[:, at + lo:at + lo + (full if w is None else w)]

        ident = cst("ident")
        small_at = {}

        def sm(name, w):
            if name not in small_at:
                at = sum(v for _, v in small_at.values())
                assert at + w <= NSMALL, name
                small_at[name] = (at, w)
            at, w0 = small_at[name]
            assert w0 == w, name
            return small[:, at:at + w]

        landed = [sem(f"landed{i}") for i in range(NRAW)]
        split_hi = sem("split_hi")
        split_lo = sem("split_lo")
        unit_used = sem("unit_used")
        bank_full = [sem(f"bank_full{i}") for i in range(8)]
        bank_free = [sem(f"bank_free{i}") for i in range(8)]
        turn_hi = sem("turn_hi")
        events = {}

        def ev(name):
            if name not in events:
                events[name] = sem("ev_" + name)
            return events[name]

        counts = {}

        def chain(eng, name, ins):
            counts[name] = counts.get(name, 0) + 1
            ins.then_inc(ev(name), 1)
            eng.wait_ge(ev(name), counts[name])

        def steps_of(H, causal):
            steps = []
            for tt in range(TT):
                klen = (tt + 1) * P if causal else T
                n = BLK // klen
                steps += [(tt, h0, n, klen) for h0 in range(0, H, n)]
            return steps

        fills = {}
        per_bank = [0] * 8
        units = []
        state = {"pos": 0}

        def open_fill(name, bank):
            per_bank[bank] += 1
            assert name not in fills, name
            fills[name] = Fill(bank, per_bank[bank])
            return fills[name]

        MEM = ({"xq": 3, "mk": 5, "mv": 6, "qT": 9, "kT": 11}, {"xq": 3, "mk": 5, "mv": 6, "qT": 8, "kT": 10})
        PROBS = {"ma0": 3, "ma1": 0, "fa": 0, "sl2": 0, "sw2": 0, "sl3": 0, "sw3": 0}
        TURNED = {"ma0": 5, "ma1": 1, "fa": 1, "sl2": 1, "sw2": 1, "sl3": 1, "sw3": 1}
        MASKED = {"fa": 4, "sl2": 10, "sw2": 10, "sl3": 10, "sw3": 10}

        def ring(table, tag, i):
            return scr[:, table[tag] * SLOT + (i % 2) * BLK:table[tag] * SLOT + (i % 2 + 1) * BLK]

        def probs(tag, i):
            return ring(PROBS, tag, i)

        def turned(tag, i):
            return ring(TURNED, tag, i)

        def masked(tag, i):
            return ring(MASKED, tag, i)

        def cpT(tt):
            return slot(5, 1024)[:, tt * P:(tt + 1) * P]

        MIXED = {0: ["mo0.0", "mo0.1"], 1: ["fo.0", "fo.1", "mo1.0", "mo1.1"]}
        for L_ in (2, 3):
            MIXED[L_] = [f"hr{L_}.0", f"hr{L_}.1", f"nr{L_}.0", f"nr{L_}.1"]

        block = ctx.enter_context(nc.Block())

        @block.tensor
        def _(pe):
            def fill(name, bank):
                f = open_fill(name, bank)
                if f.turn > 1:
                    pe.wait_ge(bank_free[bank], f.turn - 1)
                return PS[bank]

            def close(name, ins):
                f = fills[name]
                ins.then_inc(bank_full[f.bank], 1)
                f.pos = state["pos"]

            def read_out(name):
                pe.wait_ge(bank_free[fills[name].bank], fills[name].turn)

            def unit(src, nk):
                g = state["pos"]
                units.append(src)
                state["pos"] = g + 1
                pe.wait_ge(split_lo, g + 1)
                w = src.shape[1] // nk
                hi = whi[:, g % NSPLIT, 0:nk * w].rearrange("p (k n) -> p k n", k=nk)
                lo = wlo[:, g % NSPLIT, 0:nk * w].rearrange("p (k n) -> p k n", k=nk)
                return g, hi, lo, w

            def products(out, xh, xl, wh, wl, first, last, begun=None):
                m = pe.matmul(out, xh, wh, start=first, stop=False)
                if begun is not None:
                    m.then_inc(unit_used, begun)
                pe.matmul(out, xh, wl, start=False, stop=False)
                return pe.matmul(out, xl, wh, start=False, stop=last)

            def tok(pair):
                return lambda k, tt: (pair[0][:, k, tt * P:(tt + 1) * P], pair[1][:, k, tt * P:(tt + 1) * P])

            def linear(names, banks, srcs, nk, lhs, k0=0, kn=None, opened=True, closed=True):
                kn = len(srcs) * nk if kn is None else kn
                outs = [PS[fills[n].bank] if not opened else fill(n, b) for n, b in zip(names, banks)]
                for i, src in enumerate(srcs):
                    g, hi, lo, w = unit(src, nk)
                    for j in range(nk):
                        k = i * nk + j
                        for tt, name in enumerate(names):
                            xh, xl = lhs(k0 + k, tt)
                            begun = 1 if j == 0 and tt == 0 and g else None
                            last = closed and k == kn - 1
                            m = products(outs[tt][:, 0:w], xh, xl, hi[:, j], lo[:, j],
                                         opened and k == 0, last, begun)
                            if last:
                                close(name, m)

            def turn(name, bank, tiles):
                out = fill(name, bank)
                at = 0
                for t in tiles:
                    p, f = t.shape
                    m = pe.transpose(out[0:f, at:at + p], t, ident[0:p, 0:p])
                    at += P
                close(name, m)

            def turn_norm(L, k):
                for tt in range(TT):
                    pe.wait_ge(ev("xn"), 2 * k + tt + 1)
                    for h in range(2):
                        turn(f"n{k}.{tt}.{h}", 6 + h,
                             [xn[:, tt, (4 * h + j) * P:(4 * h + j + 1) * P] for j in range(4)])

            def out_rows(tag, ready, lo):
                for tt in range(TT):
                    ready(tt)
                    turn(f"{tag}.{tt}", 6 + tt, [xn[:, tt, lo + j * P:lo + (j + 1) * P] for j in range(4)])

            def attend(tag, H, hd, kd, qT, kT, V, causal, obank):
                steps = steps_of(H, causal)

                def scores(i):
                    tt, h0, n, klen = steps[i]
                    out = fill(f"{tag}.s{i}", 4 + i % 2)
                    for j in range(n):
                        m = pe.matmul(out[:, j * klen:(j + 1) * klen], qT(h0 + j)[0:kd, tt * P:(tt + 1) * P],
                                      kT(h0 + j)[0:kd, 0:klen], start=True, stop=True)
                    close(f"{tag}.s{i}", m)

                def turns(i):
                    tt, h0, n, klen = steps[i]
                    if causal:
                        pe.wait_ge(ev("probs"), state["probs"] + i + 1)
                    else:
                        read_out(f"{tag}.s{i}")
                    turn(f"{tag}.t{i}", 6 + i % 2, [probs(tag, i)[:, j * P:(j + 1) * P] for j in range(4)])

                def values(i):
                    tt, h0, n, klen = steps[i]
                    if h0 == 0:
                        fill(f"{tag}.o{tt}", obank[tt])
                    out = PS[obank[tt]]
                    read_out(f"{tag}.t{i}")
                    kt = klen // P
                    for j in range(n):
                        h = h0 + j
                        for t in range(kt):
                            m = pe.matmul(out[:, h * hd:(h + 1) * hd],
                                          turned(tag, i)[:, (j * kt + t) * P:(j * kt + t + 1) * P],
                                          V(h, t), start=(t == 0), stop=(t == kt - 1))
                    if h0 + n == H:
                        close(f"{tag}.o{tt}", m)

                n = len(steps)
                scores(0)
                for i in range(n + 1):
                    if i + 1 < n:
                        scores(i + 1)
                    if i < n:
                        turns(i)
                    if i > 0:
                        values(i - 1)
                state["probs"] += n if causal else 0

            state["probs"] = 0
            pe.wait_ge(ev("const"), 16 * 5)

            def mem_kv(i, tag):
                b = a[f"w_kv{i}"]
                j = 0 if tag == "mk" else 1
                linear([f"{tag}{i}.0", f"{tag}{i}.1"], [2, 3], [b[4 * j + u] for u in range(4)], 2, tok(MX))

            def block_of(name, w, j, lhs, banks, n=4):
                linear([f"{name}.0", f"{name}.1"], banks, [a[w][n * j + u] for u in range(n)], KT // n, lhs)

            def mem_attend(i):
                c = MEM[i]
                for tt in range(TT):
                    read_out(f"xq{i}.{tt}")
                    turn(f"xqT{i}.{tt}", 6 + tt,
                         [slot(c["xq"], 1024)[:, tt * BLK + h * P:tt * BLK + (h + 1) * P] for h in range(4)])
                pe.wait_ge(ev("mkn"), i + 1)
                for tt in range(TT):
                    turn(f"mkT{i}.{tt}", 6 + tt,
                         [slot(c["mk"], 1024)[:, tt * BLK + h * P:tt * BLK + (h + 1) * P] for h in range(4)])
                for tt in range(TT):
                    read_out(f"xqT{i}.{tt}")
                    read_out(f"mkT{i}.{tt}")
                    read_out(f"mv{i}.{tt}")
                qT, kT, mv = slot(c["qT"], 1024), slot(c["kT"], 1024), slot(c["mv"], 1024)
                attend(f"ma{i}", 4, P, P, lambda h: qT[:, h * T:(h + 1) * T], lambda h: kT[:, h * T:(h + 1) * T],
                       lambda h, t: mv[:, t * BLK + h * P:t * BLK + (h + 1) * P], False, [2, 3])
                out_rows(f"mo{i}", lambda tt: read_out(f"ma{i}.o{tt}"), 512)

            def out_proj(L, w):
                for nb in range(2):
                    if nb == 0:
                        for n in MIXED[L]:
                            read_out(n)
                    block_of(f"out{L}.{nb}", w, nb, tok(MX), [2 * nb, 2 * nb + 1])

            def mlp(L, w_in, w_out, blocks, kts, squared):
                def inner(j):
                    linear([f"h{L}.{j}.0", f"h{L}.{j}.1"], [4, 5], [a[w_in][4 * j + u] for u in range(4)], 2, tok(XT))

                def outer(j):
                    for tt in range(TT):
                        read_out(f"ht{L}.{j}.{tt}")
                    pair = tuple(h[:, j % 2] for h in HT)
                    n = kts // 2
                    for nb in range(2):
                        linear([f"y{L}.{nb}.0", f"y{L}.{nb}.1"], [2 * nb, 2 * nb + 1],
                               [a[w_out][(2 * j + nb) * n + u] for u in range(n)], 2, tok(pair), 0, kts,
                               opened=(j == 0), closed=(j == blocks - 1))

                def turned_hidden(j):
                    for tt in range(TT):
                        if squared:
                            pe.wait_ge(ev("act"), state["act"] + 2 * j + tt + 1)
                        else:
                            read_out(f"h{L}.{j}.{tt}")
                        turn(f"ht{L}.{j}.{tt}", 6 + tt, [hrow[:, tt, i * P:(i + 1) * P] for i in range(kts)])

                for j in range(blocks + 1):
                    if j < blocks:
                        inner(j)
                    if j > 0:
                        outer(j - 1)
                    if j < blocks:
                        turned_hidden(j)
                state["act"] += 2 * blocks if squared else 0

            state["act"] = 0

            turn_norm(0, 0)
            for tt in range(TT):
                for h in range(2):
                    read_out(f"n0.{tt}.{h}")
            block_of("u", "w_a", 0, tok(XT), [0, 1])
            turn_norm(0, 1)
            block_of("xq0", "w_a", 1, tok(XT), [2, 3])
            for tt in range(TT):
                read_out(f"u.{tt}")
                turn(f"uT.{tt}", 6 + tt,
                     [slot(2, 1024)[:, tt * BLK + f * P:tt * BLK + (f + 1) * P] for f in range(4)])
            for tt in range(TT):
                for h in range(2):
                    read_out(f"n1.{tt}.{h}")
            mem_kv(0, "mk")
            block_of("gate", "w_a", 2, tok(XT), [0, 1])
            for tt in range(TT):
                read_out(f"gate.{tt}")
                turn(f"gateT.{tt}", 6 + tt,
                     [slot(4, 1024)[:, tt * BLK + f * P:tt * BLK + (f + 1) * P] for f in range(4)])
            mem_kv(0, "mv")
            pe.wait_ge(ev("conv"), 1)
            for g, banks in ((0, (0, 1)), (1, (4, 5))):
                for half in range(2):
                    out = fill(f"rg{g}.{half}", banks[half])
                    for j in range(2):
                        f = 2 * half + j
                        m = pe.matmul(out[:, j * T:(j + 1) * T], slot(8, 1024)[:, (4 * g + f) * P:(4 * g + f + 1) * P],
                                      slot(0, 1024)[:, f * T:(f + 1) * T], start=True, stop=True)
                    close(f"rg{g}.{half}", m)
            mem_attend(0)
            pe.wait_ge(ev("ylo"), 1)
            out_proj(0, "w_o0")
            turn_norm(0, 2)
            for tt in range(TT):
                for h in range(2):
                    read_out(f"n2.{tt}.{h}")
            mem_kv(1, "mk")
            turn_norm(0, 3)
            for tt in range(TT):
                for h in range(2):
                    read_out(f"n3.{tt}.{h}")
            mlp(0, "w_m0", "w_n0", MLP_BLOCKS, 4, True)
            mem_kv(1, "mv")
            turn_norm(1, 4)
            for tt in range(TT):
                for h in range(2):
                    read_out(f"n4.{tt}.{h}")
            linear(["f.0", "f.1"], [4, 5], [a["w_f"][0]], KT, tok(XT))
            block_of("q", "w_b", 0, tok(XT), [0, 1])
            block_of("k", "w_b", 1, tok(XT), [2, 3])
            pe.wait_ge(ev("logf"), 1)
            out = fill("c", 4)
            lf = sm("lf", 16)
            pe.matmul(out[:, 0:8], cst("tri"), lf[:, 0:8], start=True, stop=True)
            pe.matmul(out[:, 8:16], cst("ones"), lf[:, 0:8], start=True, stop=False)
            close("c", pe.matmul(out[:, 8:16], cst("tri"), lf[:, 8:16], start=False, stop=True))
            block_of("v", "w_b", 2, tok(XT), [0, 1])
            block_of("xq1", "w_b", 3, tok(XT), [2, 3])
            for n, s, e in (("fq", 4, "qaug"), ("fk", 7, "kaug")):
                pe.wait_ge(ev(e), 1)
                read_out("c")
                rows = slot(s, 1040).rearrange("p (t h d) -> p t h d", t=2, h=8)
                for tt in range(TT):
                    for half in range(2):
                        turn(f"{n}T.{tt}.{half}", 6 + half, [rows[:, tt, 4 * half + h, :] for h in range(4)])
            for n in ("fq", "fk"):
                for tt in range(TT):
                    for half in range(2):
                        read_out(f"{n}T.{tt}.{half}")
            for tt in range(TT):
                read_out(f"v.{tt}")
            attend("fa", 8, 64, 65, lambda h: scr[:, 8 * SLOT + h * T:8 * SLOT + (h + 1) * T],
                   lambda h: scr[:, 10 * SLOT + h * T:10 * SLOT + (h + 1) * T],
                   lambda h, t: slot(2, 1024)[:, t * BLK + h * 64:t * BLK + (h + 1) * 64], True, [0, 1])
            out_rows("fo", lambda tt: read_out(f"fa.o{tt}"), 0)
            mem_attend(1)
            out_proj(1, "w_o1")
            turn_norm(1, 5)
            for tt in range(TT):
                for h in range(2):
                    read_out(f"n5.{tt}.{h}")
            mlp(1, "w_m1", "w_n1", MLP_BLOCKS, 4, True)

            for L in (2, 3):
                i = L - 2
                k = 6 + 2 * i
                turn_norm(L, k)
                for tt in range(TT):
                    for h in range(2):
                        read_out(f"n{k}.{tt}.{h}")
                w = f"w_c{L}"
                block_of(f"hf{L}", w, 0, tok(XT), [0, 1])
                block_of(f"hq{L}", w, 1, tok(XT), [2, 3])
                for n, s in ((f"hf{L}", 0), (f"hq{L}", 1)):
                    for tt in range(TT):
                        read_out(f"{n}.{tt}")
                        turn(f"{n}T.{tt}", 6 + tt,
                             [slot(s, 1024)[:, tt * BLK + f * P:tt * BLK + (f + 1) * P] for f in range(4)])

                def level(l):
                    if l == 0:
                        read_out(f"hq{L}T.1")
                    else:
                        pe.wait_ge(ev("xlev"), 8 * i + l)
                    q, kk = slot(8, 1024), slot(1, 1024)
                    X = slot(9, 1024)
                    name = f"lev{L}.{l}"
                    if l == 0:
                        for tt in range(TT):
                            out = fill(f"{name}.{tt}", 4 + tt)
                            for h in range(4):
                                c = h * T + tt * P
                                m = pe.matmul(out[:, h * P:(h + 1) * P], kk[:, c:c + P], q[:, c:c + P],
                                              start=True, stop=True)
                            close(f"{name}.{tt}", m)
                        return
                    out = fill(name, 4 + l % 2)
                    if l == LEVELS:
                        for h in range(4):
                            m = pe.matmul(out[:, h * P:(h + 1) * P], X[:, h * T:h * T + P],
                                          X[:, h * T + P:(h + 1) * T], start=True, stop=True)
                        close(name, m)
                        return
                    s = 1 << (l - 1)
                    for tt in range(TT):
                        for h in range(4):
                            c = h * T + tt * P
                            q2 = X[:, c:c + P].rearrange("p (n two m) -> p n two m", two=2, m=s)[:, :, 1, :]
                            m = pe.matmul(out[:, (tt * 4 + h) * 64:(tt * 4 + h + 1) * 64], X[:, c:c + P], q2,
                                          start=True, stop=True)
                    close(name, m)

                def mixed_in(name, src, nk, banks, levels):
                    n = len(src)
                    lv = list(levels)
                    for u in range(n):
                        nm = [f"{name}.0", f"{name}.1"]
                        g0 = u * nk
                        outs = banks
                        if u == 0:
                            for q_, b_ in zip(nm, banks):
                                fill(q_, b_)
                        g, hi, lo, wd = unit(src[u], nk)
                        for j in range(nk):
                            kk_ = g0 + j
                            for tt in range(TT):
                                xh, xl = tok(XT)(kk_, tt)
                                last = kk_ == n * nk - 1
                                m = products(PS[banks[tt]][:, 0:wd], xh, xl, hi[:, j], lo[:, j], kk_ == 0, last,
                                             1 if j == 0 and tt == 0 and g else None)
                                if last:
                                    close(nm[tt], m)
                        if u % 2 == 1 and lv:
                            level(lv.pop(0))
                    for l_ in lv:
                        level(l_)

                mixed_in(f"A{L}", [a[w][8 + u] for u in range(4)], 2, [0, 1], [0])
                mixed_in(f"B{L}", [a[f"w_d{L}"][u] for u in range(4)], 2, [2, 3], [1, 2])
                mixed_in(f"nq{L}", [a[w][12 + u] for u in range(4)], 2, [0, 1], [3, 4])
                mixed_in(f"hi{L}", [a[w][16 + u] for u in range(4)], 2, [2, 3], [5, 6])
                mixed_in(f"hg{L}", [a[w][20 + u] for u in range(4)], 2, [0, 1], [7, 8])
                for tt in range(TT):
                    read_out(f"hi{L}.{tt}")
                read_out(f"lev{L}.{LEVELS}")
                AT = slot(10, 1024).rearrange("p (t h q) -> p t h q", t=2, h=4)
                AX_ = slot(11, 512)
                vr = slot(5, 1024)
                for tt in range(TT):
                    out = fill(f"ho{L}.{tt}", 2 + tt)
                    for h in range(4):
                        o = out[:, h * P:(h + 1) * P]
                        if tt == 1:
                            pe.matmul(o, AX_[:, h * P:(h + 1) * P], vr[:, h * P:(h + 1) * P], start=True, stop=False)
                        m = pe.matmul(o, AT[:, tt, h, :], vr[:, tt * BLK + h * P:tt * BLK + (h + 1) * P],
                                      start=(tt == 0), stop=True)
                    close(f"ho{L}.{tt}", m)

                A_ = slot(2, 1024)
                for tt in range(TT):
                    read_out(f"A{L}.{tt}")
                turn(f"cT{L}", 6, [A_[:, tt * BLK + kv * P:tt * BLK + (kv + 1) * P] for kv in range(2) for tt in range(TT)])
                pe.wait_ge(ev("xclo"), i + 1)
                flat = tuple(h[:, :, :, :].rearrange("p a b c -> p (a b c)") for h in HT)
                for kv in range(2):
                    def windows(k_, tt):
                        at = kv * 1024 + k_ * 32
                        return flat[0][:, at:at + P], flat[1][:, at:at + P]
                    linear([f"ch{L}.{kv}"], [4 + kv], [a[f"w_w{L}"][4 * kv + u] for u in range(4)], 4, windows)
                read_out(f"ch{L}.0")
                read_out(f"ch{L}.1")
                ch = slot(9, 512)
                turn(f"chT{L}", 6, [ch[0:2 * NCMP, j * P:(j + 1) * P] for j in range(4)])
                read_out(f"chT{L}")
                chT = sm("chT", 4 * 2 * NCMP).rearrange("p (j n) -> p j n", j=4)
                out = fill(f"kc{L}", 4)
                for m_ in range(2):
                    mm = pe.matmul(out[0:2 * NCMP, 0:64], chT[:, m_, :], w2c[:, i, 0, m_, :], start=(m_ == 0),
                                   stop=(m_ == 1))
                close(f"kc{L}", mm)
                pe.wait_ge(ev("chrep"), i + 1)
                rep = slot(10, 2 * 8 * NCMP).rearrange("p (m n) -> p m n", m=2)
                out = fill(f"vc{L}", 5)
                for m_ in range(2):
                    mm = pe.matmul(out[0:8 * NCMP, 0:64], rep[:, m_, :], w2c[:, i, 1, m_, :],
                                   start=(m_ == 0), stop=(m_ == 1))
                close(f"vc{L}", mm)
                pe.wait_ge(ev("kcr"), i + 1)
                turn(f"kcT{L}", 7, [sm("kcr", 64)[0:2 * NCMP, :]])
                pe.wait_ge(ev("ropeD"), i + 1)
                pe.wait_ge(ev("ropeP"), i + 1)
                Z = scr[:, 9 * SLOT:9 * SLOT + 1536].rearrange("p (t g d) -> p t g d", t=2, g=12)
                for tt in range(TT):
                    for g in range(3):
                        turn(f"zT{L}.{tt}.{g}", 6 + (tt * 3 + g) % 2, [Z[:, tt, 4 * g + j, :] for j in range(4)])
                for tt in range(TT):
                    for g in range(3):
                        read_out(f"zT{L}.{tt}.{g}")
                read_out(f"kcT{L}")
                qT = scr[:, 7 * SLOT:7 * SLOT + 2048]
                kT = slot(11, 1024)
                kcT = sm("kcT", 2 * NCMP)
                for tt in range(TT):
                    out = fill(f"cs{L}.{tt}", 4 + tt)
                    for h in range(8):
                        g = h // 4
                        m = pe.matmul(out[:, h * NCMP:(h + 1) * NCMP], qT[0:64, h * T + tt * P:h * T + (tt + 1) * P],
                                      kcT[0:64, g * NCMP:(g + 1) * NCMP], start=True, stop=True)
                    close(f"cs{L}.{tt}", m)
                for tt in range(TT):
                    pe.wait_ge(ev("cprobs"), 2 * i + tt + 1)
                    turn(f"cpT{L}.{tt}", 6 + tt, [sm(f"cp{tt}", 8 * NCMP)])
                for tt in range(TT):
                    read_out(f"cpT{L}.{tt}")
                read_out(f"vc{L}")
                for tt in range(TT):
                    out = fill(f"co{L}.{tt}", tt)
                    close(f"co{L}.{tt}", pe.matmul(out[:, :], cpT(tt)[0:8 * NCMP, :], slot(6, 512)[0:8 * NCMP, :],
                                                   start=True, stop=True))
                attend(f"sl{L}", 8, 64, 64, lambda h: qT[:, h * T:(h + 1) * T],
                       lambda h: kT[:, (h // 4) * T:(h // 4 + 1) * T],
                       lambda h, t: slot(2, 1024)[:, t * BLK + 384 + (h // 4) * 64:t * BLK + 448 + (h // 4) * 64],
                       True, [2, 3])
                attend(f"sw{L}", 8, 64, 64, lambda h: qT[:, h * T:(h + 1) * T],
                       lambda h: kT[:, (2 + h // 4) * T:(3 + h // 4) * T],
                       lambda h, t: slot(3, 1024)[:, t * BLK + 128 + (h // 4) * 64:t * BLK + 192 + (h // 4) * 64],
                       True, [0, 1])
                out_rows(f"hr{L}", lambda tt: pe.wait_ge(ev("hrow"), 2 * i + tt + 1), 0)
                out_rows(f"nr{L}", lambda tt: pe.wait_ge(ev("nrow"), 2 * i + tt + 1), 512)
                out_proj(L, f"w_o{L}")
                turn_norm(L, k + 1)
                for tt in range(TT):
                    for h in range(2):
                        read_out(f"n{k + 1}.{tt}.{h}")
                mlp(L, f"w_m{L}", f"w_n{L}", FFN_BLOCKS, 2, False)

        @block.sync
        def _(sp):
            for g, src in enumerate(units):
                if g >= NRAW:
                    sp.wait_ge(split_lo, g - NRAW + 1)
                sp.dma_start(raw[:, g % NRAW, 0:src.shape[1]], src).then_inc(landed[g % NRAW], 16)
            for tt in range(TT):
                for nb in range(2):
                    f = fills[f"y3.{nb}.{tt}"]
                    sp.wait_ge(bank_free[f.bank], f.turn)
                sp.dma_start(a["out"][tt * P:(tt + 1) * P, :], x[:, tt, :]).then_inc(ev("stored"), 16)
            sp.wait_ge(ev("stored"), 32)

        @block.scalar
        def _(act):
            st = {"g": 0, "hi": 0}
            act.dma_start(x[:, 0, :], a["x"][0:P, :]).then_inc(ev("xin"), 16)
            act.dma_start(x[:, 1, :], a["x"][P:T, :]).then_inc(ev("xin"), 16)
            act.dma_start(const[:, :], a["const"]).then_inc(ev("const"), 16)
            act.dma_start(rowg[:, :], a["rowg"].partition_broadcast(P)).then_inc(ev("const"), 16)
            act.dma_start(colg[:, :], a["colg"]).then_inc(ev("const"), 16)
            act.dma_start(slot(8, 1024), a["wgate"]).then_inc(ev("const"), 16)
            act.dma_start(w2c[:, :, :, :, :].rearrange("p a b c d -> p (a b c d)"), a["w2c"]).then_inc(ev("const"), 16)

            def splits(n):
                while st["g"] < min(n, len(units)):
                    g = st["g"]
                    w = units[g].shape[1]
                    act.wait_ge(landed[g % NRAW], 16 * (g // NRAW + 1))
                    if g >= NSPLIT:
                        act.wait_ge(unit_used, g - NSPLIT + 1)
                    act.activation(whi[:, g % NSPLIT, 0:w], raw[:, g % NRAW, 0:w], ACT.Copy).then_inc(split_hi, 1)
                    st["g"] += 1

            def full(name):
                f = fills[name]
                splits(f.pos + AHEAD)
                act.wait_ge(bank_full[f.bank], f.turn)
                return PS[f.bank]

            def free(name, ins):
                ins.then_inc(bank_free[fills[name].bank], 1)

            def copy_out(name, dst, src=None):
                ps = full(name)
                free(name, act.activation(dst, ps[:, :] if src is None else src(ps), ACT.Copy))

            def hi(name, dst, n=4, w=P):
                ps = full(name)
                src = ps[:, 0:n * w].rearrange("p (k t) -> p k t", k=n)
                act.activation(dst, src, ACT.Copy).then_inc(turn_hi, 1)

            def sq(k, src, waits):
                for tt in range(TT):
                    waits(tt)
                    act.activation(xn[:, tt, :], src(tt), ACT.Square,
                                   accum_out=sm("ssq", 2)[:, tt:tt + 1]).then_inc(ev("ssq"), 1)

            def norm_hi(k, pair):
                for tt in range(TT):
                    for h in range(2):
                        hi(f"n{k}.{tt}.{h}", pair[0][:, 4 * h:4 * h + 4, tt * P:(tt + 1) * P])

            def soft(tag, H, causal, scaled, base):
                steps = steps_of(H, causal)

                def exps(i):
                    tt, h0, n, klen = steps[i]
                    splits(fills[f"{tag}.s{i}"].pos + AHEAD)
                    act.wait_ge(ev("maxed"), base + i + 1)
                    for j in range(n):
                        c = tt * H + h0 + j
                        src = (masked(tag, i) if causal else PS[fills[f"{tag}.s{i}"].bank])[:, j * klen:(j + 1) * klen]
                        kw = {"scale": sm("cq", 16)[:, c:c + 1]} if scaled else {}
                        m = act.activation(probs(tag, i)[:, j * klen:(j + 1) * klen], src, ACT.Exp,
                                           bias=sm("nmax", 16)[:, c:c + 1], accum_out=sm("rsum", 16)[:, c:c + 1], **kw)
                    if causal:
                        m.then_inc(ev("probs"), 1)
                    else:
                        free(f"{tag}.s{i}", m)

                def take(i):
                    copy_out(f"{tag}.t{i}", turned(tag, i))

                n = len(steps)
                exps(0)
                for i in range(n):
                    if i + 1 < n:
                        exps(i + 1)
                    take(i)

            cnt = {"s": 0, "p": 0}

            def mem_side(i):
                c = MEM[i]
                for tt in range(TT):
                    copy_out(f"xqT{i}.{tt}", slot(c["qT"], 1024).rearrange("p (h t) -> p h t", h=4)[:, :, tt * P:(tt + 1) * P],
                             lambda ps: ps[:, :].rearrange("p (h t) -> p h t", h=4))
                for tt in range(TT):
                    copy_out(f"mkT{i}.{tt}", slot(c["kT"], 1024).rearrange("p (h t) -> p h t", h=4)[:, :, tt * P:(tt + 1) * P],
                             lambda ps: ps[:, :].rearrange("p (h t) -> p h t", h=4))
                soft(f"ma{i}", 4, False, True, cnt["s"])
                cnt["s"] += 4
                for tt in range(TT):
                    hi(f"mo{i}.{tt}", MX[0][:, 4:8, tt * P:(tt + 1) * P])

            def mlp_side(L, blocks, kts, squared):
                def relu(j):
                    for tt in range(TT):
                        name = f"h{L}.{j}.{tt}"
                        if squared:
                            ps = full(name)
                            free(name, act.activation(hrow[:, tt, :], ps[:, :], ACT.Relu))
                        else:
                            ps = full(name)
                            act.activation(hrow[:, tt, 256:512], ps[:, 0:256], ACT.Tanh, scale=0.5).then_inc(ev("tanh"), 1)

                def ht(j):
                    for tt in range(TT):
                        hi(f"ht{L}.{j}.{tt}", HT[0][:, j % 2, 0:kts, tt * P:(tt + 1) * P], kts)

                for j in range(blocks):
                    relu(j)
                    ht(j)

            splits(NSPLIT - 1)
            sq(0, lambda tt: x[:, tt, :], lambda tt: act.wait_ge(ev("xin"), 32))
            norm_hi(0, XT)
            for tt in range(TT):
                act.wait_ge(ev("memin"), 32)
                act.wait_ge(bank_full[fills["n0.1.1"].bank], fills["n0.1.1"].turn)
                act.activation(xn[:, tt, :], slot(tt, 1024), ACT.Square,
                               accum_out=sm("ssq", 2)[:, tt:tt + 1]).then_inc(ev("ssq"), 1)
            act.wait_ge(ev("lamz"), 1)
            act.activation(sm("z4", 4), sm("z4", 4), ACT.Exp, scale=-1.0).then_inc(ev("lamexp"), 1)
            for tt in range(TT):
                copy_out(f"u.{tt}", slot(2, 1024)[:, tt * BLK:(tt + 1) * BLK])
            norm_hi(1, MX)
            for tt in range(TT):
                copy_out(f"xq0.{tt}", slot(3, 1024)[:, tt * BLK:(tt + 1) * BLK])
            for tt in range(TT):
                copy_out(f"uT.{tt}", slot(7, 1024).rearrange("p (f t) -> p f t", f=4)[:, :, tt * P:(tt + 1) * P],
                         lambda ps: ps[:, :].rearrange("p (f t) -> p f t", f=4))
            for tt in range(TT):
                copy_out(f"mk0.{tt}", slot(5, 1024)[:, tt * BLK:(tt + 1) * BLK])
            for tt in range(TT):
                copy_out(f"gate.{tt}", slot(4, 1024)[:, tt * BLK:(tt + 1) * BLK])
            for tt in range(TT):
                copy_out(f"gateT.{tt}", slot(10, 1024).rearrange("p (f t) -> p f t", f=4)[:, :, tt * P:(tt + 1) * P],
                         lambda ps: ps[:, :].rearrange("p (f t) -> p f t", f=4))
            for tt in range(TT):
                copy_out(f"mv0.{tt}", slot(6, 1024)[:, tt * BLK:(tt + 1) * BLK])
            act.wait_ge(ev("lru_c"), 1)
            for g, dst in ((0, 1), (1, 2)):
                for half in range(2):
                    ps = full(f"rg{g}.{half}")
                    for j in range(2):
                        f = 2 * half + j
                        m = act.activation(slot(dst, 1024)[:, f * T:(f + 1) * T], ps[:, j * T:(j + 1) * T], ACT.Tanh,
                                           bias=sm("hb", 8)[:, 4 * g + f:4 * g + f + 1], scale=0.5)
                    free(f"rg{g}.{half}", m)
            act.wait_ge(ev("gcub"), 1)
            act.activation(slot(8, 1024), slot(8, 1024), ACT.Tanh).then_inc(ev("gtanh"), 1)
            act.wait_ge(ev("rgate"), 1)
            for f in range(4):
                m = act.activation(slot(1, 1024)[:, f * T:(f + 1) * T], slot(1, 1024)[:, f * T:(f + 1) * T], ACT.Tanh,
                                   scale=sm("lc", 4)[:, f:f + 1])
            m.then_inc(ev("dtanh"), 1)
            act.wait_ge(ev("b2"), 1)
            act.activation(slot(8, 1024), slot(8, 1024), ACT.Sqrt).then_inc(ev("bsq"), 1)
            mem_side(0)
            act.wait_ge(ev("yrow"), 1)
            act.activation(MX[0][:, 0:4, :].rearrange("p f t -> p (f t)"), slot(7, 1024), ACT.Copy).then_inc(ev("yhi"), 1)
            act.wait_ge(ev("memin"), 64)
            act.wait_ge(bank_full[fills["mo0.1"].bank], fills["mo0.1"].turn)
            for tt in range(TT):
                act.activation(xn[:, tt, :], slot(tt, 1024), ACT.Square,
                               accum_out=sm("ssq", 2)[:, tt:tt + 1]).then_inc(ev("ssq"), 1)
            norm_hi(2, MX)

            def sq_x(rows, lastturn):
                for tt in range(TT):
                    for nb in range(2):
                        f = fills[f"{rows}.{nb}.{tt}"]
                        splits(f.pos + AHEAD)
                        act.wait_ge(bank_free[f.bank], f.turn)
                    if tt == 0:
                        f = fills[lastturn]
                        act.wait_ge(bank_full[f.bank], f.turn)
                    act.activation(xn[:, tt, :], x[:, tt, :], ACT.Square,
                                   accum_out=sm("ssq", 2)[:, tt:tt + 1]).then_inc(ev("ssq"), 1)

            splits(fills["mk1.1"].pos)
            sq_x("out0", "n2.1.1")
            for tt in range(TT):
                copy_out(f"mk1.{tt}", slot(5, 1024)[:, tt * BLK:(tt + 1) * BLK])
            norm_hi(3, XT)
            mlp_side(0, MLP_BLOCKS, 4, True)
            splits(fills["mv1.1"].pos)
            sq_x("y0", "n3.1.1")
            for tt in range(TT):
                copy_out(f"mv1.{tt}", slot(6, 1024)[:, tt * BLK:(tt + 1) * BLK])
            norm_hi(4, XT)
            splits(fills["f.1"].pos + AHEAD)
            act.wait_ge(ev("absf"), 1)
            act.activation(sm("lz", 16), sm("lz", 16), ACT.Exp, scale=-1.0).then_inc(ev("expf"), 1)
            for n, s in (("q", 0), ("k", 1), ("v", 2), ("xq1", 3)):
                for tt in range(TT):
                    copy_out(f"{n}.{tt}", slot(s, 1024)[:, tt * BLK:(tt + 1) * BLK])
            for n, s in (("fq", 8), ("fk", 10)):
                dst = scr[:, s * SLOT:s * SLOT + 2048].rearrange("p (h t) -> p h t", h=8)
                for tt in range(TT):
                    for half in range(2):
                        copy_out(f"{n}T.{tt}.{half}", dst[0:65, 4 * half:4 * half + 4, tt * P:(tt + 1) * P],
                                 lambda ps: ps[0:65, :].rearrange("p (h t) -> p h t", h=4))
            soft("fa", 8, True, False, cnt["s"])
            cnt["s"] += len(steps_of(8, True))
            for tt in range(TT):
                hi(f"fo.{tt}", MX[0][:, 0:4, tt * P:(tt + 1) * P])
            mem_side(1)
            sq_x("out1", "mo1.1")
            norm_hi(5, XT)
            mlp_side(1, MLP_BLOCKS, 4, True)
            for L in (2, 3):
                i = L - 2
                k = 6 + 2 * i
                sq_x(f"y{L - 1}", f"n{k - 1}.1.1")
                norm_hi(k, XT)
                if L == 3:
                    act.wait_ge(ev("lbd"), 1)
                    act.activation(sm("A4", 4), sm("A4", 4), ACT.Tanh, scale=0.5).then_inc(ev("lbt"), 1)
                for n, s in ((f"hf{L}", 0), (f"hq{L}", 1)):
                    for tt in range(TT):
                        copy_out(f"{n}.{tt}", slot(s, 1024)[:, tt * BLK:(tt + 1) * BLK])
                for tt in range(TT):
                    ps = full(f"hf{L}T.{tt}")
                    free(f"hf{L}T.{tt}", act.activation(
                        slot(7, 1024).rearrange("p (f t) -> p f t", f=4)[:, :, tt * P:(tt + 1) * P],
                        ps[:, :].rearrange("p (f t) -> p f t", f=4), ACT.Tanh, scale=0.5))
                for tt in range(TT):
                    ps = full(f"hq{L}T.{tt}")
                    act.activation(slot(8, 1024).rearrange("p (f t) -> p f t", f=4)[:, :, tt * P:(tt + 1) * P],
                                   ps[:, :].rearrange("p (f t) -> p f t", f=4), ACT.Tanh, scale=0.5).then_inc(ev("hqt"), 1)
                for n, s in ((f"A{L}", 2), (f"B{L}", 3), (f"nq{L}", 4), (f"hi{L}", 5)):
                    w = 280 if s == 3 else BLK
                    for tt in range(TT):
                        copy_out(f"{n}.{tt}", slot(s, 1024)[:, tt * BLK:tt * BLK + w], lambda ps: ps[:, 0:w])
                for tt in range(TT):
                    ps = full(f"hg{L}.{tt}")
                    act.activation(slot(6, 1024)[:, tt * BLK:(tt + 1) * BLK], ps[:, :], ACT.Tanh,
                                   scale=0.5).then_inc(ev("hgt"), 1)
                f = fills[f"B{L}.1"]
                act.wait_ge(bank_free[f.bank], f.turn)
                act.activation(sm("ng", 48).rearrange("p (t c) -> p t c", t=2),
                               slot(3, 1024).rearrange("p (t c) -> p t c", t=2)[:, :, 256:280], ACT.Tanh,
                               scale=0.5).then_inc(ev("ngt"), 1)
                ps = full(f"cT{L}")
                src = ps[:, :].rearrange("p (a b two) -> p a b two", a=4, two=2)
                kk = slot(9, 512).rearrange("p (kv g t) -> p kv g t", kv=2, g=2)
                for par in range(2):
                    for g in range(2):
                        dst = kk[par * 64:(par + 1) * 64, :, g, :].rearrange("p kv (t c) -> p kv t c", t=2)
                        m = act.activation(dst, src[g * 64:(g + 1) * 64, :, :, par].rearrange(
                            "p (kv t) c -> p kv t c", kv=2), ACT.Copy)
                free(f"cT{L}", m)
                act.wait_ge(ev("xc"), i + 1)
                flat = HT[0][:, :, :, :].rearrange("p a b c -> p (a b c)").rearrange("p (kv c) -> p kv c", kv=2)
                act.activation(flat[:, :, 0:608], scr[:, 10 * SLOT:10 * SLOT + 1216].rearrange("p (kv c) -> p kv c", kv=2),
                               ACT.Copy).then_inc(ev("xchi"), 1)
                for kv in range(2):
                    ps = full(f"ch{L}.{kv}")
                    act.activation(slot(9, 512)[0:2 * NCMP, kv * 256:(kv + 1) * 256], ps[0:2 * NCMP, 0:256], ACT.Tanh,
                                   scale=0.5).then_inc(ev("cht"), 1)
                copy_out(f"chT{L}", sm("chT", 4 * 2 * NCMP).rearrange("p (j n) -> p j n", j=4),
                         lambda ps: ps[:, :].rearrange("p (j n) -> p j n", j=4)[:, :, 0:2 * NCMP])
                copy_out(f"kc{L}", sm("kc", 64)[0:2 * NCMP, :], lambda ps: ps[0:2 * NCMP, 0:64])
                copy_out(f"kcT{L}", sm("kcT", 2 * NCMP)[0:64, :], lambda ps: ps[0:64, 0:2 * NCMP])
                qT = scr[:, 7 * SLOT:7 * SLOT + 2048].rearrange("p (h t) -> p h t", h=8)
                kT = slot(11, 1024).rearrange("p (h t) -> p h t", h=4)
                for tt in range(TT):
                    for g in range(3):
                        dst = qT[0:64, 4 * g:4 * g + 4] if g < 2 else kT[0:64]
                        copy_out(f"zT{L}.{tt}.{g}", dst[:, :, tt * P:(tt + 1) * P],
                                 lambda ps: ps[0:64, :].rearrange("p (h t) -> p h t", h=4))
                for tt in range(TT):
                    act.wait_ge(ev("cd"), 2 * i + tt + 1)
                    act.activation(sm(f"cp{tt}", 8 * NCMP), sm(f"cp{tt}", 8 * NCMP), ACT.Exp).then_inc(ev("cexp"), 1)
                for tt in range(TT):
                    copy_out(f"cpT{L}.{tt}", cpT(tt)[0:8 * NCMP, :], lambda ps: ps[0:8 * NCMP, 0:P])
                for br in ("sl", "sw"):
                    soft(f"{br}{L}", 8, True, True, cnt["s"])
                    cnt["s"] += len(steps_of(8, True))
                for tt in range(TT):
                    hi(f"hr{L}.{tt}", MX[0][:, 0:4, tt * P:(tt + 1) * P])
                for tt in range(TT):
                    hi(f"nr{L}.{tt}", MX[0][:, 4:8, tt * P:(tt + 1) * P])
                sq_x(f"out{L}", f"nr{L}.1")
                norm_hi(k + 1, XT)
                mlp_side(L, FFN_BLOCKS, 2, False)
            splits(len(units))

        @block.gpsimd
        def _(pool):
            pool.memset(powc[:, :], -0.5).then_inc(ev("powc"), 1)

            def load_gain(k):
                if k >= 2:
                    pool.wait_ge(ev("xn"), 2 * (k - 1))
                pool.dma_start(gain[:, k % 2, :], a["gains"][k, :].partition_broadcast(P)).then_inc(ev(f"gain{k % 2}"), 16)

            def rstd(src, n, width, event=None):
                chain(pool, "p_chain", pool.tensor_scalar(src, src, 1.0 / width, EPS, ALU.mult, ALU.add))
                m = pool.tensor_tensor(src, src, powc[0:src.shape[0], 0:n], ALU.pow)
                if event:
                    m.then_inc(ev(event), 1)
                else:
                    chain(pool, "p_chain", m)

            def norm(k):
                for tt in range(TT):
                    pool.wait_ge(ev("ssq"), 2 * k + tt + 1)
                    rstd(sm("ssq", 2)[:, tt:tt + 1], 1, D, "rstd")
                if k + 2 < 10:
                    load_gain(k + 2)

            def squares(src, groups, hd, wait):
                wait()
                pool.tensor_tensor(hrow[:, :, :].rearrange("p a b -> p (a b)")[:, 0:2 * groups * hd], src, src,
                                   ALU.mult).then_inc(ev("sq"), 1)

            def stat(name, n, hd, k):
                pool.wait_ge(ev("hsum"), k + 1)
                rstd(sm(name, n), n, hd, "hrstd")

            def taken(name):
                pool.wait_ge(bank_free[fills[name].bank], fills[name].turn)

            pool.dma_start(slot(0, 1024), a["mem"][0:P, :]).then_inc(ev("memin"), 16)
            pool.dma_start(slot(1, 1024), a["mem"][P:T, :]).then_inc(ev("memin"), 16)
            load_gain(0)
            load_gain(1)
            pool.wait_ge(ev("powc"), 1)
            norm(0)
            norm(1)
            pool.wait_ge(ev("const"), 80)

            def headnorm(src, n, hd, name, k, waits):
                squares(src, n // 2, hd, waits)
                stat(name, n, hd, k)

            def scale_rows(dst, src, r, g):
                n, d = src.shape[1], src.shape[2]
                chain(pool, "p_chain", pool.tensor_tensor(dst, src, bc(r, 2, d), ALU.mult))
                return pool.tensor_tensor(dst, dst, bc(g, 1, n), ALU.mult)

            def mem_norms(i, kk):
                c = MEM[i]
                headnorm(slot(c["xq"], 1024), 8, P, "cqm", kk, lambda: (taken(f"xq{i}.0"), taken(f"xq{i}.1")))
                headnorm(slot(c["mk"], 1024), 8, P, "rk8", kk + 1,
                         lambda: (taken(f"mk{i}.0"), taken(f"mk{i}.1"), pool.wait_ge(ev("hrstd"), kk + 1)))
                pool.wait_ge(ev("hrstd"), kk + 2)
                g = sm("gqk", P)
                chain(pool, "p_chain", pool.tensor_tensor(g, rg(f"xaq{i}"), rg(f"xak{i}"), ALU.mult))
                v = slot(c["mk"], 1024).rearrange("p (n d) -> p n d", d=P)
                scale_rows(v, v, sm("rk8", 8), g).then_inc(ev("mkn"), 1)

            mem_norms(0, 0)
            pool.wait_ge(ev("yrow"), 1)
            pool.dma_start(slot(0, 1024), a["mem"][0:P, :]).then_inc(ev("memin"), 16)
            pool.dma_start(slot(1, 1024), a["mem"][P:T, :]).then_inc(ev("memin"), 16)
            norm(2)
            norm(3)

            def square_hidden(L):
                for j in range(MLP_BLOCKS):
                    for tt in range(TT):
                        pool.wait_ge(bank_free[fills[f"h{L}.{j}.{tt}"].bank], fills[f"h{L}.{j}.{tt}"].turn)
                        pool.tensor_tensor(hrow[:, tt, :], hrow[:, tt, :], hrow[:, tt, :], ALU.mult).then_inc(ev("act"), 1)

            square_hidden(0)
            norm(4)
            headnorm(slot(0, 1024), 16, 64, "rq16", 2, lambda: (taken("q.0"), taken("q.1")))
            headnorm(slot(1, 1024), 16, 64, "rk16", 3, lambda: (taken("k.0"), taken("k.1"), pool.wait_ge(ev("hrstd"), 3)))
            pool.wait_ge(ev("hrstd"), 4)
            g = sm("gqk", P)
            chain(pool, "p_chain", pool.tensor_tensor(g[:, 0:64], rg("foxq"), rg("foxk"), ALU.mult))
            ka = slot(7, 1040).rearrange("p (n d) -> p n d", d=65)
            qa = slot(4, 1040).rearrange("p (n d) -> p n d", d=65)
            q = slot(0, 1024).rearrange("p (n d) -> p n d", d=64)
            k = slot(1, 1024).rearrange("p (n d) -> p n d", d=64)
            pool.memset(qa[:, :, 64:65], 1.0)
            chain(pool, "p_chain", pool.tensor_scalar(sm("rq16", 16), sm("rq16", 16), 0.125, None, ALU.mult))
            pool.tensor_tensor(qa[:, :, 0:64], q, bc(sm("rq16", 16), 2, 64), ALU.mult).then_inc(ev("qaug"), 1)
            scale_rows(ka[:, :, 0:64], k, sm("rk16", 16), g[:, 0:64]).then_inc(ev("kaug"), 1)
            mem_norms(1, 4)
            norm(5)
            square_hidden(1)
            for L in (2, 3):
                i = L - 2
                norm(6 + 2 * i)
                F, S = slot(0, 1024), slot(7, 1024)
                pool.wait_ge(ev("hfk"), i + 1)
                pool.memset(S, 1.0).then_inc(ev("lev"), 1)
                for l in range(1, LEVELS):
                    m_ = 1 << (l - 1)
                    Fv = F.rearrange("p (n two m) -> p n two m", two=2, m=m_)
                    Sv = S.rearrange("p (n two m) -> p n two m", two=2, m=m_)
                    tot = Fv[:, :, 1, m_ - 1]
                    lastf = Fv[:, :, 0, m_ - 1]
                    pool.wait_ge(ev("xlev"), 8 * i + l)
                    chain(pool, "p_chain", pool.tensor_tensor(Sv[:, :, 0, :], Sv[:, :, 0, :], bc(tot, 2, m_), ALU.mult))
                    pool.tensor_tensor(Fv[:, :, 1, :], Fv[:, :, 1, :], bc(lastf, 2, m_), ALU.mult).then_inc(ev("lev"), 1)
                kk = slot(9, 512).rearrange("p (kv g t) -> p kv g t", kv=2, g=2)
                X = scr[:, 10 * SLOT:10 * SLOT + 1216].rearrange("p (kv c) -> p kv c", kv=2)
                f = fills[f"ho{L}.1"]
                pool.wait_ge(bank_full[f.bank], f.turn)
                chain(pool, "p_chain", pool.memset(scr[:, 10 * SLOT:10 * SLOT + 1216], 0.0))
                taken(f"cT{L}")
                for kv in range(2):
                    for g_ in range(2):
                        dst = X[:, kv, 0:512].rearrange("p (j c) -> p j c", j=16)[:, :, g_ * NCMP:(g_ + 1) * NCMP]
                        lowj = kk[:, kv, g_, 0:8 * NCMP].rearrange("p (n j) -> p j n", j=8)
                        hij = kk[:, kv, g_, 8:8 + 8 * NCMP].rearrange("p (n j) -> p j n", j=8)
                        pe_ = cg(f"pe{L}", 16 * kv, 16)
                        pool.tensor_tensor(dst[:, 0:8], lowj, bc(pe_[:, 0:8], 2, NCMP), ALU.add)
                        m = pool.tensor_tensor(dst[:, 8:16], hij, bc(pe_[:, 8:16], 2, NCMP), ALU.add)
                m.then_inc(ev("xc"), 1)
                k0 = 6 + 5 * i
                headnorm(slot(4, 1024), 16, 64, "rq16", k0, lambda: (taken(f"nq{L}.0"), taken(f"nq{L}.1")))
                for n_, (s, lo) in enumerate(((2, 256), (3, 0))):
                    pool.wait_ge(ev("hrstd"), k0 + 1 + n_)
                    taken(f"A{L}.1" if s == 2 else f"B{L}.1")
                    src = slot(s, 1024).rearrange("p (t c) -> p t c", t=2)[:, :, lo:lo + P]
                    pool.tensor_tensor(hrow[:, 0, 0:256].rearrange("p (t c) -> p t c", t=2), src, src,
                                       ALU.mult).then_inc(ev("sq"), 1)
                    stat("rks" if n_ == 0 else "rkw", 4, 64, k0 + 1 + n_)
                pool.wait_ge(ev("hrstd"), k0 + 3)
                Z = scr[:, 7 * SLOT:7 * SLOT + 1536].rearrange("p (t g d) -> p t g d", t=2, g=12)
                for tt in range(TT):
                    qv = slot(4, 1024)[:, tt * BLK:(tt + 1) * BLK].rearrange("p (g d) -> p g d", d=64)
                    pool.tensor_tensor(Z[:, tt, 0:8, :], qv, bc(rg(f"q{L}"), 1, 8), ALU.mult)
                    for n_, (s, lo, nm) in enumerate(((2, 256, "rks"), (3, 0, "rkw"))):
                        kv_ = slot(s, 1024)[:, tt * BLK + lo:tt * BLK + lo + P].rearrange("p (g d) -> p g d", d=64)
                        m = scale_rows(Z[:, tt, 8 + 2 * n_:10 + 2 * n_, :], kv_, sm(nm, 4)[:, 2 * tt:2 * tt + 2],
                                       rg(f"k{L}", 64 * (n_ + 1), 64))
                m.then_inc(ev("zrow"), 1)
                taken(f"kc{L}")
                n30 = 2 * NCMP
                kc, kt_ = sm("kc", 64), sm("kct", 64)
                pool.tensor_tensor(kt_[0:n30, :], kc[0:n30, :], kc[0:n30, :], ALU.mult).then_inc(ev("sq"), 1)
                pool.wait_ge(ev("hsum"), k0 + 4)
                rstd(sm("rkc", 1)[0:n30, :], 1, 64, "hrstd")
                pool.wait_ge(ev("hrstd"), k0 + 4)
                chain(pool, "p_chain", pool.tensor_scalar(kc[0:n30, :], kc[0:n30, :], sm("rkc", 1)[0:n30, :], None, ALU.mult))
                chain(pool, "p_chain", pool.tensor_tensor(kc[0:n30, :], kc[0:n30, :], rg(f"k{L}", 0, 64)[0:n30, :], ALU.mult))
                c_, s_ = cst("ccos")[0:n30, :], cst("csin")[0:n30, :]
                kr = sm("kcr", 64)
                x1, x2 = kc[0:n30, 0:32], kc[0:n30, 32:64]
                pool.tensor_tensor(kr[0:n30, 0:32], x1, c_, ALU.mult)
                pool.tensor_tensor(kt_[0:n30, 0:32], x2, s_, ALU.mult)
                pool.tensor_tensor(kr[0:n30, 32:64], x2, c_, ALU.mult)
                chain(pool, "p_chain", pool.tensor_tensor(kt_[0:n30, 32:64], x1, s_, ALU.mult))
                pool.tensor_tensor(kr[0:n30, 0:32], kr[0:n30, 0:32], kt_[0:n30, 0:32], ALU.subtract)
                pool.tensor_tensor(kr[0:n30, 32:64], kr[0:n30, 32:64], kt_[0:n30, 32:64], ALU.add).then_inc(ev("kcr"), 1)
                f = fills[f"vc{L}"]
                pool.wait_ge(bank_full[f.bank], f.turn)
                Zr = scr[:, 9 * SLOT:9 * SLOT + 1536].rearrange("p (t g d) -> p t g d", t=2, g=12)
                tmp = hrow[:, :, :].rearrange("p a b -> p (a b)")[:, 0:768].rearrange("p (t g d) -> p t g d", t=2, g=12)
                cosb = bc(cst("cos").rearrange("p (t d) -> p t d", t=2), 2, 12)
                sinb = bc(cst("sin").rearrange("p (t d) -> p t d", t=2), 2, 12)
                pool.tensor_tensor(Zr[:, :, :, 32:64], Z[:, :, :, 32:64], cosb, ALU.mult)
                chain(pool, "p_chain", pool.tensor_tensor(tmp, Z[:, :, :, 0:32], sinb, ALU.mult))
                pool.tensor_tensor(Zr[:, :, :, 32:64], Zr[:, :, :, 32:64], tmp, ALU.add).then_inc(ev("ropeP"), 1)
                pool.wait_ge(ev("ropeP"), i + 1)
                for tt in range(TT):
                    taken(f"ho{L}.{tt}")
                pool.tensor_tensor(hrow[:, :, :], xn[:, :, 0:512], xn[:, :, 0:512], ALU.mult).then_inc(ev("sq"), 1)
                pool.wait_ge(ev("hsum"), k0 + 5)
                rstd(sm("rho", 8), 8, P, "hrstd")
                pool.wait_ge(ev("hrstd"), k0 + 5)
                for tt in range(TT):
                    o = xn[:, tt, 0:512].rearrange("p (n d) -> p n d", d=P)
                    scale_rows(o, o, sm("rho", 8)[:, 4 * tt:4 * tt + 4], rg(f"gn{L}")).then_inc(ev("hon"), 1)
                norm(7 + 2 * i)

        @block.vector
        def _(dve):
            st = {"g": 0, "hi": 0}

            def splits(n):
                while st["g"] < min(n, len(units)):
                    g = st["g"]
                    w = units[g].shape[1]
                    dve.wait_ge(split_hi, g + 1)
                    dve.tensor_tensor(wlo[:, g % NSPLIT, 0:w], raw[:, g % NRAW, 0:w],
                                      whi[:, g % NSPLIT, 0:w].bitcast(F32), ALU.subtract).then_inc(split_lo, 1)
                    st["g"] += 1

            def full(name):
                f = fills[name]
                splits(f.pos + AHEAD)
                dve.wait_ge(bank_full[f.bank], f.turn)
                return PS[f.bank]

            def free(name, ins, wait=False):
                ins.then_inc(bank_free[fills[name].bank], 1)
                if wait:
                    dve.wait_ge(bank_free[fills[name].bank], fills[name].turn)

            def lo(name, pair, sl, n=4):
                st["hi"] += 1
                ps = full(name)
                dve.wait_ge(turn_hi, st["hi"])
                src = ps[:, 0:n * P].rearrange("p (k t) -> p k t", k=n)
                free(name, dve.tensor_tensor(sl(pair[1]), src, sl(pair[0]).bitcast(F32), ALU.subtract))

            def norm_rows(k, src, waits):
                for tt in range(TT):
                    waits(tt)
                    dve.wait_ge(ev("rstd"), 2 * k + tt + 1)
                    dve.wait_ge(ev(f"gain{k % 2}"), 16 * (k // 2 + 1))
                    dve.scalar_tensor_tensor(xn[:, tt, :], src(tt), sm("ssq", 2)[:, tt:tt + 1], gain[:, k % 2, :],
                                             ALU.mult, ALU.mult).then_inc(ev("xn"), 1)

            def norm_lo(k, pair):
                for tt in range(TT):
                    for h in range(2):
                        lo(f"n{k}.{tt}.{h}", pair, lambda t: t[:, 4 * h:4 * h + 4, tt * P:(tt + 1) * P])

            def residual(names):
                for tt in range(TT):
                    for nb in range(2):
                        ps = full(names[nb][tt])
                        free(names[nb][tt], dve.tensor_tensor(x[:, tt, nb * BLK:(nb + 1) * BLK], ps[:, :],
                                                              x[:, tt, nb * BLK:(nb + 1) * BLK], ALU.add))

            def hsums(dst, src, after=None):
                if after:
                    splits(fills[after].pos + AHEAD)
                st["hs"] = st.get("hs", 0) + 1
                dve.wait_ge(ev("sq"), st["hs"])
                dve.tensor_reduce(dst, src, AX.X, ALU.add).then_inc(ev("hsum"), 1)

            def hq(n, hd):
                return hrow[:, :, :].rearrange("p a b -> p (a b)")[:, 0:n * hd].rearrange("p (n d) -> p n d", d=hd)

            def soft(tag, H, causal, scaled, base):
                for i, (tt, h0, n, klen) in enumerate(steps_of(H, causal)):
                    ps = full(f"{tag}.s{i}")
                    c = tt * H + h0
                    mx = sm("mx", 16)[:, c:c + n]
                    if causal:
                        if i >= 2:
                            dve.wait_ge(ev("probs"), base + i - 1)
                        for j in range(n):
                            m = dve.tensor_tensor_reduce(masked(tag, i)[:, j * klen:(j + 1) * klen],
                                                         ps[:, j * klen:(j + 1) * klen],
                                                         cst("mask", 256 - klen if tt == 0 else 0, klen), 1.0, -3.0e38,
                                                         ALU.add, ALU.max, mx[:, j:j + 1])
                        free(f"{tag}.s{i}", m, True)
                    else:
                        chain(dve, "v_chain", dve.tensor_reduce(
                            mx, ps[:, 0:n * klen].rearrange("p (h k) -> p h k", h=n), AX.X, ALU.max))
                    nm = sm("nmax", 16)[:, c:c + n]
                    if scaled:
                        m = dve.scalar_tensor_tensor(nm, mx, -1.0, sm("cq", 16)[:, c:c + n], ALU.mult, ALU.mult)
                    else:
                        m = dve.tensor_scalar(nm, mx, -1.0, None, ALU.mult)
                    m.then_inc(ev("maxed"), 1)

            cnt = {"p": 0}

            def mem_soft(i):
                dve.wait_ge(ev("hrstd"), (1, 5)[i])
                chain(dve, "v_chain", dve.tensor_scalar(sm("cq", 16)[:, 0:8], sm("cqm", 8), P ** -0.5, None, ALU.mult))
                soft(f"ma{i}", 4, False, True, 0)
                for s_ in (2, 3):
                    f = fills[f"ma{i}.s{s_}"]
                    dve.wait_ge(bank_free[f.bank], f.turn)
                chain(dve, "v_chain", dve.reciprocal(sm("rinv", 16)[:, 0:8], sm("rsum", 16)[:, 0:8]))
                for tt in range(TT):
                    ps = full(f"ma{i}.o{tt}")
                    free(f"ma{i}.o{tt}", dve.tensor_tensor(
                        xn[:, tt, 512:1024].rearrange("p (h d) -> p h d", h=4), ps[:, :].rearrange("p (h d) -> p h d", h=4),
                        bc(sm("rinv", 16)[:, 4 * tt:4 * tt + 4], 2, P), ALU.mult))
                for tt in range(TT):
                    lo(f"mo{i}.{tt}", MX, lambda t: t[:, 4:8, tt * P:(tt + 1) * P])

            def mlp_side(L, blocks, kts, squared, acts):
                for j in range(blocks):
                    if not squared:
                        for tt in range(TT):
                            name = f"h{L}.{j}.{tt}"
                            ps = full(name)
                            acts["t"] += 1
                            dve.wait_ge(ev("tanh"), acts["t"])
                            g2 = hrow[:, tt, 256:512]
                            chain(dve, "v_chain", dve.scalar_tensor_tensor(g2, g2, 1.0, ps[:, 0:256], ALU.add, ALU.mult))
                            free(name, dve.scalar_tensor_tensor(hrow[:, tt, 0:256], g2, 0.5, ps[:, 256:512],
                                                                ALU.mult, ALU.mult))
                    for tt in range(TT):
                        lo(f"ht{L}.{j}.{tt}", HT, lambda t: t[:, j % 2, 0:kts, tt * P:(tt + 1) * P], kts)

            def log1p(dst, z, w, t):
                chain(dve, "v_chain", dve.tensor_scalar(t, z, 2.0, None, ALU.add))
                chain(dve, "v_chain", dve.reciprocal(t, t))
                chain(dve, "v_chain", dve.tensor_tensor(w, z, t, ALU.mult))
                chain(dve, "v_chain", dve.tensor_tensor(t, w, w, ALU.mult))
                chain(dve, "v_chain", dve.tensor_scalar(dst, t, 1.0 / 15, None, ALU.mult))
                for n in (13, 11, 9, 7, 5, 3):
                    chain(dve, "v_chain", dve.scalar_tensor_tensor(dst, dst, 1.0 / n, t, ALU.add, ALU.mult))
                chain(dve, "v_chain", dve.scalar_tensor_tensor(dst, dst, 1.0, w, ALU.add, ALU.mult))
                chain(dve, "v_chain", dve.tensor_scalar(dst, dst, 2.0, None, ALU.mult))

            def step(ins):
                chain(dve, "v_chain", ins)

            splits(NSPLIT - 1)
            norm_rows(0, lambda tt: x[:, tt, :], lambda tt: None)
            norm_lo(0, XT)
            norm_rows(1, lambda tt: slot(tt, 1024), lambda tt: None)
            dve.wait_ge(ev("const"), 80)
            lam = cg("lam")
            z, w4, t4, l4 = sm("z4", 4), sm("w4", 4), sm("t4", 4), sm("l4", 4)
            step(dve.tensor_scalar(z, lam, -1.0, None, ALU.mult))
            dve.tensor_tensor(z, z, lam, ALU.max).then_inc(ev("lamz"), 1)
            norm_lo(1, MX)
            hsums(sm("cqm", 8), hq(8, P), "xq0.1")
            for tt in range(TT):
                splits(fills[f"uT.{tt}"].pos + AHEAD)
                dve.wait_ge(bank_free[fills[f"uT.{tt}"].bank], fills[f"uT.{tt}"].turn)
            u_, uc = slot(7, 1024), slot(0, 1024)
            cw, cb = cg("cw"), cg("cb")
            dve.wait_ge(bank_full[fills["n1.1.1"].bank], fills["n1.1.1"].turn)
            for f in range(4):
                step(dve.tensor_scalar(uc[:, f * T:(f + 1) * T], u_[:, f * T:(f + 1) * T],
                                       cw[:, 4 * f + 3:4 * f + 4], cb[:, f:f + 1], ALU.mult, ALU.add))
            for s in (1, 2, 3):
                for f in range(4):
                    m = dve.scalar_tensor_tensor(uc[:, f * T + s:(f + 1) * T], u_[:, f * T:(f + 1) * T - s],
                                                 cw[:, 4 * f + 3 - s:4 * f + 4 - s], uc[:, f * T + s:(f + 1) * T],
                                                 ALU.mult, ALU.add)
                    if s < 3 or f < 3:
                        step(m)
            m.then_inc(ev("conv"), 1)
            dve.wait_ge(ev("conv"), 1)
            dve.wait_ge(ev("lamexp"), 1)
            log1p(l4, z, w4, t4)
            step(dve.tensor_scalar(t4, lam, -1.0, 0.0, ALU.mult, ALU.max))
            step(dve.tensor_tensor(l4, l4, t4, ALU.add))
            step(dve.tensor_scalar(sm("lc", 4), l4, -4.0, None, ALU.mult))
            dve.tensor_scalar(sm("hb", 8)[:, 0:8], cg("br", 0, 8), 0.5, None, ALU.mult).then_inc(ev("lru_c"), 1)
            hsums(sm("rk8", 8), hq(8, P), "mk0.1")
            for tt in range(TT):
                splits(fills[f"gateT.{tt}"].pos + AHEAD)
                dve.wait_ge(bank_free[fills[f"gateT.{tt}"].bank], fills[f"gateT.{tt}"].turn)
            gt, r, ig, s8 = slot(10, 1024), slot(1, 1024), slot(2, 1024), slot(8, 1024)
            splits(fills["mv0.1"].pos)
            for g in range(2):
                for half in range(2):
                    nm = fills[f"rg{g}.{half}"]
                    splits(nm.pos + AHEAD)
                    dve.wait_ge(bank_free[nm.bank], nm.turn)
            dve.tensor_scalar(r, r, 0.5, 0.5, ALU.mult, ALU.add).then_inc(ev("rgate"), 1)
            step(dve.tensor_tensor(s8, gt, gt, ALU.mult))
            step(dve.tensor_scalar(s8, s8, 0.044715 * 0.7978845608028654, 0.7978845608028654, ALU.mult, ALU.add))
            dve.tensor_tensor(s8, s8, gt, ALU.mult).then_inc(ev("gcub"), 1)
            step(dve.tensor_scalar(ig, ig, 0.5, 0.5, ALU.mult, ALU.add))
            step(dve.tensor_tensor(uc, uc, ig, ALU.mult))
            dve.wait_ge(ev("gtanh"), 1)
            step(dve.scalar_tensor_tensor(gt, s8, 1.0, gt, ALU.add, ALU.mult))
            dve.wait_ge(ev("dtanh"), 1)
            om = slot(7, 1024)
            step(dve.tensor_scalar(om, r, -1.0, 1.0, ALU.mult, ALU.add))
            step(dve.reciprocal(om, om))
            step(dve.scalar_tensor_tensor(ig, r, 1.0, om, ALU.add, ALU.mult))
            step(dve.scalar_tensor_tensor(om, r, -2.0, om, ALU.mult, ALU.mult))
            dve.scalar_tensor_tensor(s8, ig, 1.0, om, ALU.add, ALU.mult).then_inc(ev("b2"), 1)
            dve.wait_ge(ev("bsq"), 1)
            step(dve.tensor_tensor(uc, uc, s8, ALU.mult))
            for f in range(4):
                step(dve.tensor_tensor_scan(om[:, f * T:(f + 1) * T], ig[:, f * T:(f + 1) * T],
                                            uc[:, f * T:(f + 1) * T], 0.0, ALU.mult, ALU.add))
            dve.scalar_tensor_tensor(om, om, 0.5, gt, ALU.mult, ALU.mult).then_inc(ev("yrow"), 1)
            mem_soft(0)
            dve.wait_ge(ev("yhi"), 1)
            dve.tensor_tensor(MX[1][:, 0:4, :].rearrange("p f t -> p (f t)"), om,
                              MX[0][:, 0:4, :].rearrange("p f t -> p (f t)").bitcast(F32), ALU.subtract).then_inc(ev("ylo"), 1)
            norm_rows(2, lambda tt: slot(tt, 1024), lambda tt: None)
            residual([[f"out0.{nb}.{tt}" for tt in range(TT)] for nb in range(2)])
            norm_lo(2, MX)
            splits(fills["mk1.1"].pos)
            norm_rows(3, lambda tt: x[:, tt, :], lambda tt: None)
            norm_lo(3, XT)
            acts = {"t": 0}
            mlp_side(0, MLP_BLOCKS, 4, True, acts)
            residual([[f"y0.{nb}.{tt}" for tt in range(TT)] for nb in range(2)])
            splits(fills["mv1.1"].pos)
            norm_rows(4, lambda tt: x[:, tt, :], lambda tt: None)
            norm_lo(4, XT)
            fz, lz, lf = sm("fz", 16), sm("lz", 16), sm("lf", 16)
            for tt in range(TT):
                ps = full(f"f.{tt}")
                free(f"f.{tt}", dve.tensor_tensor(fz[:, 8 * tt:8 * tt + 8], ps[:, 0:8], rg("bf"), ALU.add))
            dve.wait_ge(bank_free[fills["f.1"].bank], fills["f.1"].turn)
            step(dve.tensor_scalar(lz, fz, -1.0, None, ALU.mult))
            dve.tensor_tensor(lz, lz, fz, ALU.max).then_inc(ev("absf"), 1)
            dve.wait_ge(ev("expf"), 1)
            w16, t16 = sm("w16", 16), sm("t16", 16)
            log1p(lf, lz, w16, t16)
            step(dve.tensor_scalar(t16, fz, 0.0, None, ALU.min))
            dve.tensor_tensor(lf, t16, lf, ALU.subtract).then_inc(ev("logf"), 1)
            ka = slot(7, 1040).rearrange("p (n d) -> p n d", d=65)
            ps = full("c")
            free("c", dve.tensor_scalar(ka[:, :, 64], ps[:, 0:16], -1.0, None, ALU.mult))
            hsums(sm("rq16", 16), hq(16, 64), "q.1")
            hsums(sm("rk16", 16), hq(16, 64), "k.1")
            splits(fills["xq1.1"].pos)
            soft("fa", 8, True, False, cnt["p"])
            cnt["p"] += len(steps_of(8, True))
            dve.wait_ge(ev("probs"), cnt["p"])
            step(dve.reciprocal(sm("rinv", 16), sm("rsum", 16)))
            for tt in range(TT):
                ps = full(f"fa.o{tt}")
                free(f"fa.o{tt}", dve.tensor_tensor(xn[:, tt, 0:512].rearrange("p (h d) -> p h d", h=8),
                                                    ps[:, :].rearrange("p (h d) -> p h d", h=8),
                                                    bc(sm("rinv", 16)[:, 8 * tt:8 * tt + 8], 2, 64), ALU.mult))
            hsums(sm("cqm", 8), hq(8, P))
            hsums(sm("rk8", 8), hq(8, P))
            for tt in range(TT):
                lo(f"fo.{tt}", MX, lambda t: t[:, 0:4, tt * P:(tt + 1) * P])
            mem_soft(1)
            residual([[f"out1.{nb}.{tt}" for tt in range(TT)] for nb in range(2)])
            norm_rows(5, lambda tt: x[:, tt, :], lambda tt: None)
            norm_lo(5, XT)
            mlp_side(1, MLP_BLOCKS, 4, True, acts)
            residual([[f"y1.{nb}.{tt}" for tt in range(TT)] for nb in range(2)])
            for L in (2, 3):
                i = L - 2
                k = 6 + 2 * i
                norm_rows(k, lambda tt: x[:, tt, :], lambda tt: None)
                norm_lo(k, XT)
                A4, B4 = sm("A4", 4), sm("B4", 4)
                if L == 2:
                    dve.memset(A4, 0.5)
                    step(dve.memset(B4, 0.5))
                else:
                    dve.tensor_tensor(A4, cg("lb", 4, 4), cg("lb", 0, 4), ALU.subtract).then_inc(ev("lbd"), 1)
                    dve.wait_ge(ev("lbt"), 1)
                    step(dve.tensor_scalar(A4, A4, 0.5, 0.5, ALU.mult, ALU.add))
                    step(dve.tensor_scalar(B4, A4, -0.5, 0.5, ALU.mult, ALU.add))
                    step(dve.tensor_tensor(A4, A4, B4, ALU.add))
                F, K, S, Q, X = slot(0, 1024), slot(1, 1024), slot(7, 1024), slot(8, 1024), slot(9, 1024)
                for tt in range(TT):
                    splits(fills[f"hf{L}T.{tt}"].pos + AHEAD)
                    dve.wait_ge(bank_free[fills[f"hf{L}T.{tt}"].bank], fills[f"hf{L}T.{tt}"].turn)
                    dve.wait_ge(bank_full[fills[f"hq{L}T.{tt}"].bank], fills[f"hq{L}T.{tt}"].turn)
                for h in range(4):
                    dve.tensor_scalar(F[:, h * T:(h + 1) * T], S[:, h * T:(h + 1) * T], B4[:, h:h + 1], A4[:, h:h + 1],
                                      ALU.mult, ALU.add)
                step(dve.tensor_scalar(sm("Bn", 4), B4, -1.0, None, ALU.mult))
                for h in range(4):
                    m = dve.tensor_scalar(K[:, h * T:(h + 1) * T], S[:, h * T:(h + 1) * T],
                                          sm("Bn", 4)[:, h:h + 1], B4[:, h:h + 1], ALU.mult, ALU.add)
                m.then_inc(ev("hfk"), 1)
                dve.wait_ge(ev("hfk"), i + 1)
                for tt in range(TT):
                    ps = full(f"hq{L}T.{tt}")
                    dve.wait_ge(ev("hqt"), 2 * i + tt + 1)
                    q = Q.rearrange("p (f t) -> p f t", f=4)[:, :, tt * P:(tt + 1) * P]
                    step(dve.tensor_scalar(q, q, 0.5, 0.5, ALU.mult, ALU.add))
                    free(f"hq{L}T.{tt}", dve.tensor_tensor(q, ps[:, :].rearrange("p (f t) -> p f t", f=4), q, ALU.mult))
                dve.wait_ge(bank_free[fills[f"hq{L}T.1"].bank], fills[f"hq{L}T.1"].turn)

                AT = slot(10, 1024).rearrange("p (g q) -> p g q", g=8)

                def take(l):
                    if l == 0:
                        for tt in range(TT):
                            ps = full(f"lev{L}.0.{tt}")
                            free(f"lev{L}.0.{tt}", dve.tensor_tensor(
                                AT[:, 4 * tt:4 * tt + 4, :], ps[:, :].rearrange("p (h q) -> p h q", h=4),
                                bc(ident, 1, 4), ALU.mult))
                        return
                    ps = full(f"lev{L}.{l}")
                    f = fills[f"lev{L}.{l - 1}" if l > 1 else f"lev{L}.0.1"]
                    dve.wait_ge(bank_free[f.bank], f.turn)
                    if l == LEVELS:
                        free(f"lev{L}.{l}", dve.tensor_copy(slot(11, 512), ps[:, :]))
                        return
                    m_ = 1 << (l - 1)
                    nb = 64 // m_
                    out = AT.rearrange("p g (n two m) -> p g n two m", two=2, m=m_)[:, :, :, 1, :]
                    msk = bc(cst("hmask", 64 * (l - 1), 64).bitcast(U32).rearrange("p (n m) -> p n m", m=m_), 1, 8)
                    data = ps[:, :].rearrange("p (g n m) -> p g n m", g=8, m=m_)
                    free(f"lev{L}.{l}", dve.copy_predicated(out, msk, data))

                for l in range(1, LEVELS + 1):
                    m_ = 1 << (l - 1)
                    v = lambda t: t.rearrange("p (n two m) -> p n two m", two=2, m=m_)
                    f = fills[f"lev{L}.{l - 1}" if l > 1 else f"lev{L}.0.1"]
                    splits(f.pos + AHEAD)
                    dve.wait_ge(bank_full[f.bank], f.turn)
                    dve.wait_ge(ev("lev"), 8 * i + l)
                    dve.tensor_tensor(v(X)[:, :, 0, :], v(K)[:, :, 0, :], v(S)[:, :, 0, :], ALU.mult)
                    dve.tensor_tensor(v(X)[:, :, 1, :], v(Q)[:, :, 1, :], v(F)[:, :, 1, :], ALU.mult).then_inc(ev("xlev"), 1)
                    take(l - 1)
                take(LEVELS)
                sg = slot(6, 1024)
                for tt in range(TT):
                    ps = full(f"hg{L}.{tt}")
                    dve.wait_ge(ev("hgt"), 2 * i + tt + 1)
                    g_ = sg[:, tt * BLK:(tt + 1) * BLK]
                    step(dve.tensor_scalar(g_, g_, 0.5, 0.5, ALU.mult, ALU.add))
                    free(f"hg{L}.{tt}", dve.tensor_tensor(g_, ps[:, :], g_, ALU.mult))
                dve.wait_ge(ev("ngt"), i + 1)
                step(dve.tensor_scalar(sm("ng", 48), sm("ng", 48), 0.5, 0.5, ALU.mult, ALU.add))
                for tt in range(TT):
                    ps = full(f"ho{L}.{tt}")
                    free(f"ho{L}.{tt}", dve.tensor_copy(xn[:, tt, 0:512], ps[:, :]))
                dve.wait_ge(ev("xchi"), i + 1)
                fl = [h[:, :, :, :].rearrange("p a b c -> p (a b c)").rearrange("p (kv c) -> p kv c", kv=2)[:, :, 0:608]
                      for h in HT]
                dve.tensor_tensor(fl[1], scr[:, 10 * SLOT:10 * SLOT + 1216].rearrange("p (kv c) -> p kv c", kv=2),
                                  fl[0].bitcast(F32), ALU.subtract).then_inc(ev("xclo"), 1)
                k0 = 6 + 5 * i
                splits(fills[f"ch{L}.0"].pos - 1)
                hsums(sm("rq16", 16), hq(16, 64))
                dve.wait_ge(ev("hrstd"), k0 + 1)
                step(dve.tensor_scalar(sm("cq", 16), sm("rq16", 16), 0.125, None, ALU.mult))
                hsums(sm("rks", 4), hq(4, 64))
                hsums(sm("rkw", 4), hq(4, 64))
                ch = slot(9, 512)
                n30 = 2 * NCMP
                for kv in range(2):
                    ps = full(f"ch{L}.{kv}")
                    dve.wait_ge(ev("cht"), 2 * i + kv + 1)
                    c_ = ch[0:n30, kv * 256:(kv + 1) * 256]
                    step(dve.tensor_scalar(c_, c_, 0.5, 0.5, ALU.mult, ALU.add))
                    free(f"ch{L}.{kv}", dve.tensor_tensor(c_, ps[0:n30, 0:256], c_, ALU.mult))
                splits(fills[f"chT{L}"].pos)
                dve.wait_ge(bank_free[fills[f"chT{L}"].bank], fills[f"chT{L}"].turn)
                chT = sm("chT", 4 * n30).rearrange("p (j g n) -> p j g n", j=4, g=2)
                rep = slot(10, 2 * 8 * NCMP).rearrange("p (m g r n) -> p m g r n", m=2, g=2, r=4)
                for m_ in range(2):
                    m = dve.tensor_copy(rep[:, m_], bc(chT[:, 2 + m_], 2, 4))
                m.then_inc(ev("chrep"), 1)
                hsums(sm("rkc", 1)[0:n30, :], sm("kct", 64)[0:n30, :])
                ps = full(f"vc{L}")
                n120 = 8 * NCMP
                Z = scr[:, 7 * SLOT:7 * SLOT + 1536].rearrange("p (t g d) -> p t g d", t=2, g=12)
                Zr = scr[:, 9 * SLOT:9 * SLOT + 1536].rearrange("p (t g d) -> p t g d", t=2, g=12)
                tmp = scr[:, 11 * SLOT:11 * SLOT + 768].rearrange("p (t g d) -> p t g d", t=2, g=12)
                cosb = bc(cst("cos").rearrange("p (t d) -> p t d", t=2), 2, 12)
                sinb = bc(cst("sin").rearrange("p (t d) -> p t d", t=2), 2, 12)
                dve.wait_ge(ev("zrow"), i + 1)
                dve.tensor_tensor(Zr[:, :, :, 0:32], Z[:, :, :, 0:32], cosb, ALU.mult)
                step(dve.tensor_tensor(tmp, Z[:, :, :, 32:64], sinb, ALU.mult))
                dve.tensor_tensor(Zr[:, :, :, 0:32], Zr[:, :, :, 0:32], tmp, ALU.subtract).then_inc(ev("ropeD"), 1)
                hsums(sm("rho", 8), hq(8, P))
                for tt in range(TT):
                    dve.wait_ge(ev("hon"), 2 * i + tt + 1)
                    dve.tensor_tensor(xn[:, tt, 0:512], xn[:, tt, 0:512], sg[:, tt * BLK:(tt + 1) * BLK],
                                      ALU.mult).then_inc(ev("hrow"), 1)
                dve.wait_ge(ev("hrow"), 2 * i + 2)
                free(f"vc{L}", dve.tensor_tensor(slot(6, 512)[0:n120, :].rearrange("p (h d) -> p h d", h=8),
                                                 bc(ps[0:n120, 0:64], 1, 8), bc(cst("bd")[0:n120, :], 2, 64), ALU.mult))
                for tt in range(TT):
                    ps = full(f"cs{L}.{tt}")
                    cp = sm(f"cp{tt}", n120)
                    cv = cp.rearrange("p (h n) -> p h n", h=8)
                    free(f"cs{L}.{tt}", dve.tensor_tensor(cv, ps[:, 0:n120].rearrange("p (h n) -> p h n", h=8),
                                                          bc(cst("cadd", NCMP * tt, NCMP), 1, 8), ALU.add), True)
                    m8 = sm(f"cmax{tt}", 8)
                    step(dve.tensor_reduce(m8, cv, AX.X, ALU.max))
                    step(dve.tensor_tensor(cv, cv, bc(m8, 2, NCMP), ALU.subtract))
                    dve.tensor_tensor(cv, cv, bc(sm("cq", 16)[:, 8 * tt:8 * tt + 8], 2, NCMP), ALU.mult).then_inc(ev("cd"), 1)
                ng = sm("ng", 48).rearrange("p (t h b) -> p t h b", t=2, b=3)
                for tt in range(TT):
                    dve.wait_ge(ev("cexp"), 2 * i + tt + 1)
                    cv = sm(f"cp{tt}", n120).rearrange("p (h n) -> p h n", h=8)
                    m8 = sm(f"cinv{tt}", 8)
                    step(dve.tensor_reduce(m8, cv, AX.X, ALU.add))
                    step(dve.reciprocal(m8, m8))
                    step(dve.tensor_tensor(m8, m8, ng[:, tt, :, 0], ALU.mult))
                    step(dve.tensor_tensor(cv, cv, bc(cst("cmul", NCMP * tt, NCMP), 1, 8), ALU.mult))
                    dve.tensor_tensor(cv, cv, bc(m8, 2, NCMP), ALU.mult).then_inc(ev("cprobs"), 1)
                for tt in range(TT):
                    ps = full(f"co{L}.{tt}")
                    free(f"co{L}.{tt}", dve.tensor_copy(xn[:, tt, 512:1024], ps[:, :]), True)
                for b, br in ((1, "sl"), (2, "sw")):
                    soft(f"{br}{L}", 8, True, True, cnt["p"])
                    cnt["p"] += len(steps_of(8, True))
                    dve.wait_ge(ev("probs"), cnt["p"])
                    r16 = sm("rinv", 16)
                    step(dve.reciprocal(r16, sm("rsum", 16)))
                    step(dve.tensor_tensor(r16.rearrange("p (t h) -> p t h", t=2), r16.rearrange("p (t h) -> p t h", t=2),
                                           ng[:, :, :, b], ALU.mult))
                    for tt in range(TT):
                        ps = full(f"{br}{L}.o{tt}")
                        t_ = hrow[:, tt, :]
                        free(f"{br}{L}.o{tt}", dve.tensor_tensor(t_.rearrange("p (h d) -> p h d", h=8),
                                                                 ps[:, :].rearrange("p (h d) -> p h d", h=8),
                                                                 bc(r16[:, 8 * tt:8 * tt + 8], 2, 64), ALU.mult), True)
                        m = dve.tensor_tensor(xn[:, tt, 512:1024], xn[:, tt, 512:1024], t_, ALU.add)
                        if b == 1:
                            step(m)
                        else:
                            m.then_inc(ev("nrow"), 1)
                for tt in range(TT):
                    lo(f"hr{L}.{tt}", MX, lambda t: t[:, 0:4, tt * P:(tt + 1) * P])
                for tt in range(TT):
                    lo(f"nr{L}.{tt}", MX, lambda t: t[:, 4:8, tt * P:(tt + 1) * P])
                residual([[f"out{L}.{nb}.{tt}" for tt in range(TT)] for nb in range(2)])
                norm_rows(k + 1, lambda tt: x[:, tt, :], lambda tt: None)
                norm_lo(k + 1, XT)
                mlp_side(L, FFN_BLOCKS, 2, False, acts)
                residual([[f"y{L}.{nb}.{tt}" for tt in range(TT)] for nb in range(2)])


def _units(w, nk):
    k, n = w.shape
    b = min(n, BLK)
    return np.ascontiguousarray(
        w.reshape(k // (nk * P), nk, P, n // b, b).transpose(3, 0, 2, 1, 4).reshape(-1, P, nk * b))


def _constants():
    c = np.zeros((P, NCONST), np.float32)

    def put(name, v):
        at, w = CONST[name]
        v = np.asarray(v, np.float32).reshape(len(v), -1)
        c[:v.shape[0], at:at + w] = v

    s, t = np.arange(P)[:, None], np.arange(P)[None, :]
    put("ident", s == t)
    put("mask", np.concatenate([np.zeros((P, P)), np.where(t <= s, 0.0, NEG)], 1))
    put("tri", s <= t)
    put("ones", np.ones((P, P)))
    half = 32
    freqs = (np.float32(10000.0) ** (-np.arange(half, dtype=np.float32) / np.float32(half))).astype(np.float32)

    def angles(pos):
        return (pos.astype(np.float32)[:, None] * freqs[None, :]).astype(np.float32)

    ang = angles(np.arange(T)).reshape(TT, P, half).transpose(1, 0, 2)
    put("cos", np.cos(ang).reshape(P, -1))
    put("sin", np.sin(ang).reshape(P, -1))
    cend = np.arange(NCMP) * 16 + 31
    put("ccos", np.cos(angles(np.tile(cend, 2))))
    put("csin", np.sin(angles(np.tile(cend, 2))))
    seen = (cend[None, None, :] <= np.arange(T).reshape(TT, P, 1)).transpose(1, 0, 2)
    put("cadd", np.where(seen, 0.0, NEG))
    put("cmul", seen)
    lev = np.zeros((P, 7, 64))
    for l in range(7):
        m = 1 << l
        k, q = np.arange(P)[:, None], np.arange(64)[None, :]
        lev[:, l] = (k // (2 * m) == q // m) & (k % (2 * m) < m)
    put("hmask", lev)
    put("bd", (np.arange(8 * NCMP)[:, None] // NCMP) == np.arange(8)[None, :])
    return c


def kernel(**inputs):
    import numpy as _np
    import concourse.bacc as _bacc
    from concourse import mybir as _mybir
    from concourse.bass_utils import run_bass_kernel_spmd as _run

    v = {n: _np.asarray(t) for n, t in inputs.items()}
    cat = _np.concatenate
    arr = {"x": v["x"][0], "mem": v["mem"][0], "const": _constants()}
    arr["gains"] = cat([v["norm_mix"][0:1], v["norm_mem"][0:1], v["norm_mem"][1:2], v["norm_mlp"][0:1], v["norm_mix"][1:2],
                        v["norm_mlp"][1:2], v["norm_mix_2"][0:1], v["norm_ffn_2"][0:1], v["norm_mix_2"][1:2],
                        v["norm_ffn_2"][1:2]])
    arr["rowg"] = cat([v["xa_q_gain"][0], v["xa_k_gain"][0], v["xa_q_gain"][1], v["xa_k_gain"][1], v["fox_q_gain"][0],
                       v["fox_k_gain"][0], v["b_forget"][0]]
                      + [t for i in range(2) for t in (v["hg_gnorm_2"][i], v["q_gain_2"][i], v["k_gain_2"][i].ravel())])
    col = lambda t: t.reshape(4, P).T
    arr["colg"] = cat([v["conv_w"][0].reshape(4, 4, P).transpose(2, 1, 0).reshape(P, 16), col(v["conv_b"][0]),
                       col(v["b_rgate"][0]), col(v["b_igate"][0]), col(v["lru_lambda"][0]),
                       col(v["hg_lb_logits_2"][0]), col(v["hg_lb_logits_2"][1])]
                      + [v[n][i].reshape(16, P).T for i in range(2) for n in ("cmp_pe_k_2", "cmp_pe_v_2")], axis=1)
    wg = _np.zeros((P, 8, P), _np.float32)
    for g, n in enumerate(("w_rgate", "w_igate")):
        for b in range(8):
            r = 64 * (b % 2)
            wg[r:r + 64, 4 * g + b // 2, r:r + 64] = v[n][0, b]
    arr["wgate"] = wg.reshape(P, -1)
    arr["w2c"] = _np.stack([_np.stack([v[n][i].reshape(2, P, 64) for n in ("cmp_w2_k_2", "cmp_w2_v_2")])
                            for i in range(2)]).transpose(3, 0, 1, 2, 4).reshape(P, -1)
    wa = v["w_in_a"][0]
    arr["w_a"] = _units(cat([wa[:, 0:512], wa[:, 1024:1536], wa[:, 512:1024]], axis=1), 2)
    for i in range(2):
        arr[f"w_kv{i}"] = _units(v["w_mem_kv"][i], 2)
        arr[f"w_o{i}"] = _units(v["w_out"][i], 2)
        arr[f"w_m{i}"] = _units(v["w_mlp_in"][i], 2)
        w = v["w_mlp_out"][i]
        arr[f"w_n{i}"] = cat([_units(w[j * BLK:(j + 1) * BLK], 2) for j in range(MLP_BLOCKS)])
    wb = v["w_in_b"][0]
    arr["w_b"] = _units(cat([wb[:, 0:1536], wb[:, 1544:2056]], axis=1), 2)
    arr["w_f"] = wb[:, 1536:1544].reshape(1, KT, P, 8).transpose(0, 2, 1, 3).reshape(1, P, KT * 8)
    for L in (2, 3):
        i = L - 2
        w = v["w_in_2"][i]
        arr[f"w_c{L}"] = _units(cat([w[:, 512:1024], w[:, 0:512], w[:, 2560:3072], w[:, 2048:2560], w[:, 1024:1536],
                                     w[:, 1536:2048]], axis=1), 2)
        arr[f"w_d{L}"] = _units(w[:, 3072:3352], 2)
        arr[f"w_w{L}"] = cat([_units(v["cmp_w1_k_2"][i], 4), _units(v["cmp_w1_v_2"][i], 4)])
        arr[f"w_o{L}"] = _units(v["w_out_2"][i], 2)
        g = v["w_ffn_in_2"][i].reshape(D, 2, FFN_BLOCKS, FFN_HALF).transpose(0, 2, 1, 3).reshape(D, -1)
        arr[f"w_m{L}"] = _units(g, 2)
        w = v["w_ffn_out_2"][i]
        arr[f"w_n{L}"] = cat([_units(w[j * FFN_HALF:(j + 1) * FFN_HALF], 2) for j in range(FFN_BLOCKS)])

    nc = _bacc.Bacc("TRN2", target_bir_lowering=False, num_devices=1)
    arrays, args = {}, {}
    for n, t in arr.items():
        t = _np.ascontiguousarray(t)
        arrays[f"in_{n}"] = t
        args[n] = nc.dram_tensor(f"in_{n}", t.shape, _mybir.dt.from_np(t.dtype), kind="ExternalInput").ap()
    args["out"] = nc.dram_tensor("out_0", (T, D), _mybir.dt.float32, kind="ExternalOutput").ap()
    program(nc, args)
    r = _run(nc, [arrays], core_ids=[0])
    return r.results[0]["out_0"].reshape(1, T, D)
```

```python
from contextlib import ExitStack

import concourse.bass as bass
import numpy as np
from concourse import mybir

ACT = mybir.ActivationFunctionType
ALU = mybir.AluOpType
AX = mybir.AxisListType
F32 = mybir.dt.float32
F32R = mybir.dt.float32r
U32 = mybir.dt.uint32

P = 128
T = 256
TT = T // P
D = 1024
KT = D // P
EPS = 1e-6
NEG = -1e30
BLK = 512
UNIT = 1024
NRAW = 8
NSPLIT = 4
AHEAD = NSPLIT - 1
NSLOT = 12
SLOT = 1040
MLP_BLOCKS = 4 * D // BLK
D_FF2 = 2816
FFN_HALF = BLK // 2
FFN_BLOCKS = D_FF2 // FFN_HALF
NCMP = (T - 32) // 16 + 1
LEVELS = 8
NSMALL = 1130

CONST = {}
_at = 0
for _n, _w in (("ident", 128), ("mask", 256), ("tri", 128), ("ones", 128), ("cos", 64), ("sin", 64), ("ccos", 32),
               ("csin", 32), ("cadd", 2 * NCMP), ("cmul", 2 * NCMP), ("hmask", 7 * 64), ("bd", 8)):
    CONST[_n] = (_at, _w)
    _at += _w
NCONST = _at
ROWG = {}
_at = 0
for _n, _w in (("xaq0", 128), ("xak0", 128), ("xaq1", 128), ("xak1", 128), ("foxq", 64), ("foxk", 64), ("bf", 8),
               ("gn2", 128), ("q2", 64), ("k2", 192), ("gn3", 128), ("q3", 64), ("k3", 192)):
    ROWG[_n] = (_at, _w)
    _at += _w
NROWG = _at
COLG = {}
_at = 0
for _n, _w in (("cw", 16), ("cb", 4), ("br", 4), ("bi", 4), ("lam", 4), ("lb", 8), ("pe2", 32), ("pe3", 32)):
    COLG[_n] = (_at, _w)
    _at += _w
NCOLG = _at


def bc(ap, axis, n):
    v = ap.unsqueeze(axis)
    shape = list(v.shape)
    shape[axis] = n
    return v.broadcast_to(shape)


class Fill:

    def __init__(self, bank, turn):
        self.bank, self.turn, self.pos = bank, turn, None


def program(nc, a):
    ctx = ExitStack()
    with ctx:
        def sb(name, shape, dt=F32):
            return ctx.enter_context(nc.sbuf_tensor(name, shape, dt))

        def sem(name):
            return ctx.enter_context(nc.semaphore(name))

        x = sb("x", [P, TT, D])
        xn = sb("xn", [P, TT, D])
        XT = (sb("XT_hi", [P, KT, T], F32R), sb("XT_lo", [P, KT, T], F32R))
        MX = (sb("MX_hi", [P, KT, T], F32R), sb("MX_lo", [P, KT, T], F32R))
        HT = (sb("HT_hi", [P, 2, 4, T], F32R), sb("HT_lo", [P, 2, 4, T], F32R))
        raw = sb("raw", [P, NRAW, UNIT])
        whi = sb("whi", [P, NSPLIT, UNIT], F32R)
        wlo = sb("wlo", [P, NSPLIT, UNIT], F32R)
        gain = sb("gain", [P, 2, D])
        hrow = sb("hrow", [P, TT, BLK])
        scr = sb("scr", [P, NSLOT * SLOT])
        const = sb("const", [P, NCONST])
        rowg = sb("rowg", [P, NROWG])
        colg = sb("colg", [P, NCOLG])
        w2c = sb("w2c", [P, 2, 2, 2, 64])
        powc = sb("powc", [P, 16])
        small = sb("small", [P, NSMALL])
        PS = [ctx.enter_context(nc.psum_tensor(f"ps{i}", [P, BLK], F32)) for i in range(8)]

        def slot(i, w):
            return scr[:, i * SLOT:i * SLOT + w]

        def cst(name, lo=0, w=None):
            at, full = CONST[name]
            return const[:, at + lo:at + lo + (full if w is None else w)]

        def rg(name, lo=0, w=None):
            at, full = ROWG[name]
            return rowg[:, at + lo:at + lo + (full if w is None else w)]

        def cg(name, lo=0, w=None):
            at, full = COLG[name]
            return colg[:, at + lo:at + lo + (full if w is None else w)]

        ident = cst("ident")
        small_at = {}

        def sm(name, w):
            if name not in small_at:
                at = sum(v for _, v in small_at.values())
                assert at + w <= NSMALL, name
                small_at[name] = (at, w)
            at, w0 = small_at[name]
            assert w0 == w, name
            return small[:, at:at + w]

        landed = [sem(f"landed{i}") for i in range(NRAW)]
        split_hi = sem("split_hi")
        split_lo = sem("split_lo")
        unit_used = sem("unit_used")
        bank_full = [sem(f"bank_full{i}") for i in range(8)]
        bank_free = [sem(f"bank_free{i}") for i in range(8)]
        turn_hi = sem("turn_hi")
        events = {}

        def ev(name):
            if name not in events:
                events[name] = sem("ev_" + name)
            return events[name]

        counts = {}

        def chain(eng, name, ins):
            counts[name] = counts.get(name, 0) + 1
            ins.then_inc(ev(name), 1)
            eng.wait_ge(ev(name), counts[name])

        ATTENTION = {"ma0": (4, False, True), "ma1": (4, False, True), "fa": (8, True, False),
                     "sl2": (8, True, True), "sw2": (8, True, True), "sl3": (8, True, True), "sw3": (8, True, True)}

        def steps_of(tags):
            steps = []
            for which, tag in enumerate(tags):
                H, causal, _ = ATTENTION[tag]
                i = 0
                for tt in range(TT):
                    klen = (tt + 1) * P if causal else T
                    n = BLK // klen
                    for h0 in range(0, H, n):
                        steps.append((tag, i, tt, h0, n, klen, which))
                        i += 1
            return steps

        def probs_after(steps, n):
            return sum(ATTENTION[st_[0]][1] for st_ in steps[:n])

        fills = {}
        per_bank = [0] * 8
        units = []
        state = {"pos": 0, "used": 0}

        def open_fill(name, bank):
            per_bank[bank] += 1
            assert name not in fills, name
            fills[name] = Fill(bank, per_bank[bank])
            return fills[name]

        MEM = ({"xq": 3, "mk": 5, "mv": 6}, {"xq": 3, "mk": 5, "mv": 6})
        PROBS = {"ma0": 3, "fa": 0, "ma1": 0, "sl2": 0, "sw2": 0, "sl3": 0, "sw3": 0}
        TURNED = {"ma0": 5, "fa": 1, "ma1": 1, "sl2": 1, "sw2": 1, "sl3": 1, "sw3": 1}
        MASKED = {"fa": 4, "sl2": 10, "sw2": 10, "sl3": 10, "sw3": 10}

        def ring(table, tag, i):
            return scr[:, table[tag] * SLOT + (i % 2) * BLK:table[tag] * SLOT + (i % 2 + 1) * BLK]

        def probs(tag, n):
            return ring(PROBS, tag, n)

        def turned(tag, n):
            return ring(TURNED, tag, n)

        def masked(tag, n):
            return ring(MASKED, tag, n)

        def memT(i, which):
            return slot(((9, 11), (7, 3))[i][which], 1024)

        xflat = xn[:, :, :].rearrange("p t d -> p (t d)")
        pairs_, windows_, chid, chrep = xflat[:, 0:512], xflat[:, 512:1728], xflat[:, 0:512], xflat[:, 512:512 + 16 * NCMP]
        Z_rows, Z_turned = scr[:, 7 * SLOT:7 * SLOT + 1536], scr[:, 0:1536]

        def cpT(tt):
            return slot(5, 1024)[:, tt * P:(tt + 1) * P]

        def cvals():
            return slot(5, 1024)[:, 256:768]

        block = ctx.enter_context(nc.Block())

        @block.tensor
        def _(pe):
            def fill(name, bank):
                f = open_fill(name, bank)
                if f.turn > 1:
                    pe.wait_ge(bank_free[bank], f.turn - 1)
                return PS[bank]

            def close(name, ins):
                f = fills[name]
                ins.then_inc(bank_full[f.bank], 1)
                f.pos = state["used"] + 1 if state["pos"] else 1 - AHEAD

            def read_out(name):
                pe.wait_ge(bank_free[fills[name].bank], fills[name].turn)

            def unit(src, nk):
                g = state["pos"]
                units.append(src)
                state["pos"] = g + 1
                pe.wait_ge(split_lo, g + 1)
                w = src.shape[1] // nk
                hi = whi[:, g % NSPLIT, 0:nk * w].rearrange("p (k n) -> p k n", k=nk)
                lo = wlo[:, g % NSPLIT, 0:nk * w].rearrange("p (k n) -> p k n", k=nk)
                return g, hi, lo, w

            def products(out, xh, xl, wh, wl, first, last, begun=None):
                m = pe.matmul(out, xh, wh, start=first, stop=False)
                if begun is not None:
                    m.then_inc(unit_used, begun)
                    state["used"] += 1
                pe.matmul(out, xh, wl, start=False, stop=False)
                return pe.matmul(out, xl, wh, start=False, stop=last)

            def tok(pair):
                return lambda k, tt: (pair[0][:, k, tt * P:(tt + 1) * P], pair[1][:, k, tt * P:(tt + 1) * P])

            def linear(names, banks, srcs, nk, lhs, k0=0, kn=None, opened=True, closed=True, behind=None):
                kn = len(srcs) * nk if kn is None else kn
                outs = [PS[fills[n].bank] if not opened else fill(n, b) for n, b in zip(names, banks)]
                for i, src in enumerate(srcs):
                    g, hi, lo, w = unit(src, nk)
                    for j in range(nk):
                        k = k0 + i * nk + j
                        for tt, name in enumerate(names):
                            xh, xl = lhs(k, tt)
                            begun = 1 if j == 0 and tt == 0 and g else None
                            last = closed and k == kn - 1
                            m = products(outs[tt][:, 0:w], xh, xl, hi[:, j], lo[:, j],
                                         opened and k == 0, last, begun)
                            if last:
                                close(name, m)
                    if behind and i in behind:
                        behind[i]()

            def by_token(groups, between):
                held = []
                for tt in range(TT):
                    n = 0
                    for names, banks, srcs, nk, lhs, opened, closed in groups:
                        kn = len(srcs) * nk
                        for i, src in enumerate(srcs):
                            if (tt, n) in between:
                                between[(tt, n)]()
                            if tt == 0:
                                held.append(unit(src, nk))
                            g, hi, lo, w = held[n]
                            if i == 0 and opened:
                                fill(names[tt], banks[tt])
                            for j in range(nk):
                                k = i * nk + j
                                xh, xl = lhs(k, tt)
                                begun = 1 if j == 0 and ((tt == 0 and n == 0 and g) or (tt == 1 and n > 0)) else None
                                last = closed and k == kn - 1
                                m = products(PS[fills[names[tt]].bank][:, 0:w], xh, xl, hi[:, j], lo[:, j],
                                             opened and k == 0, last, begun)
                                if last:
                                    close(names[tt], m)
                            n += 1

            def block_by_token(name, w, j, lhs, banks, between):
                by_token([([f"{name}.0", f"{name}.1"], banks, [a[w][4 * j + u] for u in range(4)], 2, lhs, True, True)],
                         between)

            def turn(name, bank, tiles):
                out = fill(name, bank)
                at = 0
                for t in tiles:
                    p, f = t.shape
                    m = pe.transpose(out[0:f, at:at + p], t, ident[0:p, 0:p])
                    at += P
                close(name, m)

            def turn_norm(k, tt):
                pe.wait_ge(ev("xn"), 2 * k + tt + 1)
                for h in range(2):
                    turn(f"n{k}.{tt}.{h}", 6 + h, [xn[:, tt, (4 * h + j) * P:(4 * h + j + 1) * P] for j in range(4)])

            def normed(k, tt):
                for h in range(2):
                    read_out(f"n{k}.{tt}.{h}")

            def after_norm(k, extra=None):
                normed(k, 0)
                return {(0, 3): lambda: turn_norm(k, 1), (1, 0): lambda: normed(k, 1)}

            def out_rows(tag, tt, lo):
                turn(f"{tag}.{tt}", 6 + tt, [xn[:, tt, lo + j * P:lo + (j + 1) * P] for j in range(4)])

            def attend(tags, specs, between):
                steps = steps_of(tags)
                base = state["probs"]

                def scores(n):
                    tag, i, tt, h0, nh, klen, _ = steps[n]
                    hd, kd, qT, kT, V, obank = specs[tag]
                    out = fill(f"{tag}.s{i}", 4 + n % 2)
                    for j in range(nh):
                        m = pe.matmul(out[:, j * klen:(j + 1) * klen], qT(h0 + j)[0:kd, tt * P:(tt + 1) * P],
                                      kT(h0 + j)[0:kd, 0:klen], start=True, stop=True)
                    close(f"{tag}.s{i}", m)

                def turns(n):
                    tag, i = steps[n][0:2]
                    if ATTENTION[tag][1]:
                        pe.wait_ge(ev("probs"), base + probs_after(steps, n + 1))
                    else:
                        read_out(f"{tag}.s{i}")
                    turn(f"{tag}.t{i}", 6 + n % 2, [probs(tag, n)[:, j * P:(j + 1) * P] for j in range(4)])

                def values(n):
                    tag, i, tt, h0, nh, klen, _ = steps[n]
                    hd, kd, qT, kT, V, obank = specs[tag]
                    if h0 == 0:
                        fill(f"{tag}.o{tt}", obank[tt])
                    out = PS[obank[tt]]
                    read_out(f"{tag}.t{i}")
                    kt = klen // P
                    for j in range(nh):
                        h = h0 + j
                        for t in range(kt):
                            m = pe.matmul(out[:, h * hd:(h + 1) * hd],
                                          turned(tag, n)[:, (j * kt + t) * P:(j * kt + t + 1) * P],
                                          V(h, t), start=(t == 0), stop=(t == kt - 1))
                    if h0 + nh == ATTENTION[tag][0]:
                        close(f"{tag}.o{tt}", m)

                scores(0)
                for n in range(len(steps) + 1):
                    if n in between:
                        between[n]()
                    if n + 1 < len(steps):
                        scores(n + 1)
                    if n < len(steps):
                        turns(n)
                    if n > 0:
                        values(n - 1)
                state["probs"] += probs_after(steps, len(steps))

            state["probs"] = 0
            pe.wait_ge(ev("ident"), 16)

            def mem_kv(i, tag, banks=(2, 3)):
                b = a[f"w_kv{i}"]
                j = 0 if tag == "mk" else 1
                linear([f"{tag}{i}.0", f"{tag}{i}.1"], banks, [b[4 * j + u] for u in range(4)], 2, tok(MX))

            def block_of(name, w, j, lhs, banks, behind=None):
                linear([f"{name}.0", f"{name}.1"], banks, [a[w][4 * j + u] for u in range(4)], 2, lhs, behind=behind)

            def mem_queries(i):
                for tt in range(TT):
                    read_out(f"xq{i}.{tt}")
                    turn(f"xqT{i}.{tt}", 6 + tt,
                         [slot(MEM[i]["xq"], 1024)[:, tt * BLK + h * P:tt * BLK + (h + 1) * P] for h in range(4)])

            def mem_keys(i):
                pe.wait_ge(ev("mkn"), i + 1)
                for tt in range(TT):
                    turn(f"mkT{i}.{tt}", 6 + tt,
                         [slot(MEM[i]["mk"], 1024)[:, tt * BLK + h * P:tt * BLK + (h + 1) * P] for h in range(4)])

            def mem_ready(i):
                for tt in range(TT):
                    read_out(f"xqT{i}.{tt}")
                    read_out(f"mkT{i}.{tt}")
                    read_out(f"mv{i}.{tt}")

            def mem_spec(i):
                qT, kT, mv = memT(i, 0), memT(i, 1), slot(MEM[i]["mv"], 1024)
                return (P, P, lambda h: qT[:, h * T:(h + 1) * T], lambda h: kT[:, h * T:(h + 1) * T],
                        lambda h, t: mv[:, t * BLK + h * P:t * BLK + (h + 1) * P], [2, 3])

            def out_proj(L, w, k, first_half, late, second_half):
                names = [f"out{L}.0.0", f"out{L}.0.1"]
                first_half()
                linear(names, [0, 1], [a[w][0]], 2, tok(MX), 0, KT)
                late(0)
                linear(names, [0, 1], [a[w][1]], 2, tok(MX), 2, KT, opened=False)
                late(1)
                for tt in range(TT):
                    read_out(f"{second_half}.{tt}")
                linear(names, [0, 1], [a[w][2], a[w][3]], 2, tok(MX), 4, KT, opened=False)
                block_by_token(f"out{L}.1", w, 1, tok(MX), [2, 3], {(1, 3): lambda: turn_norm(k, 0)})

            def mlp(L, w_in, w_out, blocks, kts, squared, k):
                n = kts // 2
                final = blocks - 1

                def inner(j):
                    if j == 0:
                        block_by_token(f"h{L}.0", w_in, 0, tok(XT), [4, 5], after_norm(k))
                    else:
                        block_of(f"h{L}.{j}", w_in, j, tok(XT), [4, 5])

                def outer_part(j, nb):
                    pair = tuple(h[:, j % 2] for h in HT)
                    return ([f"y{L}.{nb}.0", f"y{L}.{nb}.1"], [2 * nb, 2 * nb + 1],
                            [a[w_out][(2 * j + nb) * n + u] for u in range(n)], 2, tok(pair), j == 0, j == final)

                def outer(j):
                    for tt in range(TT):
                        read_out(f"ht{L}.{j}.{tt}")
                    for nb in range(2):
                        names, banks, srcs, nk, lhs, opened, closed = outer_part(j, nb)
                        linear(names, banks, srcs, nk, lhs, 0, kts, opened=opened, closed=closed)

                def turned_hidden(j, tt):
                    if squared:
                        pe.wait_ge(ev("act"), state["act"] + 2 * j + tt + 1)
                    else:
                        read_out(f"h{L}.{j}.{tt}")
                    turn(f"ht{L}.{j}.{tt}", 6 + tt, [hrow[:, tt, i * P:(i + 1) * P] for i in range(kts)])

                next_norm = {(1, 3): lambda: turn_norm(k + 1, 0)} if k + 1 < 10 else {}
                for j in range(blocks):
                    inner(j)
                    if j > 0 and (squared or j < final):
                        outer(j - 1)
                    if squared or j < final:
                        for tt in range(TT):
                            turned_hidden(j, tt)
                if squared:
                    for tt in range(TT):
                        read_out(f"ht{L}.{final}.{tt}")
                    by_token([outer_part(final, nb) for nb in range(2)], next_norm)
                    state["act"] += 2 * blocks
                else:
                    def second():
                        turned_hidden(final, 1)
                        read_out(f"ht{L}.{final}.0")
                    for tt in range(TT):
                        read_out(f"ht{L}.{final - 1}.{tt}")
                    by_token([outer_part(j, nb) for j in (final - 1, final) for nb in range(2)],
                             {(0, 1): lambda: turned_hidden(final, 0), (0, 2): second,
                              (1, 2): lambda: read_out(f"ht{L}.{final}.1"), **next_norm})

            state["act"] = 0

            turn_norm(0, 0)
            block_by_token("u", "w_a", 0, tok(XT), [0, 1], after_norm(0))

            def u_turned():
                for tt in range(TT):
                    read_out(f"u.{tt}")
                    turn(f"uT.{tt}", 6 + tt,
                         [slot(2, 1024)[:, tt * BLK + f * P:tt * BLK + (f + 1) * P] for f in range(4)])

            block_of("xq0", "w_a", 1, tok(XT), [2, 3],
                     {0: u_turned, 1: lambda: turn_norm(1, 0), 2: lambda: turn_norm(1, 1)})
            for tt in range(TT):
                normed(1, tt)
            mem_kv(0, "mk", [0, 1])
            pe.wait_ge(ev("const"), 16 * 5)
            pe.wait_ge(ev("conv"), 1)
            for g, banks in ((0, (2, 3)), (1, (4, 5))):
                for half in range(2):
                    out = fill(f"rg{g}.{half}", banks[half])
                    for j in range(2):
                        f = 2 * half + j
                        m = pe.matmul(out[:, j * T:(j + 1) * T], slot(8, 1024)[:, (4 * g + f) * P:(4 * g + f + 1) * P],
                                      slot(0, 1024)[:, f * T:(f + 1) * T], start=True, stop=True)
                    close(f"rg{g}.{half}", m)
            block_of("gate", "w_a", 2, tok(XT), [0, 1])
            for tt in range(TT):
                read_out(f"gate.{tt}")
                turn(f"gateT.{tt}", 6 + tt,
                     [slot(4, 1024)[:, tt * BLK + f * P:tt * BLK + (f + 1) * P] for f in range(4)])
            mem_kv(0, "mv")
            mem_queries(0)
            mem_keys(0)
            mem_ready(0)
            attend(["ma0"], {"ma0": mem_spec(0)}, {})
            out_proj(0, "w_o0", 2, lambda: pe.wait_ge(ev("ylo"), 1),
                     lambda tt: (read_out(f"ma0.o{tt}"), out_rows("mo0", tt, 512)), "mo0")
            mlp(0, "w_m0", "w_n0", MLP_BLOCKS, 4, True, 2)
            block_by_token("q", "w_b", 0, tok(XT), [0, 1], after_norm(3))
            for tt in range(TT):
                turn_norm(4, tt)
            linear(["f.0", "f.1"], [4, 5], [a["w_f"][0]], KT, tok(XT))
            block_of("k", "w_b", 1, tok(XT), [2, 3])
            for tt in range(TT):
                normed(4, tt)
            mem_kv(1, "mk", [0, 1])
            pe.wait_ge(ev("logf"), 1)
            out = fill("c", 4)
            lf = sm("lf", 16)
            pe.matmul(out[:, 0:8], cst("tri"), lf[:, 0:8], start=True, stop=True)
            pe.matmul(out[:, 8:16], cst("ones"), lf[:, 0:8], start=True, stop=False)
            close("c", pe.matmul(out[:, 8:16], cst("tri"), lf[:, 8:16], start=False, stop=True))
            block_of("v", "w_b", 2, tok(XT), [2, 3])
            block_of("xq1", "w_b", 3, tok(XT), [0, 1])
            mem_kv(1, "mv")
            for n, s, e in (("fq", 4, "qaug"), ("fk", 7, "kaug")):
                pe.wait_ge(ev(e), 1)
                read_out("c")
                rows = slot(s, 1040).rearrange("p (t h d) -> p t h d", t=2, h=8)
                for tt in range(TT):
                    for half in range(2):
                        turn(f"{n}T.{tt}.{half}", 6 + half, [rows[:, tt, 4 * half + h, :] for h in range(4)])
            for n in ("fq", "fk"):
                for tt in range(TT):
                    for half in range(2):
                        read_out(f"{n}T.{tt}.{half}")
            for tt in range(TT):
                read_out(f"v.{tt}")
            attend(["fa", "ma1"], {
                "fa": (64, 65, lambda h: scr[:, 8 * SLOT + h * T:8 * SLOT + (h + 1) * T],
                       lambda h: scr[:, 10 * SLOT + h * T:10 * SLOT + (h + 1) * T],
                       lambda h, t: slot(2, 1024)[:, t * BLK + h * 64:t * BLK + (h + 1) * 64], [0, 1]),
                "ma1": mem_spec(1)}, {2: lambda: mem_queries(1), 5: lambda: (mem_keys(1), mem_ready(1)),
                                      9: lambda: [(read_out(f"fa.o{tt}"), out_rows("fo", tt, 0)) for tt in range(TT)]})
            out_proj(1, "w_o1", 5, lambda: [read_out(f"fo.{tt}") for tt in range(TT)],
                     lambda tt: (read_out(f"ma1.o{tt}"), out_rows("mo1", tt, 512)), "mo1")
            mlp(1, "w_m1", "w_n1", MLP_BLOCKS, 4, True, 5)

            for L in (2, 3):
                i = L - 2
                k = 6 + 2 * i
                w = f"w_c{L}"
                block_by_token(f"hf{L}", w, 0, tok(XT), [0, 1], after_norm(k))
                block_of(f"hq{L}", w, 1, tok(XT), [2, 3])
                for n, s in ((f"hf{L}", 0), (f"hq{L}", 1)):
                    for tt in range(TT):
                        read_out(f"{n}.{tt}")
                        turn(f"{n}T.{tt}", 6 + tt,
                             [slot(s, 1024)[:, tt * BLK + f * P:tt * BLK + (f + 1) * P] for f in range(4)])

                def level(l):
                    if l == 0:
                        read_out(f"hq{L}T.1")
                    else:
                        pe.wait_ge(ev("xlev"), 8 * i + l)
                    q, kk = slot(8, 1024), slot(1, 1024)
                    X = slot(9, 1024)
                    name = f"lev{L}.{l}"
                    if l == 0:
                        for tt in range(TT):
                            out = fill(f"{name}.{tt}", 4 + tt)
                            for h in range(4):
                                c = h * T + tt * P
                                m = pe.matmul(out[:, h * P:(h + 1) * P], kk[:, c:c + P], q[:, c:c + P],
                                              start=True, stop=True)
                            close(f"{name}.{tt}", m)
                        return
                    out = fill(name, 4 + l % 2)
                    if l == LEVELS:
                        for h in range(4):
                            m = pe.matmul(out[:, h * P:(h + 1) * P], X[:, h * T:h * T + P],
                                          X[:, h * T + P:(h + 1) * T], start=True, stop=True)
                        close(name, m)
                        return
                    s = 1 << (l - 1)
                    for tt in range(TT):
                        for h in range(4):
                            c = h * T + tt * P
                            q2 = X[:, c:c + P].rearrange("p (n two m) -> p n two m", two=2, m=s)[:, :, 1, :]
                            m = pe.matmul(out[:, (tt * 4 + h) * 64:(tt * 4 + h + 1) * 64], X[:, c:c + P], q2,
                                          start=True, stop=True)
                    close(name, m)

                def cmp_turned():
                    for tt in range(TT):
                        read_out(f"A{L}.{tt}")
                    turn(f"cT{L}", 6, [slot(2, 1024)[:, tt * BLK + kv * P:tt * BLK + (kv + 1) * P]
                                       for kv in range(2) for tt in range(TT)])

                def hgrn_out():
                    for tt in range(TT):
                        read_out(f"hi{L}.{tt}")
                    read_out(f"lev{L}.{LEVELS}")
                    AT = slot(10, 1024).rearrange("p (t h q) -> p t h q", t=2, h=4)
                    AX_, vr = slot(11, 512), slot(5, 1024)
                    for tt in range(TT):
                        out = fill(f"ho{L}.{tt}", tt)
                        for h in range(4):
                            o = out[:, h * P:(h + 1) * P]
                            if tt == 1:
                                pe.matmul(o, AX_[:, h * P:(h + 1) * P], vr[:, h * P:(h + 1) * P], start=True, stop=False)
                            m = pe.matmul(o, AT[:, tt, h, :], vr[:, tt * BLK + h * P:tt * BLK + (h + 1) * P],
                                          start=(tt == 0), stop=True)
                        close(f"ho{L}.{tt}", m)

                def ch_turned():
                    read_out(f"ch{L}.0")
                    read_out(f"ch{L}.1")
                    turn(f"chT{L}", 6, [chid[0:2 * NCMP, j * P:(j + 1) * P] for j in range(4)])

                def cmp_keys():
                    read_out(f"chT{L}")
                    chT = sm("chT", 4 * 2 * NCMP).rearrange("p (j n) -> p j n", j=4)
                    out = fill(f"kc{L}", 4)
                    for m_ in range(2):
                        mm = pe.matmul(out[0:2 * NCMP, 0:64], chT[:, m_, :], w2c[:, i, 0, m_, :], start=(m_ == 0),
                                       stop=(m_ == 1))
                    close(f"kc{L}", mm)

                def cmp_values():
                    pe.wait_ge(ev("chrep"), i + 1)
                    rep_ = chrep.rearrange("p (m n) -> p m n", m=2)
                    out = fill(f"vc{L}", 5)
                    for m_ in range(2):
                        mm = pe.matmul(out[0:8 * NCMP, 0:64], rep_[:, m_, :], w2c[:, i, 1, m_, :],
                                       start=(m_ == 0), stop=(m_ == 1))
                    close(f"vc{L}", mm)

                block_of(f"A{L}", w, 2, tok(XT), [0, 1], {1: lambda: level(0), 3: lambda: level(1)})
                linear([f"B{L}.0", f"B{L}.1"], [2, 3], [a[f"w_d{L}"][u] for u in range(4)], 2, tok(XT),
                       behind={1: lambda: level(2), 3: cmp_turned})
                block_of(f"nq{L}", w, 3, tok(XT), [0, 1], {0: lambda: level(3), 2: lambda: level(4)})
                block_of(f"hi{L}", w, 4, tok(XT), [2, 3], {0: lambda: level(5), 2: lambda: level(6)})
                pe.wait_ge(ev("xclo"), i + 1)
                flat = tuple(h[:, :, :, :].rearrange("p a b c -> p (a b c)") for h in HT)
                for kv in range(2):
                    def windows(k_, tt):
                        at = kv * 1024 + k_ * 32
                        return flat[0][:, at:at + P], flat[1][:, at:at + P]
                    linear([f"ch{L}.{kv}"], [kv], [a[f"w_w{L}"][4 * kv + u] for u in range(4)], 4, windows,
                           behind={1: lambda: level(7 + kv)})
                block_of(f"hg{L}", w, 5, tok(XT), [2, 3], {0: hgrn_out, 1: ch_turned, 2: cmp_keys, 3: cmp_values})
                pe.wait_ge(ev("ropeD"), i + 1)
                pe.wait_ge(ev("ropeP"), i + 1)
                Z = Z_turned.rearrange("p (t g d) -> p t g d", t=2, g=12)
                for tt in range(TT):
                    for g in range(3):
                        turn(f"zT{L}.{tt}.{g}", 6 + (tt * 3 + g) % 2, [Z[:, tt, 4 * g + j, :] for j in range(4)])
                pe.wait_ge(ev("kcr"), i + 1)
                turn(f"kcT{L}", 6, [sm("kcr", 64)[0:2 * NCMP, :]])
                for tt in range(TT):
                    for g in range(3):
                        read_out(f"zT{L}.{tt}.{g}")
                read_out(f"kcT{L}")
                qT = scr[:, 7 * SLOT:7 * SLOT + 2048]
                kT = slot(11, 1024)
                kcT = sm("kcT", 2 * NCMP)
                for tt in range(TT):
                    out = fill(f"cs{L}.{tt}", 4 + tt)
                    for h in range(8):
                        g = h // 4
                        m = pe.matmul(out[:, h * NCMP:(h + 1) * NCMP], qT[0:64, h * T + tt * P:h * T + (tt + 1) * P],
                                      kcT[0:64, g * NCMP:(g + 1) * NCMP], start=True, stop=True)
                    close(f"cs{L}.{tt}", m)

                def cmp_probs():
                    for tt in range(TT):
                        pe.wait_ge(ev("cprobs"), 2 * i + tt + 1)
                        turn(f"cpT{L}.{tt}", 6 + tt, [sm(f"cp{tt}", 8 * NCMP)])

                def cmp_out():
                    read_out(f"vc{L}")
                    for tt in range(TT):
                        read_out(f"cpT{L}.{tt}")
                        out = fill(f"co{L}.{tt}", tt)
                        close(f"co{L}.{tt}", pe.matmul(out[:, :], cpT(tt)[0:8 * NCMP, :], cvals()[0:8 * NCMP, :],
                                                       start=True, stop=True))

                attend([f"sl{L}", f"sw{L}"], {
                    f"sl{L}": (64, 64, lambda h: qT[:, h * T:(h + 1) * T],
                               lambda h: kT[:, (h // 4) * T:(h // 4 + 1) * T],
                               lambda h, t: slot(2, 1024)[:, t * BLK + 384 + (h // 4) * 64:t * BLK + 448 + (h // 4) * 64],
                               [2, 3]),
                    f"sw{L}": (64, 64, lambda h: qT[:, h * T:(h + 1) * T],
                               lambda h: kT[:, (2 + h // 4) * T:(3 + h // 4) * T],
                               lambda h, t: slot(3, 1024)[:, t * BLK + 128 + (h // 4) * 64:t * BLK + 192 + (h // 4) * 64],
                               [0, 1])},
                    {1: cmp_probs, 2: cmp_out,
                     9: lambda: [(pe.wait_ge(ev("hrow"), 2 * i + tt + 1), out_rows(f"hr{L}", tt, 0)) for tt in range(TT)]})
                out_proj(L, f"w_o{L}", k + 1, lambda: [read_out(f"hr{L}.{tt}") for tt in range(TT)],
                         lambda tt: (pe.wait_ge(ev("nrow"), 2 * i + tt + 1), out_rows(f"nr{L}", tt, 512)), f"nr{L}")
                mlp(L, f"w_m{L}", f"w_n{L}", FFN_BLOCKS, 2, False, k + 1)

        @block.sync
        def _(sp):
            sp.dma_start(x[:, 0, :], a["x"][0:P, :]).then_inc(ev("xin0"), 16)
            sp.dma_start(ident, a["const"][:, 0:P]).then_inc(ev("ident"), 16)
            sp.dma_start(x[:, 1, :], a["x"][P:T, :]).then_inc(ev("xin1"), 16)
            for g, src in enumerate(units):
                if g >= NRAW:
                    sp.wait_ge(split_lo, g - NRAW + 1)
                sp.dma_start(raw[:, g % NRAW, 0:src.shape[1]], src).then_inc(landed[g % NRAW], 16)
            for tt in range(TT):
                for nb in range(2):
                    f = fills[f"y3.{nb}.{tt}"]
                    sp.wait_ge(bank_free[f.bank], f.turn)
                sp.dma_start(a["out"][tt * P:(tt + 1) * P, :], x[:, tt, :]).then_inc(ev("stored"), 16)
            sp.wait_ge(ev("stored"), 32)

        @block.scalar
        def _(act):
            st = {"g": 0, "hi": 0}
            def splits(n):
                while st["g"] < min(n, len(units)):
                    g = st["g"]
                    w = units[g].shape[1]
                    act.wait_ge(landed[g % NRAW], 16 * (g // NRAW + 1))
                    if g >= NSPLIT:
                        act.wait_ge(unit_used, g - NSPLIT + 1)
                    act.activation(whi[:, g % NSPLIT, 0:w], raw[:, g % NRAW, 0:w], ACT.Copy).then_inc(split_hi, 1)
                    st["g"] += 1

            def full(name):
                f = fills[name]
                splits(f.pos + AHEAD)
                act.wait_ge(bank_full[f.bank], f.turn)
                return PS[f.bank]

            def free(name, ins):
                ins.then_inc(bank_free[fills[name].bank], 1)

            def copy_out(name, dst, src=None):
                ps = full(name)
                free(name, act.activation(dst, ps[:, :] if src is None else src(ps), ACT.Copy))

            def hi(name, dst, n=4, w=P):
                ps = full(name)
                src = ps[:, 0:n * w].rearrange("p (k t) -> p k t", k=n)
                act.activation(dst, src, ACT.Copy).then_inc(turn_hi, 1)

            def norm_hi(k, tt, pair):
                for h in range(2):
                    hi(f"n{k}.{tt}.{h}", pair[0][:, 4 * h:4 * h + 4, tt * P:(tt + 1) * P])

            def squares(tt, src):
                act.activation(xn[:, tt, :], src, ACT.Square, accum_out=sm("ssq", 2)[:, tt:tt + 1]).then_inc(ev("ssq"), 1)

            def soft(tags, between):
                steps = steps_of(tags)
                base = cnt["s"]

                def exps(n):
                    tag, i, tt, h0, nh, klen, which = steps[n]
                    H, causal, scaled = ATTENTION[tag]
                    splits(fills[f"{tag}.s{i}"].pos + AHEAD)
                    act.wait_ge(ev("maxed"), base + n + 1)
                    for j in range(nh):
                        c = tt * H + h0 + j
                        src = (masked(tag, n) if causal else PS[fills[f"{tag}.s{i}"].bank])[:, j * klen:(j + 1) * klen]
                        kw = {"scale": sm("cq", 16)[:, c:c + 1]} if scaled else {}
                        m = act.activation(probs(tag, n)[:, j * klen:(j + 1) * klen], src, ACT.Exp,
                                           bias=sm(f"nmax{which}", 16)[:, c:c + 1],
                                           accum_out=sm(f"rsum{which}", 16)[:, c:c + 1], **kw)
                    if causal:
                        m.then_inc(ev("probs"), 1)
                    else:
                        free(f"{tag}.s{i}", m)

                exps(0)
                for n in range(len(steps)):
                    if n in between:
                        between[n]()
                    if n + 1 < len(steps):
                        exps(n + 1)
                    tag, i = steps[n][0:2]
                    copy_out(f"{tag}.t{i}", turned(tag, n))
                cnt["s"] += len(steps)

            cnt = {"s": 0}

            def mem_turned(i, which):
                for tt in range(TT):
                    copy_out(f"{('xqT', 'mkT')[which]}{i}.{tt}",
                             memT(i, which).rearrange("p (h t) -> p h t", h=4)[:, :, tt * P:(tt + 1) * P],
                             lambda ps: ps[:, :].rearrange("p (h t) -> p h t", h=4))

            def mlp_side(L, blocks, kts, squared):
                def relu(j):
                    for tt in range(TT):
                        name = f"h{L}.{j}.{tt}"
                        if squared:
                            ps = full(name)
                            free(name, act.activation(hrow[:, tt, :], ps[:, :], ACT.Relu))
                        else:
                            ps = full(name)
                            act.activation(hrow[:, tt, 256:512], ps[:, 0:256], ACT.Tanh, scale=0.5).then_inc(ev("tanh"), 1)

                def ht(j):
                    for tt in range(TT):
                        hi(f"ht{L}.{j}.{tt}", HT[0][:, j % 2, 0:kts, tt * P:(tt + 1) * P], kts)

                for j in range(blocks):
                    relu(j)
                    ht(j)

            for tt in range(TT):
                act.wait_ge(ev(f"xin{tt}"), 16)
                squares(tt, x[:, tt, :])
            act.dma_start(colg[:, :], a["colg"]).then_inc(ev("const"), 16)
            act.dma_start(slot(8, 1024), a["wgate"]).then_inc(ev("const"), 16)
            act.dma_start(const[:, P:], a["const"][:, P:]).then_inc(ev("const"), 16)
            act.dma_start(rowg[:, :], a["rowg"].partition_broadcast(P)).then_inc(ev("const"), 16)
            act.dma_start(w2c[:, :, :, :, :].rearrange("p a b c d -> p (a b c d)"), a["w2c"]).then_inc(ev("const"), 16)
            for tt in range(TT):
                norm_hi(0, tt, XT)
            for tt in range(TT):
                act.wait_ge(ev("memin"), 32)
                act.wait_ge(bank_full[fills["n0.1.1"].bank], fills["n0.1.1"].turn)
                squares(tt, slot(tt, 1024))
            for tt in range(TT):
                copy_out(f"u.{tt}", slot(2, 1024)[:, tt * BLK:(tt + 1) * BLK])
            for tt in range(TT):
                copy_out(f"uT.{tt}", slot(7, 1024).rearrange("p (f t) -> p f t", f=4)[:, :, tt * P:(tt + 1) * P],
                         lambda ps: ps[:, :].rearrange("p (f t) -> p f t", f=4))
            for tt in range(TT):
                norm_hi(1, tt, MX)
            act.wait_ge(ev("lamz"), 1)
            act.activation(sm("z4", 4), sm("z4", 4), ACT.Exp, scale=-1.0).then_inc(ev("lamexp"), 1)
            for tt in range(TT):
                copy_out(f"xq0.{tt}", slot(3, 1024)[:, tt * BLK:(tt + 1) * BLK])
            for tt in range(TT):
                copy_out(f"mk0.{tt}", slot(5, 1024)[:, tt * BLK:(tt + 1) * BLK])
            act.wait_ge(ev("lru_c"), 1)
            for g, dst in ((0, 1), (1, 2)):
                for half in range(2):
                    ps = full(f"rg{g}.{half}")
                    for j in range(2):
                        f = 2 * half + j
                        m = act.activation(slot(dst, 1024)[:, f * T:(f + 1) * T], ps[:, j * T:(j + 1) * T], ACT.Tanh,
                                           bias=sm("hb", 8)[:, 4 * g + f:4 * g + f + 1], scale=0.5)
                    free(f"rg{g}.{half}", m)
            act.wait_ge(ev("rgate"), 1)
            for f in range(4):
                at = slice(f * T, (f + 1) * T)
                act.activation(slot(11, 1024)[:, at], slot(1, 1024)[:, at], ACT.Tanh, scale=sm("lh", 4)[:, f:f + 1])
            act.wait_ge(ev("gated_in"), 1)
            for f in range(4):
                at = slice(f * T, (f + 1) * T)
                m = act.activation(slot(2, 1024)[:, at], slot(1, 1024)[:, at], ACT.Exp, scale=sm("lc", 4)[:, f:f + 1])
            m.then_inc(ev("decay"), 1)
            for tt in range(TT):
                copy_out(f"gate.{tt}", slot(4, 1024)[:, tt * BLK:(tt + 1) * BLK])
            act.wait_ge(ev("b2"), 1)
            act.activation(slot(8, 1024), slot(8, 1024), ACT.Sqrt, scale=-1.0).then_inc(ev("bsq"), 1)
            for tt in range(TT):
                copy_out(f"gateT.{tt}", slot(10, 1024).rearrange("p (f t) -> p f t", f=4)[:, :, tt * P:(tt + 1) * P],
                         lambda ps: ps[:, :].rearrange("p (f t) -> p f t", f=4))
            for tt in range(TT):
                copy_out(f"mv0.{tt}", slot(6, 1024)[:, tt * BLK:(tt + 1) * BLK])
            act.wait_ge(ev("gcub"), 1)
            act.activation(slot(8, 1024), slot(8, 1024), ACT.Tanh).then_inc(ev("gtanh"), 1)
            mem_turned(0, 0)
            mem_turned(0, 1)
            act.wait_ge(ev("yrow"), 1)
            act.activation(MX[0][:, 0:4, :].rearrange("p f t -> p (f t)"), slot(7, 1024), ACT.Copy).then_inc(ev("yhi"), 1)
            soft(["ma0"], {})
            for tt in range(TT):
                hi(f"mo0.{tt}", MX[0][:, 4:8, tt * P:(tt + 1) * P])

            def norm_x(rows, lastturn, k):
                for tt in range(TT):
                    for nb in range(2):
                        f = fills[f"{rows}.{nb}.{tt}"]
                        splits(f.pos + AHEAD)
                        act.wait_ge(bank_free[f.bank], f.turn)
                    if tt == 0:
                        f = fills[lastturn]
                        act.wait_ge(bank_full[f.bank], f.turn)
                    squares(tt, x[:, tt, :])
                    norm_hi(k, tt, XT)

            norm_x("out0", "mo0.1", 2)
            mlp_side(0, MLP_BLOCKS, 4, True)
            norm_x("y0", "n2.1.1", 3)
            for tt in range(TT):
                act.wait_ge(ev("memin"), 64)
                act.wait_ge(bank_full[fills["n3.1.1"].bank], fills["n3.1.1"].turn)
                squares(tt, slot(8 + tt, 1024))
            for tt in range(TT):
                copy_out(f"q.{tt}", slot(0, 1024)[:, tt * BLK:(tt + 1) * BLK])
            for tt in range(TT):
                norm_hi(4, tt, MX)
            splits(fills["f.1"].pos + AHEAD)
            act.wait_ge(ev("absf"), 1)
            act.activation(sm("lz", 16), sm("lz", 16), ACT.Exp, scale=-1.0).then_inc(ev("expf"), 1)
            for n, s in (("k", 1), ("mk1", 5), ("v", 2), ("xq1", 3), ("mv1", 6)):
                for tt in range(TT):
                    copy_out(f"{n}.{tt}", slot(s, 1024)[:, tt * BLK:(tt + 1) * BLK])
            for n, s in (("fq", 8), ("fk", 10)):
                dst = scr[:, s * SLOT:s * SLOT + 2048].rearrange("p (h t) -> p h t", h=8)
                for tt in range(TT):
                    for half in range(2):
                        copy_out(f"{n}T.{tt}.{half}", dst[0:65, 4 * half:4 * half + 4, tt * P:(tt + 1) * P],
                                 lambda ps: ps[0:65, :].rearrange("p (h t) -> p h t", h=4))
            soft(["fa", "ma1"], {2: lambda: mem_turned(1, 0), 5: lambda: mem_turned(1, 1),
                                 9: lambda: [hi(f"fo.{tt}", MX[0][:, 0:4, tt * P:(tt + 1) * P]) for tt in range(TT)]})
            for tt in range(TT):
                hi(f"mo1.{tt}", MX[0][:, 4:8, tt * P:(tt + 1) * P])
            norm_x("out1", "mo1.1", 5)
            mlp_side(1, MLP_BLOCKS, 4, True)
            for L in (2, 3):
                i = L - 2
                k = 6 + 2 * i
                norm_x(f"y{L - 1}", f"n{k - 1}.1.1", k)
                if L == 3:
                    act.wait_ge(ev("lbd"), 1)
                    act.activation(sm("A4", 4), sm("A4", 4), ACT.Tanh, scale=0.5).then_inc(ev("lbt"), 1)
                for n, s in ((f"hf{L}", 0), (f"hq{L}", 1)):
                    for tt in range(TT):
                        copy_out(f"{n}.{tt}", slot(s, 1024)[:, tt * BLK:(tt + 1) * BLK])
                for tt in range(TT):
                    ps = full(f"hf{L}T.{tt}")
                    free(f"hf{L}T.{tt}", act.activation(
                        slot(7, 1024).rearrange("p (f t) -> p f t", f=4)[:, :, tt * P:(tt + 1) * P],
                        ps[:, :].rearrange("p (f t) -> p f t", f=4), ACT.Tanh, scale=0.5))
                for tt in range(TT):
                    ps = full(f"hq{L}T.{tt}")
                    act.activation(slot(8, 1024).rearrange("p (f t) -> p f t", f=4)[:, :, tt * P:(tt + 1) * P],
                                   ps[:, :].rearrange("p (f t) -> p f t", f=4), ACT.Tanh, scale=0.5).then_inc(ev("hqt"), 1)
                def rows_in(n, s, w=BLK):
                    for tt in range(TT):
                        copy_out(f"{n}{L}.{tt}", slot(s, 1024)[:, tt * BLK:tt * BLK + w], lambda ps: ps[:, 0:w])

                rows_in("A", 2)
                rows_in("B", 3, 280)
                f = fills[f"B{L}.1"]
                act.wait_ge(bank_free[f.bank], f.turn)
                act.activation(sm("ng", 48).rearrange("p (t c) -> p t c", t=2),
                               slot(3, 1024).rearrange("p (t c) -> p t c", t=2)[:, :, 256:280], ACT.Tanh,
                               scale=0.5).then_inc(ev("ngt"), 1)
                ps = full(f"cT{L}")
                src = ps[:, :].rearrange("p (a b two) -> p a b two", a=4, two=2)
                kk = pairs_.rearrange("p (kv g t) -> p kv g t", kv=2, g=2)
                for par in range(2):
                    for g in range(2):
                        dst = kk[par * 64:(par + 1) * 64, :, g, :].rearrange("p kv (t c) -> p kv t c", t=2)
                        m = act.activation(dst, src[g * 64:(g + 1) * 64, :, :, par].rearrange(
                            "p (kv t) c -> p kv t c", kv=2), ACT.Copy)
                free(f"cT{L}", m)
                rows_in("nq", 4)
                rows_in("hi", 5)
                act.wait_ge(ev("xc"), i + 1)
                flat = HT[0][:, :, :, :].rearrange("p a b c -> p (a b c)").rearrange("p (kv c) -> p kv c", kv=2)
                act.activation(flat[:, :, 0:608], windows_.rearrange("p (kv c) -> p kv c", kv=2),
                               ACT.Copy).then_inc(ev("xchi"), 1)
                for kv in range(2):
                    ps = full(f"ch{L}.{kv}")
                    act.activation(chid[0:2 * NCMP, kv * 256:(kv + 1) * 256], ps[0:2 * NCMP, 0:256], ACT.Tanh,
                                   scale=0.5).then_inc(ev("cht"), 1)
                copy_out(f"chT{L}", sm("chT", 4 * 2 * NCMP).rearrange("p (j n) -> p j n", j=4),
                         lambda ps: ps[:, :].rearrange("p (j n) -> p j n", j=4)[:, :, 0:2 * NCMP])
                copy_out(f"kc{L}", sm("kc", 64)[0:2 * NCMP, :], lambda ps: ps[0:2 * NCMP, 0:64])
                for tt in range(TT):
                    ps = full(f"hg{L}.{tt}")
                    act.activation(slot(6, 1024)[:, tt * BLK:(tt + 1) * BLK], ps[:, :], ACT.Tanh,
                                   scale=0.5).then_inc(ev("hgt"), 1)
                qT = scr[:, 7 * SLOT:7 * SLOT + 2048].rearrange("p (h t) -> p h t", h=8)
                kT = slot(11, 1024).rearrange("p (h t) -> p h t", h=4)
                for tt in range(TT):
                    for g in range(3):
                        dst = qT[0:64, 4 * g:4 * g + 4] if g < 2 else kT[0:64]
                        copy_out(f"zT{L}.{tt}.{g}", dst[:, :, tt * P:(tt + 1) * P],
                                 lambda ps: ps[0:64, :].rearrange("p (h t) -> p h t", h=4))
                copy_out(f"kcT{L}", sm("kcT", 2 * NCMP)[0:64, :], lambda ps: ps[0:64, 0:2 * NCMP])
                for tt in range(TT):
                    act.wait_ge(ev("cd"), 2 * i + tt + 1)
                    act.activation(sm(f"cp{tt}", 8 * NCMP), sm(f"cp{tt}", 8 * NCMP), ACT.Exp).then_inc(ev("cexp"), 1)
                soft([f"sl{L}", f"sw{L}"],
                     {1: lambda: [copy_out(f"cpT{L}.{tt}", cpT(tt)[0:8 * NCMP, :], lambda ps: ps[0:8 * NCMP, 0:P])
                                  for tt in range(TT)],
                      9: lambda: [hi(f"hr{L}.{tt}", MX[0][:, 0:4, tt * P:(tt + 1) * P]) for tt in range(TT)]})
                for tt in range(TT):
                    hi(f"nr{L}.{tt}", MX[0][:, 4:8, tt * P:(tt + 1) * P])
                norm_x(f"out{L}", f"nr{L}.1", k + 1)
                mlp_side(L, FFN_BLOCKS, 2, False)
            splits(len(units))

        @block.gpsimd
        def _(pool):
            pool.memset(powc[:, :], -0.5).then_inc(ev("powc"), 1)

            def load_gain(k):
                if k >= 2:
                    pool.wait_ge(ev("xn"), 2 * (k - 1))
                pool.dma_start(gain[:, k % 2, :], a["gains"][k, :].partition_broadcast(P)).then_inc(ev(f"gain{k % 2}"), 16)

            def rstd(src, n, width, event=None):
                chain(pool, "p_chain", pool.tensor_scalar(src, src, 1.0 / width, EPS, ALU.mult, ALU.add))
                m = pool.tensor_tensor(src, src, powc[0:src.shape[0], 0:n], ALU.pow)
                if event:
                    m.then_inc(ev(event), 1)
                else:
                    chain(pool, "p_chain", m)

            def norm(k):
                for tt in range(TT):
                    pool.wait_ge(ev("ssq"), 2 * k + tt + 1)
                    rstd(sm("ssq", 2)[:, tt:tt + 1], 1, D, "rstd")
                if k + 2 < 10:
                    load_gain(k + 2)

            def squares(src, groups, hd, wait):
                wait()
                pool.tensor_tensor(hrow[:, :, :].rearrange("p a b -> p (a b)")[:, 0:2 * groups * hd], src, src,
                                   ALU.mult).then_inc(ev("sq"), 1)

            def stat(name, n, hd, k):
                pool.wait_ge(ev("hsum"), k + 1)
                rstd(sm(name, n), n, hd, "hrstd")

            def taken(name):
                pool.wait_ge(bank_free[fills[name].bank], fills[name].turn)

            def load_memory(s):
                for tt in range(TT):
                    pool.dma_start(slot(s + tt, 1024), a["mem"][tt * P:(tt + 1) * P, :]).then_inc(ev("memin"), 16)

            load_gain(0)
            pool.wait_ge(ev("xin1"), 16)
            load_memory(0)
            load_gain(1)
            pool.wait_ge(ev("powc"), 1)
            norm(0)
            norm(1)
            pool.wait_ge(ev("const"), 80)

            def headnorm(src, n, hd, name, k, waits):
                squares(src, n // 2, hd, waits)
                stat(name, n, hd, k)

            def scale_rows(dst, src, r, g):
                n, d = src.shape[1], src.shape[2]
                chain(pool, "p_chain", pool.tensor_tensor(dst, src, bc(r, 2, d), ALU.mult))
                return pool.tensor_tensor(dst, dst, bc(g, 1, n), ALU.mult)

            def mem_norms(i, kk):
                c = MEM[i]
                headnorm(slot(c["xq"], 1024), 8, P, "cqm", kk, lambda: (taken(f"xq{i}.0"), taken(f"xq{i}.1")))
                headnorm(slot(c["mk"], 1024), 8, P, "rk8", kk + 1,
                         lambda: (taken(f"mk{i}.0"), taken(f"mk{i}.1"), pool.wait_ge(ev("hrstd"), kk + 1)))
                pool.wait_ge(ev("hrstd"), kk + 2)
                g = sm("gqk", P)
                chain(pool, "p_chain", pool.tensor_tensor(g, rg(f"xaq{i}"), rg(f"xak{i}"), ALU.mult))
                v = slot(c["mk"], 1024).rearrange("p (n d) -> p n d", d=P)
                scale_rows(v, v, sm("rk8", 8), g).then_inc(ev("mkn"), 1)

            mem_norms(0, 0)
            norm(2)
            load_memory(8)

            def square_hidden(L):
                for j in range(MLP_BLOCKS):
                    for tt in range(TT):
                        pool.wait_ge(bank_free[fills[f"h{L}.{j}.{tt}"].bank], fills[f"h{L}.{j}.{tt}"].turn)
                        pool.tensor_tensor(hrow[:, tt, :], hrow[:, tt, :], hrow[:, tt, :], ALU.mult).then_inc(ev("act"), 1)

            square_hidden(0)
            norm(3)
            norm(4)
            headnorm(slot(0, 1024), 16, 64, "rq16", 2, lambda: (taken("q.0"), taken("q.1")))
            headnorm(slot(1, 1024), 16, 64, "rk16", 3, lambda: (taken("k.0"), taken("k.1"), pool.wait_ge(ev("hrstd"), 3)))
            pool.wait_ge(ev("hrstd"), 4)
            g = sm("gqk", P)
            chain(pool, "p_chain", pool.tensor_tensor(g[:, 0:64], rg("foxq"), rg("foxk"), ALU.mult))
            ka = slot(7, 1040).rearrange("p (n d) -> p n d", d=65)
            qa = slot(4, 1040).rearrange("p (n d) -> p n d", d=65)
            q = slot(0, 1024).rearrange("p (n d) -> p n d", d=64)
            k = slot(1, 1024).rearrange("p (n d) -> p n d", d=64)
            pool.memset(qa[:, :, 64:65], 1.0)
            chain(pool, "p_chain", pool.tensor_scalar(sm("rq16", 16), sm("rq16", 16), 0.125, None, ALU.mult))
            pool.tensor_tensor(qa[:, :, 0:64], q, bc(sm("rq16", 16), 2, 64), ALU.mult).then_inc(ev("qaug"), 1)
            scale_rows(ka[:, :, 0:64], k, sm("rk16", 16), g[:, 0:64]).then_inc(ev("kaug"), 1)
            mem_norms(1, 4)
            norm(5)
            square_hidden(1)
            for L in (2, 3):
                i = L - 2
                norm(6 + 2 * i)
                F, S = slot(0, 1024), slot(7, 1024)
                pool.wait_ge(ev("hfk"), i + 1)
                pool.memset(S, 1.0).then_inc(ev("lev"), 1)
                f = fills[f"n{6 + 2 * i}.1.1"]
                pool.wait_ge(bank_full[f.bank], f.turn)
                chain(pool, "p_chain", pool.memset(windows_, 0.0))
                k0 = 6 + 5 * i

                def square_rows(src, dst):
                    pool.tensor_tensor(dst, src, src, ALU.mult).then_inc(ev("sq"), 1)

                def key_squares(s, lo, n_, row):
                    taken(row)
                    square_rows(slot(s, 1024).rearrange("p (t c) -> p t c", t=2)[:, :, lo:lo + P],
                                hrow[:, 0, 0:256].rearrange("p (t c) -> p t c", t=2))

                def windows_in():
                    kk = pairs_.rearrange("p (kv g t) -> p kv g t", kv=2, g=2)
                    X = windows_.rearrange("p (kv c) -> p kv c", kv=2)
                    taken(f"cT{L}")
                    for kv in range(2):
                        for g_ in range(2):
                            dst = X[:, kv, 0:512].rearrange("p (j c) -> p j c", j=16)[:, :, g_ * NCMP:(g_ + 1) * NCMP]
                            lowj = kk[:, kv, g_, 0:8 * NCMP].rearrange("p (n j) -> p j n", j=8)
                            hij = kk[:, kv, g_, 8:8 + 8 * NCMP].rearrange("p (n j) -> p j n", j=8)
                            pe_ = cg(f"pe{L}", 16 * kv, 16)
                            pool.tensor_tensor(dst[:, 0:8], lowj, bc(pe_[:, 0:8], 2, NCMP), ALU.add)
                            m = pool.tensor_tensor(dst[:, 8:16], hij, bc(pe_[:, 8:16], 2, NCMP), ALU.add)
                    m.then_inc(ev("xc"), 1)

                for l in range(1, LEVELS):
                    m_ = 1 << (l - 1)
                    Fv = F.rearrange("p (n two m) -> p n two m", two=2, m=m_)
                    Sv = S.rearrange("p (n two m) -> p n two m", two=2, m=m_)
                    tot = Fv[:, :, 1, m_ - 1]
                    lastf = Fv[:, :, 0, m_ - 1]
                    pool.wait_ge(ev("xlev"), 8 * i + l)
                    chain(pool, "p_chain", pool.tensor_tensor(Sv[:, :, 0, :], Sv[:, :, 0, :], bc(tot, 2, m_), ALU.mult))
                    pool.tensor_tensor(Fv[:, :, 1, :], Fv[:, :, 1, :], bc(lastf, 2, m_), ALU.mult).then_inc(ev("lev"), 1)
                    if l == 3:
                        windows_in()
                    if l == 4:
                        key_squares(2, 256, 0, f"A{L}.1")
                    if l == 5:
                        stat("rks", 4, 64, k0)
                        key_squares(3, 0, 1, f"B{L}.1")
                    if l == 6:
                        stat("rkw", 4, 64, k0 + 1)
                        taken(f"nq{L}.1")
                        square_rows(slot(4, 1024), hrow[:, :, :].rearrange("p a b -> p (a b)"))
                    if l == 7:
                        stat("rq16", 16, 64, k0 + 2)
                pool.wait_ge(ev("hrstd"), k0 + 3)
                pool.wait_ge(ev("xlev"), 8 * i + LEVELS)
                Z = Z_rows.rearrange("p (t g d) -> p t g d", t=2, g=12)
                for tt in range(TT):
                    qv = slot(4, 1024)[:, tt * BLK:(tt + 1) * BLK].rearrange("p (g d) -> p g d", d=64)
                    pool.tensor_tensor(Z[:, tt, 0:8, :], qv, bc(rg(f"q{L}"), 1, 8), ALU.mult)
                    for n_, (s, lo, nm) in enumerate(((2, 256, "rks"), (3, 0, "rkw"))):
                        kv_ = slot(s, 1024)[:, tt * BLK + lo:tt * BLK + lo + P].rearrange("p (g d) -> p g d", d=64)
                        m = scale_rows(Z[:, tt, 8 + 2 * n_:10 + 2 * n_, :], kv_, sm(nm, 4)[:, 2 * tt:2 * tt + 2],
                                       rg(f"k{L}", 64 * (n_ + 1), 64))
                m.then_inc(ev("zrow"), 1)
                pool.wait_ge(ev("zrow"), i + 1)
                Zr = Z_turned.rearrange("p (t g d) -> p t g d", t=2, g=12)
                tmp = hrow[:, :, :].rearrange("p a b -> p (a b)")[:, 0:768].rearrange("p (t g d) -> p t g d", t=2, g=12)
                cosb = bc(cst("cos").rearrange("p (t d) -> p t d", t=2), 2, 12)
                sinb = bc(cst("sin").rearrange("p (t d) -> p t d", t=2), 2, 12)
                pool.tensor_tensor(Zr[:, :, :, 32:64], Z[:, :, :, 32:64], cosb, ALU.mult)
                chain(pool, "p_chain", pool.tensor_tensor(tmp, Z[:, :, :, 0:32], sinb, ALU.mult))
                pool.tensor_tensor(Zr[:, :, :, 32:64], Zr[:, :, :, 32:64], tmp, ALU.add).then_inc(ev("ropeP"), 1)
                taken(f"kc{L}")
                n30 = 2 * NCMP
                kc, kt_ = sm("kc", 64), sm("kct", 64)
                pool.tensor_tensor(kt_[0:n30, :], kc[0:n30, :], kc[0:n30, :], ALU.mult).then_inc(ev("sq"), 1)
                pool.wait_ge(ev("hsum"), k0 + 4)
                rstd(sm("rkc", 1)[0:n30, :], 1, 64, "hrstd")
                pool.wait_ge(ev("hrstd"), k0 + 4)
                chain(pool, "p_chain", pool.tensor_scalar(kc[0:n30, :], kc[0:n30, :], sm("rkc", 1)[0:n30, :], None, ALU.mult))
                chain(pool, "p_chain", pool.tensor_tensor(kc[0:n30, :], kc[0:n30, :], rg(f"k{L}", 0, 64)[0:n30, :], ALU.mult))
                c_, s_ = cst("ccos")[0:n30, :], cst("csin")[0:n30, :]
                kr = sm("kcr", 64)
                x1, x2 = kc[0:n30, 0:32], kc[0:n30, 32:64]
                pool.tensor_tensor(kr[0:n30, 0:32], x1, c_, ALU.mult)
                pool.tensor_tensor(kt_[0:n30, 0:32], x2, s_, ALU.mult)
                pool.tensor_tensor(kr[0:n30, 32:64], x2, c_, ALU.mult)
                chain(pool, "p_chain", pool.tensor_tensor(kt_[0:n30, 32:64], x1, s_, ALU.mult))
                pool.tensor_tensor(kr[0:n30, 0:32], kr[0:n30, 0:32], kt_[0:n30, 0:32], ALU.subtract)
                pool.tensor_tensor(kr[0:n30, 32:64], kr[0:n30, 32:64], kt_[0:n30, 32:64], ALU.add).then_inc(ev("kcr"), 1)
                pool.wait_ge(ev("ropeP"), i + 1)
                ho = slot(10, 1024)
                for tt in range(TT):
                    taken(f"ho{L}.{tt}")
                square_rows(ho, hrow[:, :, :].rearrange("p a b -> p (a b)"))
                pool.wait_ge(ev("hsum"), k0 + 5)
                rstd(sm("rho", 8), 8, P, "hrstd")
                pool.wait_ge(ev("hrstd"), k0 + 5)
                for tt in range(TT):
                    o = ho[:, tt * BLK:(tt + 1) * BLK].rearrange("p (n d) -> p n d", d=P)
                    scale_rows(o, o, sm("rho", 8)[:, 4 * tt:4 * tt + 4], rg(f"gn{L}")).then_inc(ev("hon"), 1)
                norm(7 + 2 * i)

        @block.vector
        def _(dve):
            st = {"g": 0, "hi": 0}

            def splits(n):
                while st["g"] < min(n, len(units)):
                    g = st["g"]
                    w = units[g].shape[1]
                    dve.wait_ge(split_hi, g + 1)
                    dve.tensor_tensor(wlo[:, g % NSPLIT, 0:w], raw[:, g % NRAW, 0:w],
                                      whi[:, g % NSPLIT, 0:w].bitcast(F32), ALU.subtract).then_inc(split_lo, 1)
                    st["g"] += 1

            def full(name):
                f = fills[name]
                splits(f.pos + AHEAD)
                dve.wait_ge(bank_full[f.bank], f.turn)
                return PS[f.bank]

            def free(name, ins, wait=False):
                ins.then_inc(bank_free[fills[name].bank], 1)
                if wait:
                    dve.wait_ge(bank_free[fills[name].bank], fills[name].turn)

            def lo(name, pair, sl, n=4):
                st["hi"] += 1
                ps = full(name)
                dve.wait_ge(turn_hi, st["hi"])
                src = ps[:, 0:n * P].rearrange("p (k t) -> p k t", k=n)
                free(name, dve.tensor_tensor(sl(pair[1]), src, sl(pair[0]).bitcast(F32), ALU.subtract))

            def norm_rows(k, tt, src):
                dve.wait_ge(ev("rstd"), 2 * k + tt + 1)
                dve.wait_ge(ev(f"gain{k % 2}"), 16 * (k // 2 + 1))
                dve.scalar_tensor_tensor(xn[:, tt, :], src, sm("ssq", 2)[:, tt:tt + 1], gain[:, k % 2, :],
                                         ALU.mult, ALU.mult).then_inc(ev("xn"), 1)

            def norm_lo(k, tt, pair):
                for h in range(2):
                    lo(f"n{k}.{tt}.{h}", pair, lambda t: t[:, 4 * h:4 * h + 4, tt * P:(tt + 1) * P])

            def residual(rows, tt):
                for nb in range(2):
                    name = f"{rows}.{nb}.{tt}"
                    ps = full(name)
                    free(name, dve.tensor_tensor(x[:, tt, nb * BLK:(nb + 1) * BLK], ps[:, :],
                                                 x[:, tt, nb * BLK:(nb + 1) * BLK], ALU.add))

            def norm_x(rows, k):
                for tt in range(TT):
                    residual(rows, tt)
                    norm_rows(k, tt, x[:, tt, :])
                    norm_lo(k, tt, XT)

            def hsums(dst, src, after=None):
                if after:
                    splits(fills[after].pos + AHEAD)
                st["hs"] = st.get("hs", 0) + 1
                dve.wait_ge(ev("sq"), st["hs"])
                dve.tensor_reduce(dst, src, AX.X, ALU.add).then_inc(ev("hsum"), 1)

            def hq(n, hd):
                return hrow[:, :, :].rearrange("p a b -> p (a b)")[:, 0:n * hd].rearrange("p (n d) -> p n d", d=hd)

            def soft(tags, between):
                steps = steps_of(tags)
                base = cnt["p"]
                for n, (tag, i, tt, h0, nh, klen, which) in enumerate(steps):
                    H, causal, scaled = ATTENTION[tag]
                    ps = full(f"{tag}.s{i}")
                    c = tt * H + h0
                    mx = sm("mx", 16)[:, c:c + nh]
                    if causal:
                        if n >= 2:
                            dve.wait_ge(ev("probs"), base + probs_after(steps, n - 1))
                        for j in range(nh):
                            m = dve.tensor_tensor_reduce(masked(tag, n)[:, j * klen:(j + 1) * klen],
                                                         ps[:, j * klen:(j + 1) * klen],
                                                         cst("mask", 256 - klen if tt == 0 else 0, klen), 1.0, -3.0e38,
                                                         ALU.add, ALU.max, mx[:, j:j + 1])
                        free(f"{tag}.s{i}", m, True)
                    else:
                        chain(dve, "v_chain", dve.tensor_reduce(
                            mx, ps[:, 0:nh * klen].rearrange("p (h k) -> p h k", h=nh), AX.X, ALU.max))
                    nm = sm(f"nmax{which}", 16)[:, c:c + nh]
                    if scaled:
                        m = dve.scalar_tensor_tensor(nm, mx, -1.0, sm("cq", 16)[:, c:c + nh], ALU.mult, ALU.mult)
                    else:
                        m = dve.tensor_scalar(nm, mx, -1.0, None, ALU.mult)
                    m.then_inc(ev("maxed"), 1)
                    if n in between:
                        between[n]()
                cnt["p"] += probs_after(steps, len(steps))

            def weights_of(tags, tag, tt, base, gate=None):
                steps = steps_of(tags)
                last = max(n for n, s_ in enumerate(steps) if s_[0] == tag and s_[2] == tt)
                H, causal, _ = ATTENTION[tag]
                if causal:
                    dve.wait_ge(ev("probs"), base + probs_after(steps, last + 1))
                else:
                    f = fills[f"{tag}.s{steps[last][1]}"]
                    dve.wait_ge(bank_free[f.bank], f.turn)
                r = sm("rinv", 16)[:, tt * H:(tt + 1) * H]
                chain(dve, "v_chain", dve.reciprocal(r, sm(f"rsum{steps[last][6]}", 16)[:, tt * H:(tt + 1) * H]))
                if gate is not None:
                    chain(dve, "v_chain", dve.tensor_tensor(r, r, gate, ALU.mult))
                return r

            cnt = {"p": 0}

            def rows_out(tags, tag, tt, base, dst):
                H = ATTENTION[tag][0]
                ps = full(f"{tag}.o{tt}")
                r = weights_of(tags, tag, tt, base)
                free(f"{tag}.o{tt}", dve.tensor_tensor(dst.rearrange("p (h d) -> p h d", h=H),
                                                       ps[:, :].rearrange("p (h d) -> p h d", h=H),
                                                       bc(r, 2, BLK // H), ALU.mult))

            def mem_scale(i):
                dve.wait_ge(ev("hrstd"), (1, 5)[i])
                chain(dve, "v_chain", dve.tensor_scalar(sm("cq", 16)[:, 0:8], sm("cqm", 8), P ** -0.5, None, ALU.mult))

            def mlp_side(L, blocks, kts, squared, acts):
                for j in range(blocks):
                    if not squared:
                        for tt in range(TT):
                            name = f"h{L}.{j}.{tt}"
                            ps = full(name)
                            acts["t"] += 1
                            dve.wait_ge(ev("tanh"), acts["t"])
                            g2 = hrow[:, tt, 256:512]
                            chain(dve, "v_chain", dve.scalar_tensor_tensor(g2, g2, 1.0, ps[:, 0:256], ALU.add, ALU.mult))
                            free(name, dve.scalar_tensor_tensor(hrow[:, tt, 0:256], g2, 0.5, ps[:, 256:512],
                                                                ALU.mult, ALU.mult))
                    for tt in range(TT):
                        lo(f"ht{L}.{j}.{tt}", HT, lambda t: t[:, j % 2, 0:kts, tt * P:(tt + 1) * P], kts)

            def log1p(dst, z, w, t):
                chain(dve, "v_chain", dve.tensor_scalar(t, z, 2.0, None, ALU.add))
                chain(dve, "v_chain", dve.reciprocal(t, t))
                chain(dve, "v_chain", dve.tensor_tensor(w, z, t, ALU.mult))
                chain(dve, "v_chain", dve.tensor_tensor(t, w, w, ALU.mult))
                chain(dve, "v_chain", dve.tensor_scalar(dst, t, 1.0 / 15, None, ALU.mult))
                for n in (13, 11, 9, 7, 5, 3):
                    chain(dve, "v_chain", dve.scalar_tensor_tensor(dst, dst, 1.0 / n, t, ALU.add, ALU.mult))
                chain(dve, "v_chain", dve.scalar_tensor_tensor(dst, dst, 1.0, w, ALU.add, ALU.mult))
                chain(dve, "v_chain", dve.tensor_scalar(dst, dst, 2.0, None, ALU.mult))

            def step(ins):
                chain(dve, "v_chain", ins)

            for tt in range(TT):
                norm_rows(0, tt, x[:, tt, :])
            for tt in range(TT):
                norm_lo(0, tt, XT)
            for tt in range(TT):
                norm_rows(1, tt, slot(tt, 1024))
            dve.wait_ge(ev("const"), 80)
            lam = cg("lam")
            z, w4, t4, l4 = sm("z4", 4), sm("w4", 4), sm("t4", 4), sm("l4", 4)
            step(dve.tensor_scalar(z, lam, -1.0, None, ALU.mult))
            dve.tensor_tensor(z, z, lam, ALU.max).then_inc(ev("lamz"), 1)
            for tt in range(TT):
                norm_lo(1, tt, MX)
            xq = fills["xq0.1"].pos
            u_, uc = slot(7, 1024), slot(0, 1024)
            cw, cb = cg("cw"), cg("cb")
            for tt in range(TT):
                dve.wait_ge(bank_free[fills[f"uT.{tt}"].bank], fills[f"uT.{tt}"].turn)
            for f in range(4):
                step(dve.tensor_scalar(uc[:, f * T:(f + 1) * T], u_[:, f * T:(f + 1) * T],
                                       cw[:, 4 * f + 3:4 * f + 4], cb[:, f:f + 1], ALU.mult, ALU.add))
            for s in (1, 2, 3):
                for f in range(4):
                    m = dve.scalar_tensor_tensor(uc[:, f * T + s:(f + 1) * T], u_[:, f * T:(f + 1) * T - s],
                                                 cw[:, 4 * f + 3 - s:4 * f + 4 - s], uc[:, f * T + s:(f + 1) * T],
                                                 ALU.mult, ALU.add)
                    if s < 3 or f < 3:
                        step(m)
                if s < 3:
                    splits(xq + s)
            m.then_inc(ev("conv"), 1)
            dve.wait_ge(ev("conv"), 1)
            splits(xq + AHEAD)
            dve.wait_ge(ev("lamexp"), 1)
            log1p(l4, z, w4, t4)
            step(dve.tensor_scalar(t4, lam, -1.0, 0.0, ALU.mult, ALU.max))
            step(dve.tensor_tensor(l4, l4, t4, ALU.add))
            step(dve.tensor_scalar(sm("lc", 4), l4, -8.0, None, ALU.mult))
            step(dve.tensor_scalar(sm("lh", 4), l4, -4.0, None, ALU.mult))
            dve.tensor_scalar(sm("hb", 8)[:, 0:8], cg("br", 0, 8), 0.5, None, ALU.mult).then_inc(ev("lru_c"), 1)
            hsums(sm("cqm", 8), hq(8, P), "xq0.1")
            hsums(sm("rk8", 8), hq(8, P), "mk0.1")
            r, ig, s8, om = slot(1, 1024), slot(2, 1024), slot(8, 1024), slot(7, 1024)
            for g in range(2):
                for half in range(2):
                    nm = fills[f"rg{g}.{half}"]
                    splits(nm.pos + AHEAD)
                    dve.wait_ge(bank_free[nm.bank], nm.turn)
            dve.tensor_scalar(r, r, 0.5, 0.5, ALU.mult, ALU.add).then_inc(ev("rgate"), 1)
            step(dve.tensor_scalar(ig, ig, 0.5, 0.5, ALU.mult, ALU.add))
            dve.tensor_tensor(uc, uc, ig, ALU.mult).then_inc(ev("gated_in"), 1)
            dve.wait_ge(ev("gated_in"), 1)
            gated = fills["gate.0"].pos
            splits(gated - 2)
            dve.wait_ge(ev("decay"), 1)
            decay, th = ig, slot(11, 1024)
            step(dve.scalar_tensor_tensor(om, decay, 1.0, th, ALU.add, ALU.mult))
            dve.scalar_tensor_tensor(s8, decay, 1.0, om, ALU.add, ALU.mult).then_inc(ev("b2"), 1)
            splits(gated + AHEAD)
            dve.wait_ge(ev("bsq"), 1)
            step(dve.tensor_tensor(uc, uc, s8, ALU.mult))
            for tt in range(TT):
                splits(fills[f"gateT.{tt}"].pos + AHEAD)
                dve.wait_ge(bank_free[fills[f"gateT.{tt}"].bank], fills[f"gateT.{tt}"].turn)
            gt = slot(10, 1024)
            step(dve.tensor_tensor(s8, gt, gt, ALU.mult))
            step(dve.tensor_scalar(s8, s8, 0.044715 * 0.7978845608028654, 0.7978845608028654, ALU.mult, ALU.add))
            dve.tensor_tensor(s8, s8, gt, ALU.mult).then_inc(ev("gcub"), 1)
            splits(fills["mv0.0"].pos)
            for f in range(4):
                step(dve.tensor_tensor_scan(om[:, f * T:(f + 1) * T], decay[:, f * T:(f + 1) * T],
                                            uc[:, f * T:(f + 1) * T], 0.0, ALU.mult, ALU.add))
            splits(fills["mv0.1"].pos + AHEAD)
            dve.wait_ge(ev("gtanh"), 1)
            step(dve.scalar_tensor_tensor(gt, s8, 1.0, gt, ALU.add, ALU.mult))
            dve.scalar_tensor_tensor(om, om, 0.5, gt, ALU.mult, ALU.mult).then_inc(ev("yrow"), 1)
            mem_scale(0)
            dve.wait_ge(ev("yhi"), 1)
            dve.tensor_tensor(MX[1][:, 0:4, :].rearrange("p f t -> p (f t)"), om,
                              MX[0][:, 0:4, :].rearrange("p f t -> p (f t)").bitcast(F32), ALU.subtract).then_inc(ev("ylo"), 1)
            soft(["ma0"], {})
            for tt in range(TT):
                rows_out(["ma0"], "ma0", tt, 0, xn[:, tt, 512:1024])
            for tt in range(TT):
                lo(f"mo0.{tt}", MX, lambda t: t[:, 4:8, tt * P:(tt + 1) * P])
            norm_x("out0", 2)
            acts = {"t": 0}
            mlp_side(0, MLP_BLOCKS, 4, True, acts)
            norm_x("y0", 3)
            for tt in range(TT):
                norm_rows(4, tt, slot(8 + tt, 1024))
            for tt in range(TT):
                norm_lo(4, tt, MX)
            fz, lz, lf = sm("fz", 16), sm("lz", 16), sm("lf", 16)
            for tt in range(TT):
                ps = full(f"f.{tt}")
                free(f"f.{tt}", dve.tensor_tensor(fz[:, 8 * tt:8 * tt + 8], ps[:, 0:8], rg("bf"), ALU.add))
            dve.wait_ge(bank_free[fills["f.1"].bank], fills["f.1"].turn)
            step(dve.tensor_scalar(lz, fz, -1.0, None, ALU.mult))
            dve.tensor_tensor(lz, lz, fz, ALU.max).then_inc(ev("absf"), 1)
            dve.wait_ge(ev("expf"), 1)
            w16, t16 = sm("w16", 16), sm("t16", 16)
            log1p(lf, lz, w16, t16)
            step(dve.tensor_scalar(t16, fz, 0.0, None, ALU.min))
            dve.tensor_tensor(lf, t16, lf, ALU.subtract).then_inc(ev("logf"), 1)
            ka = slot(7, 1040).rearrange("p (n d) -> p n d", d=65)
            ps = full("c")
            free("c", dve.tensor_scalar(ka[:, :, 64], ps[:, 0:16], -1.0, None, ALU.mult))
            hsums(sm("rq16", 16), hq(16, 64), "q.1")
            hsums(sm("rk16", 16), hq(16, 64), "k.1")
            splits(fills["mv1.1"].pos)
            x1, base = ["fa", "ma1"], cnt["p"]
            soft(x1, {1: lambda: hsums(sm("cqm", 8), hq(8, P)),
                      3: lambda: (hsums(sm("rk8", 8), hq(8, P)), rows_out(x1, "fa", 0, base, xn[:, 0, 0:512])),
                      5: lambda: mem_scale(1),
                      8: lambda: rows_out(x1, "fa", 1, base, xn[:, 1, 0:512]),
                      9: lambda: [lo(f"fo.{tt}", MX, lambda t: t[:, 0:4, tt * P:(tt + 1) * P]) for tt in range(TT)]})
            for tt in range(TT):
                rows_out(x1, "ma1", tt, base, xn[:, tt, 512:1024])
            for tt in range(TT):
                lo(f"mo1.{tt}", MX, lambda t: t[:, 4:8, tt * P:(tt + 1) * P])
            norm_x("out1", 5)
            mlp_side(1, MLP_BLOCKS, 4, True, acts)
            for L in (2, 3):
                i = L - 2
                k = 6 + 2 * i
                norm_x(f"y{L - 1}", k)
                A4, B4 = sm("A4", 4), sm("B4", 4)
                if L == 2:
                    dve.memset(A4, 0.5)
                    step(dve.memset(B4, 0.5))
                else:
                    dve.tensor_tensor(A4, cg("lb", 4, 4), cg("lb", 0, 4), ALU.subtract).then_inc(ev("lbd"), 1)
                    dve.wait_ge(ev("lbt"), 1)
                    step(dve.tensor_scalar(A4, A4, 0.5, 0.5, ALU.mult, ALU.add))
                    step(dve.tensor_scalar(B4, A4, -0.5, 0.5, ALU.mult, ALU.add))
                    step(dve.tensor_tensor(A4, A4, B4, ALU.add))
                F, K, S, Q, X = slot(0, 1024), slot(1, 1024), slot(7, 1024), slot(8, 1024), slot(9, 1024)
                for tt in range(TT):
                    splits(fills[f"hf{L}T.{tt}"].pos + AHEAD)
                    dve.wait_ge(bank_free[fills[f"hf{L}T.{tt}"].bank], fills[f"hf{L}T.{tt}"].turn)
                    dve.wait_ge(bank_full[fills[f"hq{L}T.{tt}"].bank], fills[f"hq{L}T.{tt}"].turn)
                for h in range(4):
                    dve.tensor_scalar(F[:, h * T:(h + 1) * T], S[:, h * T:(h + 1) * T], B4[:, h:h + 1], A4[:, h:h + 1],
                                      ALU.mult, ALU.add)
                step(dve.tensor_scalar(sm("Bn", 4), B4, -1.0, None, ALU.mult))
                for h in range(4):
                    m = dve.tensor_scalar(K[:, h * T:(h + 1) * T], S[:, h * T:(h + 1) * T],
                                          sm("Bn", 4)[:, h:h + 1], B4[:, h:h + 1], ALU.mult, ALU.add)
                m.then_inc(ev("hfk"), 1)
                dve.wait_ge(ev("hfk"), i + 1)
                for tt in range(TT):
                    ps = full(f"hq{L}T.{tt}")
                    dve.wait_ge(ev("hqt"), 2 * i + tt + 1)
                    q = Q.rearrange("p (f t) -> p f t", f=4)[:, :, tt * P:(tt + 1) * P]
                    step(dve.tensor_scalar(q, q, 0.5, 0.5, ALU.mult, ALU.add))
                    free(f"hq{L}T.{tt}", dve.tensor_tensor(q, ps[:, :].rearrange("p (f t) -> p f t", f=4), q, ALU.mult))
                dve.wait_ge(bank_free[fills[f"hq{L}T.1"].bank], fills[f"hq{L}T.1"].turn)

                AT = slot(10, 1024).rearrange("p (g q) -> p g q", g=8)

                def take(l):
                    if l == 0:
                        for tt in range(TT):
                            ps = full(f"lev{L}.0.{tt}")
                            free(f"lev{L}.0.{tt}", dve.tensor_tensor(
                                AT[:, 4 * tt:4 * tt + 4, :], ps[:, :].rearrange("p (h q) -> p h q", h=4),
                                bc(ident, 1, 4), ALU.mult))
                        return
                    ps = full(f"lev{L}.{l}")
                    f = fills[f"lev{L}.{l - 1}" if l > 1 else f"lev{L}.0.1"]
                    dve.wait_ge(bank_free[f.bank], f.turn)
                    if l == LEVELS:
                        free(f"lev{L}.{l}", dve.tensor_copy(slot(11, 512), ps[:, :]))
                        return
                    m_ = 1 << (l - 1)
                    nb = 64 // m_
                    out = AT.rearrange("p g (n two m) -> p g n two m", two=2, m=m_)[:, :, :, 1, :]
                    msk = bc(cst("hmask", 64 * (l - 1), 64).bitcast(U32).rearrange("p (n m) -> p n m", m=m_), 1, 8)
                    data = ps[:, :].rearrange("p (g n m) -> p g n m", g=8, m=m_)
                    free(f"lev{L}.{l}", dve.copy_predicated(out, msk, data))

                for l in range(1, LEVELS + 1):
                    m_ = 1 << (l - 1)
                    v = lambda t: t.rearrange("p (n two m) -> p n two m", two=2, m=m_)
                    f = fills[f"lev{L}.{l - 1}" if l > 1 else f"lev{L}.0.1"]
                    splits(f.pos + AHEAD)
                    dve.wait_ge(bank_full[f.bank], f.turn)
                    dve.wait_ge(ev("lev"), 8 * i + l)
                    dve.tensor_tensor(v(X)[:, :, 0, :], v(K)[:, :, 0, :], v(S)[:, :, 0, :], ALU.mult)
                    dve.tensor_tensor(v(X)[:, :, 1, :], v(Q)[:, :, 1, :], v(F)[:, :, 1, :], ALU.mult).then_inc(ev("xlev"), 1)
                    take(l - 1)
                    if l == 5:
                        hsums(sm("rks", 4), hq(4, 64))
                    if l == 6:
                        hsums(sm("rkw", 4), hq(4, 64))
                    if l == 7:
                        dve.wait_ge(ev("xchi"), i + 1)
                        fl = [h[:, :, :, :].rearrange("p a b c -> p (a b c)").rearrange("p (kv c) -> p kv c", kv=2)[:, :, 0:608]
                              for h in HT]
                        dve.tensor_tensor(fl[1], windows_.rearrange("p (kv c) -> p kv c", kv=2),
                                          fl[0].bitcast(F32), ALU.subtract).then_inc(ev("xclo"), 1)
                        hsums(sm("rq16", 16), hq(16, 64))

                n30 = 2 * NCMP

                def ch_silu(kv):
                    ps = full(f"ch{L}.{kv}")
                    dve.wait_ge(ev("cht"), 2 * i + kv + 1)
                    c_ = chid[0:n30, kv * 256:(kv + 1) * 256]
                    step(dve.tensor_scalar(c_, c_, 0.5, 0.5, ALU.mult, ALU.add))
                    free(f"ch{L}.{kv}", dve.tensor_tensor(c_, ps[0:n30, 0:256], c_, ALU.mult))

                ch_silu(0)
                take(LEVELS)
                k0 = 6 + 5 * i
                dve.wait_ge(ev("hrstd"), k0 + 3)
                step(dve.tensor_scalar(sm("cq", 16), sm("rq16", 16), 0.125, None, ALU.mult))
                ch_silu(1)
                for tt in range(TT):
                    ps = full(f"ho{L}.{tt}")
                    free(f"ho{L}.{tt}", dve.tensor_copy(slot(10, 1024)[:, tt * BLK:(tt + 1) * BLK], ps[:, :]))
                splits(fills[f"chT{L}"].pos + AHEAD)
                dve.wait_ge(bank_free[fills[f"chT{L}"].bank], fills[f"chT{L}"].turn)
                chT = sm("chT", 4 * n30).rearrange("p (j g n) -> p j g n", j=4, g=2)
                rep_ = chrep.rearrange("p (m g r n) -> p m g r n", m=2, g=2, r=4)
                for m_ in range(2):
                    m = dve.tensor_copy(rep_[:, m_], bc(chT[:, 2 + m_], 2, 4))
                m.then_inc(ev("chrep"), 1)
                Z = Z_rows.rearrange("p (t g d) -> p t g d", t=2, g=12)
                Zr = Z_turned.rearrange("p (t g d) -> p t g d", t=2, g=12)
                tmp = slot(9, 768).rearrange("p (t g d) -> p t g d", t=2, g=12)
                cosb = bc(cst("cos").rearrange("p (t d) -> p t d", t=2), 2, 12)
                sinb = bc(cst("sin").rearrange("p (t d) -> p t d", t=2), 2, 12)
                dve.wait_ge(ev("zrow"), i + 1)
                dve.tensor_tensor(Zr[:, :, :, 0:32], Z[:, :, :, 0:32], cosb, ALU.mult)
                step(dve.tensor_tensor(tmp, Z[:, :, :, 32:64], sinb, ALU.mult))
                dve.tensor_tensor(Zr[:, :, :, 0:32], Zr[:, :, :, 0:32], tmp, ALU.subtract).then_inc(ev("ropeD"), 1)
                sg = slot(6, 1024)
                for tt in range(TT):
                    ps = full(f"hg{L}.{tt}")
                    dve.wait_ge(ev("hgt"), 2 * i + tt + 1)
                    g_ = sg[:, tt * BLK:(tt + 1) * BLK]
                    step(dve.tensor_scalar(g_, g_, 0.5, 0.5, ALU.mult, ALU.add))
                    free(f"hg{L}.{tt}", dve.tensor_tensor(g_, ps[:, :], g_, ALU.mult))
                dve.wait_ge(ev("ngt"), i + 1)
                step(dve.tensor_scalar(sm("ng", 48), sm("ng", 48), 0.5, 0.5, ALU.mult, ALU.add))
                hsums(sm("rkc", 1)[0:n30, :], sm("kct", 64)[0:n30, :])
                n120 = 8 * NCMP
                ps = full(f"vc{L}")
                free(f"vc{L}", dve.tensor_tensor(cvals()[0:n120, :].rearrange("p (h d) -> p h d", h=8),
                                                 bc(ps[0:n120, 0:64], 1, 8), bc(cst("bd")[0:n120, :], 2, 64), ALU.mult))
                hsums(sm("rho", 8), hq(8, P))
                for tt in range(TT):
                    ps = full(f"cs{L}.{tt}")
                    cp = sm(f"cp{tt}", n120)
                    cv = cp.rearrange("p (h n) -> p h n", h=8)
                    free(f"cs{L}.{tt}", dve.tensor_tensor(cv, ps[:, 0:n120].rearrange("p (h n) -> p h n", h=8),
                                                          bc(cst("cadd", NCMP * tt, NCMP), 1, 8), ALU.add), True)
                    m8 = sm(f"cmax{tt}", 8)
                    step(dve.tensor_reduce(m8, cv, AX.X, ALU.max))
                    step(dve.tensor_tensor(cv, cv, bc(m8, 2, NCMP), ALU.subtract))
                    dve.tensor_tensor(cv, cv, bc(sm("cq", 16)[:, 8 * tt:8 * tt + 8], 2, NCMP), ALU.mult).then_inc(ev("cd"), 1)
                ng = sm("ng", 48).rearrange("p (t h b) -> p t h b", t=2, b=3)

                def hgrn_rows():
                    for tt in range(TT):
                        dve.wait_ge(ev("hon"), 2 * i + tt + 1)
                        dve.tensor_tensor(xn[:, tt, 0:512], slot(10, 1024)[:, tt * BLK:(tt + 1) * BLK],
                                          sg[:, tt * BLK:(tt + 1) * BLK], ALU.mult).then_inc(ev("hrow"), 1)
                    dve.wait_ge(ev("hrow"), 2 * i + 2)

                hgrn_rows()

                def cmp_probs():
                    for tt in range(TT):
                        dve.wait_ge(ev("cexp"), 2 * i + tt + 1)
                        cv = sm(f"cp{tt}", n120).rearrange("p (h n) -> p h n", h=8)
                        m8 = sm(f"cinv{tt}", 8)
                        step(dve.tensor_reduce(m8, cv, AX.X, ALU.add))
                        step(dve.reciprocal(m8, m8))
                        step(dve.tensor_tensor(m8, m8, ng[:, tt, :, 0], ALU.mult))
                        step(dve.tensor_tensor(cv, cv, bc(cst("cmul", NCMP * tt, NCMP), 1, 8), ALU.mult))
                        dve.tensor_tensor(cv, cv, bc(m8, 2, NCMP), ALU.mult).then_inc(ev("cprobs"), 1)

                def cmp_rows():
                    for tt in range(TT):
                        ps = full(f"co{L}.{tt}")
                        free(f"co{L}.{tt}", dve.tensor_copy(xn[:, tt, 512:1024], ps[:, :]), True)

                tags, base = [f"sl{L}", f"sw{L}"], cnt["p"]

                def branch(b, tt):
                    tag = tags[b - 1]
                    ps = full(f"{tag}.o{tt}")
                    r = weights_of(tags, tag, tt, base, ng[:, tt, :, b])
                    t_ = hrow[:, tt, :]
                    free(f"{tag}.o{tt}", dve.tensor_tensor(t_.rearrange("p (h d) -> p h d", h=8),
                                                           ps[:, :].rearrange("p (h d) -> p h d", h=8),
                                                           bc(r, 2, 64), ALU.mult), True)
                    m = dve.tensor_tensor(xn[:, tt, 512:1024], xn[:, tt, 512:1024], t_, ALU.add)
                    if b == 1:
                        step(m)
                    else:
                        m.then_inc(ev("nrow"), 1)

                soft(tags, {0: cmp_probs, 3: cmp_rows, 4: lambda: branch(1, 0), 8: lambda: branch(1, 1),
                            9: lambda: [lo(f"hr{L}.{tt}", MX, lambda t: t[:, 0:4, tt * P:(tt + 1) * P])
                                        for tt in range(TT)],
                            10: lambda: branch(2, 0)})
                branch(2, 1)
                for tt in range(TT):
                    lo(f"nr{L}.{tt}", MX, lambda t: t[:, 4:8, tt * P:(tt + 1) * P])
                norm_x(f"out{L}", k + 1)
                mlp_side(L, FFN_BLOCKS, 2, False, acts)
            for tt in range(TT):
                residual("y3", tt)


def _units(w, nk):
    k, n = w.shape
    b = min(n, BLK)
    return np.ascontiguousarray(
        w.reshape(k // (nk * P), nk, P, n // b, b).transpose(3, 0, 2, 1, 4).reshape(-1, P, nk * b))


def _constants():
    c = np.zeros((P, NCONST), np.float32)

    def put(name, v):
        at, w = CONST[name]
        v = np.asarray(v, np.float32).reshape(len(v), -1)
        c[:v.shape[0], at:at + w] = v

    s, t = np.arange(P)[:, None], np.arange(P)[None, :]
    put("ident", s == t)
    put("mask", np.concatenate([np.zeros((P, P)), np.where(t <= s, 0.0, NEG)], 1))
    put("tri", s <= t)
    put("ones", np.ones((P, P)))
    half = 32
    freqs = (np.float32(10000.0) ** (-np.arange(half, dtype=np.float32) / np.float32(half))).astype(np.float32)

    def angles(pos):
        return (pos.astype(np.float32)[:, None] * freqs[None, :]).astype(np.float32)

    ang = angles(np.arange(T)).reshape(TT, P, half).transpose(1, 0, 2)
    put("cos", np.cos(ang).reshape(P, -1))
    put("sin", np.sin(ang).reshape(P, -1))
    cend = np.arange(NCMP) * 16 + 31
    put("ccos", np.cos(angles(np.tile(cend, 2))))
    put("csin", np.sin(angles(np.tile(cend, 2))))
    seen = (cend[None, None, :] <= np.arange(T).reshape(TT, P, 1)).transpose(1, 0, 2)
    put("cadd", np.where(seen, 0.0, NEG))
    put("cmul", seen)
    lev = np.zeros((P, 7, 64))
    for l in range(7):
        m = 1 << l
        k, q = np.arange(P)[:, None], np.arange(64)[None, :]
        lev[:, l] = (k // (2 * m) == q // m) & (k % (2 * m) < m)
    put("hmask", lev)
    put("bd", (np.arange(8 * NCMP)[:, None] // NCMP) == np.arange(8)[None, :])
    return c


def kernel(**inputs):
    import numpy as _np
    import concourse.bacc as _bacc
    from concourse import mybir as _mybir
    from concourse.bass_utils import run_bass_kernel_spmd as _run

    v = {n: _np.asarray(t) for n, t in inputs.items()}
    cat = _np.concatenate
    arr = {"x": v["x"][0], "mem": v["mem"][0], "const": _constants()}
    arr["gains"] = cat([v["norm_mix"][0:1], v["norm_mem"][0:1], v["norm_mlp"][0:1], v["norm_mix"][1:2], v["norm_mem"][1:2],
                        v["norm_mlp"][1:2], v["norm_mix_2"][0:1], v["norm_ffn_2"][0:1], v["norm_mix_2"][1:2],
                        v["norm_ffn_2"][1:2]])
    arr["rowg"] = cat([v["xa_q_gain"][0], v["xa_k_gain"][0], v["xa_q_gain"][1], v["xa_k_gain"][1], v["fox_q_gain"][0],
                       v["fox_k_gain"][0], v["b_forget"][0]]
                      + [t for i in range(2) for t in (v["hg_gnorm_2"][i], v["q_gain_2"][i], v["k_gain_2"][i].ravel())])
    col = lambda t: t.reshape(4, P).T
    arr["colg"] = cat([v["conv_w"][0].reshape(4, 4, P).transpose(2, 1, 0).reshape(P, 16), col(v["conv_b"][0]),
                       col(v["b_rgate"][0]), col(v["b_igate"][0]), col(v["lru_lambda"][0]),
                       col(v["hg_lb_logits_2"][0]), col(v["hg_lb_logits_2"][1])]
                      + [v[n][i].reshape(16, P).T for i in range(2) for n in ("cmp_pe_k_2", "cmp_pe_v_2")], axis=1)
    wg = _np.zeros((P, 8, P), _np.float32)
    for g, n in enumerate(("w_rgate", "w_igate")):
        for b in range(8):
            r = 64 * (b % 2)
            wg[r:r + 64, 4 * g + b // 2, r:r + 64] = v[n][0, b]
    arr["wgate"] = wg.reshape(P, -1)
    arr["w2c"] = _np.stack([_np.stack([v[n][i].reshape(2, P, 64) for n in ("cmp_w2_k_2", "cmp_w2_v_2")])
                            for i in range(2)]).transpose(3, 0, 1, 2, 4).reshape(P, -1)
    wa = v["w_in_a"][0]
    arr["w_a"] = _units(cat([wa[:, 0:512], wa[:, 1024:1536], wa[:, 512:1024]], axis=1), 2)
    for i in range(2):
        arr[f"w_kv{i}"] = _units(v["w_mem_kv"][i], 2)
        arr[f"w_o{i}"] = _units(v["w_out"][i], 2)
        arr[f"w_m{i}"] = _units(v["w_mlp_in"][i], 2)
        w = v["w_mlp_out"][i]
        arr[f"w_n{i}"] = cat([_units(w[j * BLK:(j + 1) * BLK], 2) for j in range(MLP_BLOCKS)])
    wb = v["w_in_b"][0]
    arr["w_b"] = _units(cat([wb[:, 0:1536], wb[:, 1544:2056]], axis=1), 2)
    arr["w_f"] = wb[:, 1536:1544].reshape(1, KT, P, 8).transpose(0, 2, 1, 3).reshape(1, P, KT * 8)
    for L in (2, 3):
        i = L - 2
        w = v["w_in_2"][i]
        arr[f"w_c{L}"] = _units(cat([w[:, 512:1024], w[:, 0:512], w[:, 2560:3072], w[:, 2048:2560], w[:, 1024:1536],
                                     w[:, 1536:2048]], axis=1), 2)
        arr[f"w_d{L}"] = _units(w[:, 3072:3352], 2)
        arr[f"w_w{L}"] = cat([_units(v["cmp_w1_k_2"][i], 4), _units(v["cmp_w1_v_2"][i], 4)])
        arr[f"w_o{L}"] = _units(v["w_out_2"][i], 2)
        g = v["w_ffn_in_2"][i].reshape(D, 2, FFN_BLOCKS, FFN_HALF).transpose(0, 2, 1, 3).reshape(D, -1)
        arr[f"w_m{L}"] = _units(g, 2)
        w = v["w_ffn_out_2"][i]
        arr[f"w_n{L}"] = cat([_units(w[j * FFN_HALF:(j + 1) * FFN_HALF], 2) for j in range(FFN_BLOCKS)])

    nc = _bacc.Bacc("TRN2", target_bir_lowering=False, num_devices=1)
    arrays, args = {}, {}
    for n, t in arr.items():
        t = _np.ascontiguousarray(t)
        arrays[f"in_{n}"] = t
        args[n] = nc.dram_tensor(f"in_{n}", t.shape, _mybir.dt.from_np(t.dtype), kind="ExternalInput").ap()
    args["out"] = nc.dram_tensor("out_0", (T, D), _mybir.dt.float32, kind="ExternalOutput").ap()
    program(nc, args)
    r = _run(nc, [arrays], core_ids=[0])
    return r.results[0]["out_0"].reshape(1, T, D)
```

```python
from contextlib import ExitStack

import concourse.bass as bass
import numpy as np
from concourse import mybir

ACT = mybir.ActivationFunctionType
ALU = mybir.AluOpType
AX = mybir.AxisListType
F32 = mybir.dt.float32
F32R = mybir.dt.float32r
U32 = mybir.dt.uint32

P = 128
T = 256
TT = T // P
D = 1024
KT = D // P
EPS = 1e-6
NEG = -1e30
BLK = 512
UNIT = 1024
NRAW = 8
NSPLIT = 4
AHEAD = NSPLIT - 1
NSLOT = 12
SLOT = 1040
MLP_BLOCKS = 4 * D // BLK
D_FF2 = 2816
FFN_HALF = BLK // 2
FFN_BLOCKS = D_FF2 // FFN_HALF
NCMP = (T - 32) // 16 + 1
LEVELS = 8
NORMS_OF_X = (0, 2, 3, 5, 6, 7, 8, 9)
NSMALL = 1130

CONST = {}
_at = 0
for _n, _w in (("ident", 128), ("mask", 256), ("tri", 128), ("ones", 128), ("cos", 64), ("sin", 64), ("ccos", 32),
               ("csin", 32), ("cadd", 2 * NCMP), ("cmul", 2 * NCMP), ("hmask", 7 * 64), ("bd", 8)):
    CONST[_n] = (_at, _w)
    _at += _w
NCONST = _at
ROWG = {}
_at = 0
for _n, _w in (("xaq0", 128), ("xak0", 128), ("xaq1", 128), ("xak1", 128), ("foxq", 64), ("foxk", 64), ("bf", 8),
               ("gn2", 128), ("q2", 64), ("k2", 192), ("gn3", 128), ("q3", 64), ("k3", 192)):
    ROWG[_n] = (_at, _w)
    _at += _w
NROWG = _at
COLG = {}
_at = 0
for _n, _w in (("cw", 16), ("cb", 4), ("br", 4), ("bi", 4), ("lam", 4), ("lb", 8), ("pe2", 32), ("pe3", 32)):
    COLG[_n] = (_at, _w)
    _at += _w
NCOLG = _at


def bc(ap, axis, n):
    v = ap.unsqueeze(axis)
    shape = list(v.shape)
    shape[axis] = n
    return v.broadcast_to(shape)


class Fill:

    def __init__(self, bank, turn):
        self.bank, self.turn, self.pos, self.need = bank, turn, None, None


def program(nc, a):
    ctx = ExitStack()
    with ctx:
        def sb(name, shape, dt=F32):
            return ctx.enter_context(nc.sbuf_tensor(name, shape, dt))

        def sem(name):
            return ctx.enter_context(nc.semaphore(name))

        x = sb("x", [P, TT, D])
        xn = sb("xn", [P, TT, D])
        XT = (sb("XT_hi", [P, KT, T], F32R), sb("XT_lo", [P, KT, T], F32R))
        MX = (sb("MX_hi", [P, KT, T], F32R), sb("MX_lo", [P, KT, T], F32R))
        HT = (sb("HT_hi", [P, 2, 4, T], F32R), sb("HT_lo", [P, 2, 4, T], F32R))
        raw = sb("raw", [P, NRAW, UNIT])
        whi = sb("whi", [P, NSPLIT, UNIT], F32R)
        wlo = sb("wlo", [P, NSPLIT, UNIT], F32R)
        gain = sb("gain", [P, 2, D])
        hrow = sb("hrow", [P, TT, BLK])
        scr = sb("scr", [P, NSLOT * SLOT])
        const = sb("const", [P, NCONST])
        rowg = sb("rowg", [P, NROWG])
        colg = sb("colg", [P, NCOLG])
        w2c = sb("w2c", [P, 2, 2, 2, 64])
        powc = sb("powc", [P, 16])
        small = sb("small", [P, NSMALL])
        PS = [ctx.enter_context(nc.psum_tensor(f"ps{i}", [P, BLK], F32)) for i in range(8)]

        def slot(i, w):
            return scr[:, i * SLOT:i * SLOT + w]

        def cst(name, lo=0, w=None):
            at, full = CONST[name]
            return const[:, at + lo:at + lo + (full if w is None else w)]

        def rg(name, lo=0, w=None):
            at, full = ROWG[name]
            return rowg[:, at + lo:at + lo + (full if w is None else w)]

        def cg(name, lo=0, w=None):
            at, full = COLG[name]
            return colg[:, at + lo:at + lo + (full if w is None else w)]

        ident = cst("ident")
        small_at = {}

        def sm(name, w):
            if name not in small_at:
                at = sum(v for _, v in small_at.values())
                assert at + w <= NSMALL, name
                small_at[name] = (at, w)
            at, w0 = small_at[name]
            assert w0 == w, name
            return small[:, at:at + w]

        landed = [sem(f"landed{i}") for i in range(NRAW)]
        split_hi = sem("split_hi")
        split_lo = sem("split_lo")
        pool_lo = sem("pool_lo")
        unit_used = sem("unit_used")
        bank_full = [sem(f"bank_full{i}") for i in range(8)]
        bank_free = [sem(f"bank_free{i}") for i in range(8)]
        turn_hi = sem("turn_hi")
        events = {}

        def ev(name):
            if name not in events:
                events[name] = sem("ev_" + name)
            return events[name]

        counts = {}

        def chain(eng, name, ins):
            counts[name] = counts.get(name, 0) + 1
            ins.then_inc(ev(name), 1)
            eng.wait_ge(ev(name), counts[name])

        ATTENTION = {"ma0": (4, False, True), "ma1": (4, False, True), "fa": (8, True, False),
                     "sl2": (8, True, True), "sw2": (8, True, True), "sl3": (8, True, True), "sw3": (8, True, True)}

        def steps_of(tags):
            steps = []
            for which, tag in enumerate(tags):
                H, causal, _ = ATTENTION[tag]
                i = 0
                for tt in range(TT):
                    klen = (tt + 1) * P if causal else T
                    n = BLK // klen
                    for h0 in range(0, H, n):
                        steps.append((tag, i, tt, h0, n, klen, which))
                        i += 1
            return steps

        def probs_after(steps, n):
            return sum(ATTENTION[st_[0]][1] for st_ in steps[:n])

        fills = {}
        per_bank = [0] * 8
        units = []
        lo_done = []
        pool_units = []
        state = {"pos": 0, "used": 0}

        def open_fill(name, bank):
            per_bank[bank] += 1
            assert name not in fills, name
            fills[name] = Fill(bank, per_bank[bank])
            return fills[name]

        MEM = ({"xq": 3, "mk": 5, "mv": 6}, {"xq": 3, "mk": 5, "mv": 6})
        PROBS = {"ma0": 3, "fa": 0, "ma1": 0, "sl2": 0, "sw2": 0, "sl3": 0, "sw3": 0}
        TURNED = {"ma0": 5, "fa": 1, "ma1": 1, "sl2": 1, "sw2": 1, "sl3": 1, "sw3": 1}
        MASKED = {"fa": 4, "sl2": 10, "sw2": 10, "sl3": 10, "sw3": 10}

        def ring(table, tag, i):
            return scr[:, table[tag] * SLOT + (i % 2) * BLK:table[tag] * SLOT + (i % 2 + 1) * BLK]

        def probs(tag, n):
            return ring(PROBS, tag, n)

        def turned(tag, n):
            return ring(TURNED, tag, n)

        def masked(tag, n):
            return ring(MASKED, tag, n)

        def memT(i, which):
            return slot(((9, 11), (7, 3))[i][which], 1024)

        xflat = xn[:, :, :].rearrange("p t d -> p (t d)")
        pairs_, windows_, chid, chrep = xflat[:, 0:512], xflat[:, 512:1728], xflat[:, 0:512], xflat[:, 512:512 + 16 * NCMP]
        Z_rows, Z_turned = scr[:, 7 * SLOT:7 * SLOT + 1536], scr[:, 0:1536]

        def cpT(tt):
            return slot(5, 1024)[:, tt * P:(tt + 1) * P]

        def cvals():
            return slot(5, 1024)[:, 256:768]

        block = ctx.enter_context(nc.Block())

        @block.tensor
        def _(pe):
            def fill(name, bank):
                f = open_fill(name, bank)
                if f.turn > 1:
                    pe.wait_ge(bank_free[bank], f.turn - 1)
                return PS[bank]

            def close(name, ins):
                f = fills[name]
                ins.then_inc(bank_full[f.bank], 1)
                f.pos = state["used"] + 1 if state["pos"] else 1 - AHEAD
                f.need = state["pos"]

            def read_out(name):
                pe.wait_ge(bank_free[fills[name].bank], fills[name].turn)

            def unit(src, nk, pooled=False):
                g = state["pos"]
                units.append(src)
                state["pos"] = g + 1
                if pooled:
                    pool_units.append(g)
                    lo_done.append((pool_lo, len(pool_units)))
                else:
                    lo_done.append((split_lo, g + 1 - len(pool_units)))
                pe.wait_ge(*lo_done[g])
                w = src.shape[1] // nk
                hi = whi[:, g % NSPLIT, 0:nk * w].rearrange("p (k n) -> p k n", k=nk)
                lo = wlo[:, g % NSPLIT, 0:nk * w].rearrange("p (k n) -> p k n", k=nk)
                return g, hi, lo, w

            def products(out, xh, xl, wh, wl, first, last, begun=None):
                m = pe.matmul(out, xh, wh, start=first, stop=False)
                if begun is not None:
                    m.then_inc(unit_used, begun)
                    state["used"] += 1
                pe.matmul(out, xh, wl, start=False, stop=False)
                return pe.matmul(out, xl, wh, start=False, stop=last)

            def tok(pair):
                return lambda k, tt: (pair[0][:, k, tt * P:(tt + 1) * P], pair[1][:, k, tt * P:(tt + 1) * P])

            def linear(names, banks, srcs, nk, lhs, k0=0, kn=None, opened=True, closed=True, behind=None):
                kn = len(srcs) * nk if kn is None else kn
                outs = [PS[fills[n].bank] if not opened else fill(n, b) for n, b in zip(names, banks)]
                for i, src in enumerate(srcs):
                    g, hi, lo, w = unit(src, nk)
                    for j in range(nk):
                        k = k0 + i * nk + j
                        for tt, name in enumerate(names):
                            xh, xl = lhs(k, tt)
                            begun = 1 if j == 0 and tt == 0 and g else None
                            last = closed and k == kn - 1
                            m = products(outs[tt][:, 0:w], xh, xl, hi[:, j], lo[:, j],
                                         opened and k == 0, last, begun)
                            if last:
                                close(name, m)
                    if behind and i in behind:
                        behind[i]()

            def by_feature(names, banks, srcs, pair, behind=None):
                outs = [fill(n, b) for n, b in zip(names, banks)]
                for i, src in enumerate(srcs):
                    g, hi, lo, w = unit(src, 2)
                    for j in range(2):
                        k = 2 * i + j
                        for f, name in enumerate(names):
                            at = slice(f * P, (f + 1) * P)
                            m = products(outs[f][:, 0:T], hi[:, j, at], lo[:, j, at], pair[0][:, k, :], pair[1][:, k, :],
                                         k == 0, k == KT - 1, 1 if j == 0 and f == 0 and g else None)
                            if k == KT - 1:
                                close(name, m)
                    if behind and i in behind:
                        behind[i]()

            def by_token(groups, between, after=False):
                held = []
                for tt in range(TT):
                    n = 0
                    for names, banks, srcs, nk, lhs, opened, closed in groups:
                        kn = len(srcs) * nk
                        for i, src in enumerate(srcs):
                            if (tt, n) in between:
                                between[(tt, n)]()
                            if tt == 0:
                                held.append(unit(src, nk, after and n == 1))
                            g, hi, lo, w = held[n]
                            if i == 0 and opened:
                                fill(names[tt], banks[tt])
                            for j in range(nk):
                                k = i * nk + j
                                xh, xl = lhs(k, tt)
                                begun = 1 if j == 0 and ((tt == 0 and n == 0 and g) or (tt == 1 and n > 0)) else None
                                last = closed and k == kn - 1
                                m = products(PS[fills[names[tt]].bank][:, 0:w], xh, xl, hi[:, j], lo[:, j],
                                             opened and k == 0, last, begun)
                                if last:
                                    close(names[tt], m)
                            n += 1

            def block_by_token(name, w, j, lhs, banks, between, after=False):
                by_token([([f"{name}.0", f"{name}.1"], banks, [a[w][4 * j + u] for u in range(4)], 2, lhs, True, True)],
                         between, after)

            def turn(name, bank, tiles):
                out = fill(name, bank)
                at = 0
                for t in tiles:
                    p, f = t.shape
                    m = pe.transpose(out[0:f, at:at + p], t, ident[0:p, 0:p])
                    at += P
                close(name, m)

            def turn_norm(k, tt):
                for h in range(2):
                    pe.wait_ge(ev("xn"), 4 * k + 2 * tt + h + 1)
                    turn(f"n{k}.{tt}.{h}", 6 + h, [xn[:, tt, (4 * h + j) * P:(4 * h + j + 1) * P] for j in range(4)])

            def normed(k, tt):
                for h in range(2):
                    read_out(f"n{k}.{tt}.{h}")

            def after_norm(k):
                read_out(f"n{k}.0.0")
                return {(0, 2): lambda: read_out(f"n{k}.0.1"), (0, 3): lambda: turn_norm(k, 1),
                        (1, 0): lambda: read_out(f"n{k}.1.0"), (1, 2): lambda: read_out(f"n{k}.1.1")}

            def out_rows(tag, tt, lo):
                turn(f"{tag}.{tt}", 6 + tt, [xn[:, tt, lo + j * P:lo + (j + 1) * P] for j in range(4)])

            def attend(tags, specs, between):
                steps = steps_of(tags)
                base = state["probs"]

                def scores(n):
                    tag, i, tt, h0, nh, klen, _ = steps[n]
                    hd, kd, qT, kT, V, obank = specs[tag]
                    out = fill(f"{tag}.s{i}", 4 + n % 2)
                    for j in range(nh):
                        m = pe.matmul(out[:, j * klen:(j + 1) * klen], qT(h0 + j)[0:kd, tt * P:(tt + 1) * P],
                                      kT(h0 + j)[0:kd, 0:klen], start=True, stop=True)
                    close(f"{tag}.s{i}", m)

                def turns(n):
                    tag, i = steps[n][0:2]
                    if ATTENTION[tag][1]:
                        pe.wait_ge(ev("probs"), base + probs_after(steps, n + 1))
                    else:
                        read_out(f"{tag}.s{i}")
                    turn(f"{tag}.t{i}", 6 + n % 2, [probs(tag, n)[:, j * P:(j + 1) * P] for j in range(4)])

                def values(n):
                    tag, i, tt, h0, nh, klen, _ = steps[n]
                    hd, kd, qT, kT, V, obank = specs[tag]
                    if h0 == 0:
                        fill(f"{tag}.o{tt}", obank[tt])
                    out = PS[obank[tt]]
                    read_out(f"{tag}.t{i}")
                    kt = klen // P
                    for j in range(nh):
                        h = h0 + j
                        for t in range(kt):
                            m = pe.matmul(out[:, h * hd:(h + 1) * hd],
                                          turned(tag, n)[:, (j * kt + t) * P:(j * kt + t + 1) * P],
                                          V(h, t), start=(t == 0), stop=(t == kt - 1))
                    if h0 + nh == ATTENTION[tag][0]:
                        close(f"{tag}.o{tt}", m)

                scores(0)
                for n in range(len(steps) + 1):
                    if n in between:
                        between[n]()
                    if n + 1 < len(steps):
                        scores(n + 1)
                    if n < len(steps):
                        turns(n)
                    if n > 0:
                        values(n - 1)
                state["probs"] += probs_after(steps, len(steps))

            state["probs"] = 0
            pe.wait_ge(ev("ident"), 16)

            def mem_kv(i, tag, banks=(2, 3)):
                b = a[f"w_kv{i}"]
                j = 0 if tag == "mk" else 1
                linear([f"{tag}{i}.0", f"{tag}{i}.1"], banks, [b[4 * j + u] for u in range(4)], 2, tok(MX))

            def block_of(name, w, j, lhs, banks, behind=None):
                linear([f"{name}.0", f"{name}.1"], banks, [a[w][4 * j + u] for u in range(4)], 2, lhs, behind=behind)

            def mem_queries(i):
                for tt in range(TT):
                    read_out(f"xq{i}.{tt}")
                    turn(f"xqT{i}.{tt}", 6 + tt,
                         [slot(MEM[i]["xq"], 1024)[:, tt * BLK + h * P:tt * BLK + (h + 1) * P] for h in range(4)])

            def mem_keys(i):
                pe.wait_ge(ev("mkn"), i + 1)
                for tt in range(TT):
                    turn(f"mkT{i}.{tt}", 6 + tt,
                         [slot(MEM[i]["mk"], 1024)[:, tt * BLK + h * P:tt * BLK + (h + 1) * P] for h in range(4)])

            def mem_ready(i):
                for tt in range(TT):
                    read_out(f"xqT{i}.{tt}")
                    read_out(f"mkT{i}.{tt}")
                    read_out(f"mv{i}.{tt}")

            def mem_spec(i):
                qT, kT, mv = memT(i, 0), memT(i, 1), slot(MEM[i]["mv"], 1024)
                return (P, P, lambda h: qT[:, h * T:(h + 1) * T], lambda h: kT[:, h * T:(h + 1) * T],
                        lambda h, t: mv[:, t * BLK + h * P:t * BLK + (h + 1) * P], [2, 3])

            def out_proj(L, w, k, first_half, late, second_half):
                names = [f"out{L}.0.0", f"out{L}.0.1"]
                first_half()
                linear(names, [0, 1], [a[w][0]], 2, tok(MX), 0, KT)
                late(0)
                linear(names, [0, 1], [a[w][1]], 2, tok(MX), 2, KT, opened=False)
                late(1)
                for tt in range(TT):
                    read_out(f"{second_half}.{tt}")
                linear(names, [0, 1], [a[w][2], a[w][3]], 2, tok(MX), 4, KT, opened=False)
                block_by_token(f"out{L}.1", w, 1, tok(MX), [2, 3], {(1, 3): lambda: turn_norm(k, 0)})

            def mlp(L, w_in, w_out, blocks, kts, squared, k):
                n = kts // 2
                final = blocks - 1

                def inner(j):
                    if j == 0:
                        block_by_token(f"h{L}.0", w_in, 0, tok(XT), [4, 5], after_norm(k), True)
                        return
                    behind = {1: lambda: turned_hidden(0), 2: lambda: turned_hidden(1)} if j == 1 else {}
                    by_feature([f"h{L}.{j}.{f}" for f in range(4)], [2, 3, 6, 7] if j == 1 else [4, 5, 6, 7],
                               [a[w_in][4 * j + u] for u in range(4)], XT, behind)

                def hidden_ready(j):
                    if j == 0:
                        for tt in range(TT):
                            read_out(f"ht{L}.0.{tt}")
                    else:
                        pe.wait_ge(ev("hid"), state["hid"] + j)

                def outer_part(j, nb):
                    pair = tuple(h[:, j % 2] for h in HT)
                    return ([f"y{L}.{nb}.0", f"y{L}.{nb}.1"], [2 * nb, 2 * nb + 1],
                            [a[w_out][(2 * j + nb) * n + u] for u in range(n)], 2, tok(pair), j == 0, j == final)

                def outer(j):
                    hidden_ready(j)
                    for nb in range(2):
                        names, banks, srcs, nk, lhs, opened, closed = outer_part(j, nb)
                        linear(names, banks, srcs, nk, lhs, 0, kts, opened=opened, closed=closed)

                def turned_hidden(tt):
                    if squared:
                        pe.wait_ge(ev("act"), state["act"] + tt + 1)
                    else:
                        read_out(f"h{L}.0.{tt}")
                    turn(f"ht{L}.0.{tt}", 4 + tt, [hrow[:, tt, i * P:(i + 1) * P] for i in range(kts)])

                next_norm = {(1, 3): lambda: turn_norm(k + 1, 0)} if k + 1 < 10 else {}
                for j in range(blocks):
                    inner(j)
                    if j > 0 and (squared or j < final):
                        outer(j - 1)
                if squared:
                    hidden_ready(final)
                    by_token([outer_part(final, nb) for nb in range(2)], next_norm)
                    state["act"] += TT
                else:
                    hidden_ready(final - 1)
                    by_token([outer_part(j, nb) for j in (final - 1, final) for nb in range(2)],
                             {(0, 2): lambda: hidden_ready(final), **next_norm})
                state["hid"] += final

            state["act"] = state["hid"] = 0

            turn_norm(0, 0)
            block_by_token("u", "w_a", 0, tok(XT), [0, 1], after_norm(0))

            def u_turned():
                for tt in range(TT):
                    read_out(f"u.{tt}")
                    turn(f"uT.{tt}", 6 + tt,
                         [slot(2, 1024)[:, tt * BLK + f * P:tt * BLK + (f + 1) * P] for f in range(4)])

            block_of("xq0", "w_a", 1, tok(XT), [2, 3],
                     {0: u_turned, 2: lambda: turn_norm(1, 0), 3: lambda: turn_norm(1, 1)})
            for tt in range(TT):
                normed(1, tt)
            mem_kv(0, "mk", [0, 1])
            pe.wait_ge(ev("params"), 16 * 3)
            pe.wait_ge(ev("conv"), 1)
            for g, banks in ((0, (2, 3)), (1, (4, 5))):
                for half in range(2):
                    out = fill(f"rg{g}.{half}", banks[half])
                    for j in range(2):
                        f = 2 * half + j
                        m = pe.matmul(out[:, j * T:(j + 1) * T], slot(8, 1024)[:, (4 * g + f) * P:(4 * g + f + 1) * P],
                                      slot(0, 1024)[:, f * T:(f + 1) * T], start=True, stop=True)
                    close(f"rg{g}.{half}", m)
            block_of("gate", "w_a", 2, tok(XT), [0, 1])
            for tt in range(TT):
                read_out(f"gate.{tt}")
                turn(f"gateT.{tt}", 6 + tt,
                     [slot(4, 1024)[:, tt * BLK + f * P:tt * BLK + (f + 1) * P] for f in range(4)])
            mem_kv(0, "mv")
            mem_queries(0)
            mem_keys(0)
            mem_ready(0)
            attend(["ma0"], {"ma0": mem_spec(0)}, {})
            out_proj(0, "w_o0", 2, lambda: pe.wait_ge(ev("ylo"), 1),
                     lambda tt: (read_out(f"ma0.o{tt}"), out_rows("mo0", tt, 512)), "mo0")
            mlp(0, "w_m0", "w_n0", MLP_BLOCKS, 4, True, 2)
            block_by_token("q", "w_b", 0, tok(XT), [0, 1], after_norm(3), True)
            for tt in range(TT):
                turn_norm(4, tt)
            linear(["f.0", "f.1"], [4, 5], [a["w_f"][0]], KT, tok(XT))
            block_of("k", "w_b", 1, tok(XT), [2, 3])
            for tt in range(TT):
                normed(4, tt)
            mem_kv(1, "mk", [0, 1])
            pe.wait_ge(ev("tables"), 32)
            pe.wait_ge(ev("logf"), 1)
            out = fill("c", 4)
            lf = sm("lf", 16)
            pe.matmul(out[:, 0:8], cst("tri"), lf[:, 0:8], start=True, stop=True)
            pe.matmul(out[:, 8:16], cst("ones"), lf[:, 0:8], start=True, stop=False)
            close("c", pe.matmul(out[:, 8:16], cst("tri"), lf[:, 8:16], start=False, stop=True))
            block_of("v", "w_b", 2, tok(XT), [2, 3])
            block_of("xq1", "w_b", 3, tok(XT), [0, 1])
            for n, s, e in (("fq", 4, "qaug"), ("fk", 7, "kaug")):
                pe.wait_ge(ev(e), 1)
                read_out("c")
                rows = slot(s, 1040).rearrange("p (t h d) -> p t h d", t=2, h=8)
                for tt in range(TT):
                    for half in range(2):
                        turn(f"{n}T.{tt}.{half}", 6 + half, [rows[:, tt, 4 * half + h, :] for h in range(4)])
            for n in ("fq", "fk"):
                for tt in range(TT):
                    for half in range(2):
                        read_out(f"{n}T.{tt}.{half}")
            for tt in range(TT):
                read_out(f"v.{tt}")
            def mem_values(u):
                linear(["mv1.0", "mv1.1"], [2, 3], [a["w_kv1"][4 + u]], 2, tok(MX), 2 * u, KT, opened=(u == 0))

            attend(["fa", "ma1"], {
                "fa": (64, 65, lambda h: scr[:, 8 * SLOT + h * T:8 * SLOT + (h + 1) * T],
                       lambda h: scr[:, 10 * SLOT + h * T:10 * SLOT + (h + 1) * T],
                       lambda h, t: slot(2, 1024)[:, t * BLK + h * 64:t * BLK + (h + 1) * 64], [0, 1]),
                "ma1": mem_spec(1)}, {**{1 + u: (lambda u=u: mem_values(u)) for u in (0, 2, 3)},
                                      2: lambda: (mem_values(1), mem_queries(1)), 5: lambda: (mem_keys(1), mem_ready(1)),
                                      9: lambda: [(read_out(f"fa.o{tt}"), out_rows("fo", tt, 0)) for tt in range(TT)]})
            out_proj(1, "w_o1", 5, lambda: [read_out(f"fo.{tt}") for tt in range(TT)],
                     lambda tt: (read_out(f"ma1.o{tt}"), out_rows("mo1", tt, 512)), "mo1")
            mlp(1, "w_m1", "w_n1", MLP_BLOCKS, 4, True, 5)

            for L in (2, 3):
                i = L - 2
                k = 6 + 2 * i
                w = f"w_c{L}"
                block_by_token(f"hf{L}", w, 0, tok(XT), [0, 1], after_norm(k), True)
                block_of(f"hq{L}", w, 1, tok(XT), [2, 3])
                for n, s in ((f"hf{L}", 0), (f"hq{L}", 1)):
                    for tt in range(TT):
                        read_out(f"{n}.{tt}")
                        turn(f"{n}T.{tt}", 6 + tt,
                             [slot(s, 1024)[:, tt * BLK + f * P:tt * BLK + (f + 1) * P] for f in range(4)])

                def level(l):
                    if l == 0:
                        read_out(f"hq{L}T.1")
                    else:
                        pe.wait_ge(ev("xlev"), 8 * i + l)
                    q, kk = slot(8, 1024), slot(1, 1024)
                    X = slot(9, 1024)
                    name = f"lev{L}.{l}"
                    if l == 0:
                        for tt in range(TT):
                            out = fill(f"{name}.{tt}", 4 + tt)
                            for h in range(4):
                                c = h * T + tt * P
                                m = pe.matmul(out[:, h * P:(h + 1) * P], kk[:, c:c + P], q[:, c:c + P],
                                              start=True, stop=True)
                            close(f"{name}.{tt}", m)
                        return
                    out = fill(name, 4 + l % 2)
                    if l == LEVELS:
                        for h in range(4):
                            m = pe.matmul(out[:, h * P:(h + 1) * P], X[:, h * T:h * T + P],
                                          X[:, h * T + P:(h + 1) * T], start=True, stop=True)
                        close(name, m)
                        return
                    s = 1 << (l - 1)
                    for tt in range(TT):
                        for h in range(4):
                            c = h * T + tt * P
                            q2 = X[:, c:c + P].rearrange("p (n two m) -> p n two m", two=2, m=s)[:, :, 1, :]
                            m = pe.matmul(out[:, (tt * 4 + h) * 64:(tt * 4 + h + 1) * 64], X[:, c:c + P], q2,
                                          start=True, stop=True)
                    close(name, m)

                def cmp_turned():
                    for tt in range(TT):
                        read_out(f"A{L}.{tt}")
                    turn(f"cT{L}", 6, [slot(2, 1024)[:, tt * BLK + kv * P:tt * BLK + (kv + 1) * P]
                                       for kv in range(2) for tt in range(TT)])

                def hgrn_out():
                    for tt in range(TT):
                        read_out(f"hi{L}.{tt}")
                    read_out(f"lev{L}.{LEVELS}")
                    AT = slot(10, 1024).rearrange("p (t h q) -> p t h q", t=2, h=4)
                    AX_, vr = slot(11, 512), slot(5, 1024)
                    for tt in range(TT):
                        out = fill(f"ho{L}.{tt}", tt)
                        for h in range(4):
                            o = out[:, h * P:(h + 1) * P]
                            if tt == 1:
                                pe.matmul(o, AX_[:, h * P:(h + 1) * P], vr[:, h * P:(h + 1) * P], start=True, stop=False)
                            m = pe.matmul(o, AT[:, tt, h, :], vr[:, tt * BLK + h * P:tt * BLK + (h + 1) * P],
                                          start=(tt == 0), stop=True)
                        close(f"ho{L}.{tt}", m)

                def ch_turned():
                    read_out(f"ch{L}.0")
                    read_out(f"ch{L}.1")
                    turn(f"chT{L}", 6, [chid[0:2 * NCMP, j * P:(j + 1) * P] for j in range(4)])

                def cmp_keys():
                    read_out(f"chT{L}")
                    chT = sm("chT", 4 * 2 * NCMP).rearrange("p (j n) -> p j n", j=4)
                    out = fill(f"kc{L}", 4)
                    for m_ in range(2):
                        mm = pe.matmul(out[0:2 * NCMP, 0:64], chT[:, m_, :], w2c[:, i, 0, m_, :], start=(m_ == 0),
                                       stop=(m_ == 1))
                    close(f"kc{L}", mm)

                def cmp_values():
                    pe.wait_ge(ev("chrep"), i + 1)
                    rep_ = chrep.rearrange("p (m n) -> p m n", m=2)
                    out = fill(f"vc{L}", 5)
                    for m_ in range(2):
                        mm = pe.matmul(out[0:8 * NCMP, 0:64], rep_[:, m_, :], w2c[:, i, 1, m_, :],
                                       start=(m_ == 0), stop=(m_ == 1))
                    close(f"vc{L}", mm)

                block_of(f"A{L}", w, 2, tok(XT), [0, 1], {1: lambda: level(0), 3: lambda: level(1)})
                linear([f"B{L}.0", f"B{L}.1"], [2, 3], [a[f"w_d{L}"][u] for u in range(4)], 2, tok(XT),
                       behind={1: lambda: level(2), 3: cmp_turned})
                block_of(f"nq{L}", w, 3, tok(XT), [0, 1], {0: lambda: level(3), 2: lambda: level(4)})
                block_of(f"hi{L}", w, 4, tok(XT), [2, 3], {0: lambda: level(5), 2: lambda: level(6)})
                pe.wait_ge(ev("xclo"), i + 1)
                flat = tuple(h[:, :, :, :].rearrange("p a b c -> p (a b c)") for h in HT)
                for kv in range(2):
                    def windows(k_, tt):
                        at = kv * 1024 + k_ * 32
                        return flat[0][:, at:at + P], flat[1][:, at:at + P]
                    linear([f"ch{L}.{kv}"], [kv], [a[f"w_w{L}"][4 * kv + u] for u in range(4)], 4, windows,
                           behind={1: lambda: level(7 + kv)})
                block_of(f"hg{L}", w, 5, tok(XT), [2, 3], {0: ch_turned, 1: cmp_keys, 2: cmp_values, 3: hgrn_out})
                pe.wait_ge(ev("ropeD"), i + 1)
                pe.wait_ge(ev("ropeP"), i + 1)
                Z = Z_turned.rearrange("p (t g d) -> p t g d", t=2, g=12)
                for tt in range(TT):
                    for g in range(3):
                        turn(f"zT{L}.{tt}.{g}", 6 + (tt * 3 + g) % 2, [Z[:, tt, 4 * g + j, :] for j in range(4)])
                pe.wait_ge(ev("kcr"), i + 1)
                turn(f"kcT{L}", 6, [sm("kcr", 64)[0:2 * NCMP, :]])
                for tt in range(TT):
                    for g in range(3):
                        read_out(f"zT{L}.{tt}.{g}")
                read_out(f"kcT{L}")
                qT = scr[:, 7 * SLOT:7 * SLOT + 2048]
                kT = slot(11, 1024)
                kcT = sm("kcT", 2 * NCMP)

                def cmp_scores():
                    for tt in range(TT):
                        out = fill(f"cs{L}.{tt}", 2 + tt)
                        for h in range(8):
                            g = h // 4
                            m = pe.matmul(out[:, h * NCMP:(h + 1) * NCMP], qT[0:64, h * T + tt * P:h * T + (tt + 1) * P],
                                          kcT[0:64, g * NCMP:(g + 1) * NCMP], start=True, stop=True)
                        close(f"cs{L}.{tt}", m)

                def cmp_probs():
                    for tt in range(TT):
                        pe.wait_ge(ev("cprobs"), 2 * i + tt + 1)
                        turn(f"cpT{L}.{tt}", 6 + tt, [sm(f"cp{tt}", 8 * NCMP)])

                def cmp_out():
                    read_out(f"vc{L}")
                    for tt in range(TT):
                        read_out(f"cpT{L}.{tt}")
                        out = fill(f"co{L}.{tt}", tt)
                        close(f"co{L}.{tt}", pe.matmul(out[:, :], cpT(tt)[0:8 * NCMP, :], cvals()[0:8 * NCMP, :],
                                                       start=True, stop=True))

                attend([f"sl{L}", f"sw{L}"], {
                    f"sl{L}": (64, 64, lambda h: qT[:, h * T:(h + 1) * T],
                               lambda h: kT[:, (h // 4) * T:(h // 4 + 1) * T],
                               lambda h, t: slot(2, 1024)[:, t * BLK + 384 + (h // 4) * 64:t * BLK + 448 + (h // 4) * 64],
                               [2, 3]),
                    f"sw{L}": (64, 64, lambda h: qT[:, h * T:(h + 1) * T],
                               lambda h: kT[:, (2 + h // 4) * T:(3 + h // 4) * T],
                               lambda h, t: slot(3, 1024)[:, t * BLK + 128 + (h // 4) * 64:t * BLK + 192 + (h // 4) * 64],
                               [0, 1])},
                    {0: cmp_scores, 2: cmp_probs, 3: cmp_out,
                     11: lambda: [(pe.wait_ge(ev("hrow"), 2 * i + tt + 1), out_rows(f"hr{L}", tt, 0)) for tt in range(TT)]})
                out_proj(L, f"w_o{L}", k + 1, lambda: [read_out(f"hr{L}.{tt}") for tt in range(TT)],
                         lambda tt: (pe.wait_ge(ev("nrow"), 2 * i + tt + 1), out_rows(f"nr{L}", tt, 512)), f"nr{L}")
                mlp(L, f"w_m{L}", f"w_n{L}", FFN_BLOCKS, 2, False, k + 1)

        @block.sync
        def _(sp):
            sp.dma_start(x[:, 0, :], a["x"][0:P, :]).then_inc(ev("xin0"), 16)
            sp.dma_start(ident, a["const"][:, 0:P]).then_inc(ev("ident"), 16)
            for g, src in enumerate(units):
                if g == 1:
                    sp.dma_start(x[:, 1, :], a["x"][P:T, :]).then_inc(ev("xin1"), 16)
                if g >= NRAW:
                    sp.wait_ge(*lo_done[g - NRAW])
                sp.dma_start(raw[:, g % NRAW, 0:src.shape[1]], src).then_inc(landed[g % NRAW], 16)
            for tt in range(TT):
                for nb in range(2):
                    f = fills[f"y3.{nb}.{tt}"]
                    sp.wait_ge(bank_free[f.bank], f.turn)
                sp.dma_start(a["out"][tt * P:(tt + 1) * P, :], x[:, tt, :]).then_inc(ev("stored"), 16)
            sp.wait_ge(ev("stored"), 32)

        @block.scalar
        def _(act):
            st = {"g": 0, "hi": 0}
            def splits(n):
                while st["g"] < min(n, len(units)):
                    g = st["g"]
                    w = units[g].shape[1]
                    act.wait_ge(landed[g % NRAW], 16 * (g // NRAW + 1))
                    if g >= NSPLIT:
                        act.wait_ge(unit_used, g - NSPLIT + 1)
                    act.activation(whi[:, g % NSPLIT, 0:w], raw[:, g % NRAW, 0:w], ACT.Copy).then_inc(split_hi, 1)
                    st["g"] += 1

            def full(name):
                f = fills[name]
                splits(f.pos + AHEAD)
                act.wait_ge(bank_full[f.bank], f.turn)
                return PS[f.bank]

            def free(name, ins):
                ins.then_inc(bank_free[fills[name].bank], 1)

            def copy_out(name, dst, src=None):
                ps = full(name)
                free(name, act.activation(dst, ps[:, :] if src is None else src(ps), ACT.Copy))

            def hi(name, dst, n=4, w=P):
                ps = full(name)
                src = ps[:, 0:n * w].rearrange("p (k t) -> p k t", k=n)
                act.activation(dst, src, ACT.Copy).then_inc(turn_hi, 1)

            def norm_hi(k, tt, pair):
                for h in range(2):
                    hi(f"n{k}.{tt}.{h}", pair[0][:, 4 * h:4 * h + 4, tt * P:(tt + 1) * P])

            def squares(tt, h, src):
                act.activation(xn[:, tt, h * BLK:(h + 1) * BLK], src[:, h * BLK:(h + 1) * BLK], ACT.Square,
                               accum_out=sm("ssq", 4)[:, 2 * tt + h:2 * tt + h + 1]).then_inc(ev("ssq"), 1)

            def soft(tags, between):
                steps = steps_of(tags)
                base = cnt["s"]

                def exps(n):
                    tag, i, tt, h0, nh, klen, which = steps[n]
                    H, causal, scaled = ATTENTION[tag]
                    splits(fills[f"{tag}.s{i}"].pos + AHEAD)
                    act.wait_ge(ev("maxed"), base + n + 1)
                    for j in range(nh):
                        c = tt * H + h0 + j
                        src = (masked(tag, n) if causal else PS[fills[f"{tag}.s{i}"].bank])[:, j * klen:(j + 1) * klen]
                        kw = {"scale": sm("cq", 16)[:, c:c + 1]} if scaled else {}
                        m = act.activation(probs(tag, n)[:, j * klen:(j + 1) * klen], src, ACT.Exp,
                                           bias=sm(f"nmax{which}", 16)[:, c:c + 1],
                                           accum_out=sm(f"rsum{which}", 16)[:, c:c + 1], **kw)
                    if causal:
                        m.then_inc(ev("probs"), 1)
                    else:
                        free(f"{tag}.s{i}", m)

                exps(0)
                for n in range(len(steps)):
                    if n in between:
                        between[n]()
                    if n + 1 < len(steps):
                        exps(n + 1)
                    tag, i = steps[n][0:2]
                    copy_out(f"{tag}.t{i}", turned(tag, n))
                cnt["s"] += len(steps)

            cnt = {"s": 0, "hid": 0, "hid_sq": 0}

            def mem_turned(i, which):
                for tt in range(TT):
                    copy_out(f"{('xqT', 'mkT')[which]}{i}.{tt}",
                             memT(i, which).rearrange("p (h t) -> p h t", h=4)[:, :, tt * P:(tt + 1) * P],
                             lambda ps: ps[:, :].rearrange("p (h t) -> p h t", h=4))

            def mlp_side(L, blocks, kts, squared):
                for tt in range(TT):
                    ps = full(f"h{L}.0.{tt}")
                    if squared:
                        free(f"h{L}.0.{tt}", act.activation(hrow[:, tt, :], ps[:, :], ACT.Relu))
                    else:
                        act.activation(hrow[:, tt, 256:512], ps[:, 0:256], ACT.Tanh, scale=0.5).then_inc(ev("tanh"), 1)
                for tt in range(TT):
                    hi(f"ht{L}.0.{tt}", HT[0][:, 0, 0:kts, tt * P:(tt + 1) * P], kts)
                flat = hrow[:, :, :].rearrange("p a b -> p (a b)")
                for j in range(1, blocks):
                    for f in range(4 if squared else 2):
                        ps = full(f"h{L}.{j}.{f}")
                        if f == 0 and j > 1:
                            act.wait_ge(ev("hid"), cnt["hid"] + j - 1)
                        dst = flat[:, f * T:(f + 1) * T]
                        if squared:
                            free(f"h{L}.{j}.{f}", act.activation(dst, ps[:, 0:T], ACT.Relu))
                        else:
                            act.activation(dst, ps[:, 0:T], ACT.Tanh, scale=0.5).then_inc(ev("tanh"), 1)
                    splits(fills[f"h{L}.{j}.3"].pos + AHEAD)
                    if squared:
                        act.wait_ge(ev("squared"), cnt["hid_sq"] + j)
                    else:
                        for f in (2, 3):
                            act.wait_ge(bank_free[fills[f"h{L}.{j}.{f}"].bank], fills[f"h{L}.{j}.{f}"].turn)
                    at = 0 if squared else 2 * T
                    act.activation(HT[0][:, j % 2, 0:kts, :].rearrange("p f t -> p (f t)"),
                                   flat[:, at:at + kts * T], ACT.Copy).then_inc(turn_hi, 1)
                cnt["hid"] += blocks - 1
                cnt["hid_sq"] += blocks - 1 if squared else 0

            for tt in range(TT):
                act.wait_ge(ev(f"xin{tt}"), 16)
                for h in range(2):
                    squares(tt, h, x[:, tt, :])
                norm_hi(0, tt, XT)
            act.dma_start(colg[:, :], a["colg"]).then_inc(ev("params"), 16)
            act.dma_start(slot(8, 1024), a["wgate"]).then_inc(ev("params"), 16)
            act.dma_start(rowg[:, :], a["rowg"].partition_broadcast(P)).then_inc(ev("params"), 16)
            for tt in range(TT):
                copy_out(f"u.{tt}", slot(2, 1024)[:, tt * BLK:(tt + 1) * BLK])
            for tt in range(TT):
                act.wait_ge(ev("memin"), 32)
                act.wait_ge(bank_full[fills["n0.1.1"].bank], fills["n0.1.1"].turn)
                for h in range(2):
                    squares(tt, h, slot(tt, 1024))
            act.dma_start(const[:, P:], a["const"][:, P:]).then_inc(ev("tables"), 16)
            act.dma_start(w2c[:, :, :, :, :].rearrange("p a b c d -> p (a b c d)"), a["w2c"]).then_inc(ev("tables"), 16)
            for tt in range(TT):
                copy_out(f"uT.{tt}", slot(7, 1024).rearrange("p (f t) -> p f t", f=4)[:, :, tt * P:(tt + 1) * P],
                         lambda ps: ps[:, :].rearrange("p (f t) -> p f t", f=4))
            for tt in range(TT):
                norm_hi(1, tt, MX)
            act.wait_ge(ev("lamz"), 1)
            act.activation(sm("z4", 4), sm("z4", 4), ACT.Exp, scale=-1.0).then_inc(ev("lamexp"), 1)
            for tt in range(TT):
                copy_out(f"xq0.{tt}", slot(3, 1024)[:, tt * BLK:(tt + 1) * BLK])
            for tt in range(TT):
                copy_out(f"mk0.{tt}", slot(5, 1024)[:, tt * BLK:(tt + 1) * BLK])
            act.wait_ge(ev("lru_c"), 1)
            for g, dst in ((0, 1), (1, 2)):
                for half in range(2):
                    ps = full(f"rg{g}.{half}")
                    for j in range(2):
                        f = 2 * half + j
                        m = act.activation(slot(dst, 1024)[:, f * T:(f + 1) * T], ps[:, j * T:(j + 1) * T], ACT.Tanh,
                                           bias=sm("hb", 8)[:, 4 * g + f:4 * g + f + 1], scale=0.5)
                    free(f"rg{g}.{half}", m)
            splits(fills["gate.0"].pos)
            act.wait_ge(ev("rgate"), 1)
            for f in range(4):
                at = slice(f * T, (f + 1) * T)
                act.activation(slot(11, 1024)[:, at], slot(1, 1024)[:, at], ACT.Tanh, scale=sm("lh", 4)[:, f:f + 1])
            act.wait_ge(ev("gated_in"), 1)
            for f in range(4):
                at = slice(f * T, (f + 1) * T)
                m = act.activation(slot(2, 1024)[:, at], slot(1, 1024)[:, at], ACT.Exp, scale=sm("lc", 4)[:, f:f + 1])
            m.then_inc(ev("decay"), 1)
            for tt in range(TT):
                copy_out(f"gate.{tt}", slot(4, 1024)[:, tt * BLK:(tt + 1) * BLK])
            act.wait_ge(ev("b2"), 1)
            act.activation(slot(8, 1024), slot(8, 1024), ACT.Sqrt, scale=-1.0).then_inc(ev("bsq"), 1)
            for tt in range(TT):
                copy_out(f"gateT.{tt}", slot(10, 1024).rearrange("p (f t) -> p f t", f=4)[:, :, tt * P:(tt + 1) * P],
                         lambda ps: ps[:, :].rearrange("p (f t) -> p f t", f=4))
            for tt in range(TT):
                copy_out(f"mv0.{tt}", slot(6, 1024)[:, tt * BLK:(tt + 1) * BLK])
            act.wait_ge(ev("gcub"), 1)
            act.activation(slot(8, 1024), slot(8, 1024), ACT.Tanh).then_inc(ev("gtanh"), 1)
            mem_turned(0, 0)
            mem_turned(0, 1)
            act.wait_ge(ev("yrow"), 1)
            act.activation(MX[0][:, 0:4, :].rearrange("p f t -> p (f t)"), slot(7, 1024), ACT.Copy).then_inc(ev("yhi"), 1)
            soft(["ma0"], {})
            for tt in range(TT):
                hi(f"mo0.{tt}", MX[0][:, 4:8, tt * P:(tt + 1) * P])

            def norm_x(rows, lastturn, k):
                for tt in range(TT):
                    for nb in range(2):
                        f = fills[f"{rows}.{nb}.{tt}"]
                        splits(fills[f"{rows}.1.1"].pos + AHEAD if tt else f.pos + AHEAD)
                        act.wait_ge(bank_free[f.bank], f.turn)
                        if tt == 0 and nb == 0:
                            f = fills[lastturn]
                            act.wait_ge(bank_full[f.bank], f.turn)
                        squares(tt, nb, x[:, tt, :])
                    norm_hi(k, tt, XT)

            norm_x("out0", "mo0.1", 2)
            mlp_side(0, MLP_BLOCKS, 4, True)
            norm_x("y0", "n2.1.1", 3)
            for tt in range(TT):
                act.wait_ge(ev("memin"), 64)
                act.wait_ge(bank_full[fills["n3.1.1"].bank], fills["n3.1.1"].turn)
                for h in range(2):
                    squares(tt, h, slot(8 + tt, 1024))
            for tt in range(TT):
                copy_out(f"q.{tt}", slot(0, 1024)[:, tt * BLK:(tt + 1) * BLK])
            for tt in range(TT):
                norm_hi(4, tt, MX)
            splits(fills["f.1"].pos + AHEAD)
            act.wait_ge(ev("absf"), 1)
            act.activation(sm("lz", 16), sm("lz", 16), ACT.Exp, scale=-1.0).then_inc(ev("expf"), 1)
            for n, s in (("k", 1), ("mk1", 5), ("v", 2), ("xq1", 3)):
                for tt in range(TT):
                    copy_out(f"{n}.{tt}", slot(s, 1024)[:, tt * BLK:(tt + 1) * BLK])
            for n, s in (("fq", 8), ("fk", 10)):
                dst = scr[:, s * SLOT:s * SLOT + 2048].rearrange("p (h t) -> p h t", h=8)
                for tt in range(TT):
                    for half in range(2):
                        copy_out(f"{n}T.{tt}.{half}", dst[0:65, 4 * half:4 * half + 4, tt * P:(tt + 1) * P],
                                 lambda ps: ps[0:65, :].rearrange("p (h t) -> p h t", h=4))
            def mem_rows_in():
                for tt in range(TT):
                    copy_out(f"mv1.{tt}", slot(6, 1024)[:, tt * BLK:(tt + 1) * BLK])
                mem_turned(1, 1)

            soft(["fa", "ma1"], {2: lambda: mem_turned(1, 0), 5: mem_rows_in,
                                 9: lambda: [hi(f"fo.{tt}", MX[0][:, 0:4, tt * P:(tt + 1) * P]) for tt in range(TT)]})
            for tt in range(TT):
                hi(f"mo1.{tt}", MX[0][:, 4:8, tt * P:(tt + 1) * P])
            norm_x("out1", "mo1.1", 5)
            mlp_side(1, MLP_BLOCKS, 4, True)
            for L in (2, 3):
                i = L - 2
                k = 6 + 2 * i
                norm_x(f"y{L - 1}", f"n{k - 1}.1.1", k)
                if L == 3:
                    act.wait_ge(ev("lbd"), 1)
                    act.activation(sm("A4", 4), sm("A4", 4), ACT.Tanh, scale=0.5).then_inc(ev("lbt"), 1)
                for n, s in ((f"hf{L}", 0), (f"hq{L}", 1)):
                    for tt in range(TT):
                        copy_out(f"{n}.{tt}", slot(s, 1024)[:, tt * BLK:(tt + 1) * BLK])
                for tt in range(TT):
                    ps = full(f"hf{L}T.{tt}")
                    free(f"hf{L}T.{tt}", act.activation(
                        slot(7, 1024).rearrange("p (f t) -> p f t", f=4)[:, :, tt * P:(tt + 1) * P],
                        ps[:, :].rearrange("p (f t) -> p f t", f=4), ACT.Tanh, scale=0.5))
                for tt in range(TT):
                    ps = full(f"hq{L}T.{tt}")
                    act.activation(slot(8, 1024).rearrange("p (f t) -> p f t", f=4)[:, :, tt * P:(tt + 1) * P],
                                   ps[:, :].rearrange("p (f t) -> p f t", f=4), ACT.Tanh, scale=0.5).then_inc(ev("hqt"), 1)
                def rows_in(n, s, w=BLK):
                    for tt in range(TT):
                        copy_out(f"{n}{L}.{tt}", slot(s, 1024)[:, tt * BLK:tt * BLK + w], lambda ps: ps[:, 0:w])

                rows_in("A", 2)
                rows_in("B", 3, 280)
                f = fills[f"B{L}.1"]
                act.wait_ge(bank_free[f.bank], f.turn)
                act.activation(sm("ng", 48).rearrange("p (t c) -> p t c", t=2),
                               slot(3, 1024).rearrange("p (t c) -> p t c", t=2)[:, :, 256:280], ACT.Tanh,
                               scale=0.5).then_inc(ev("ngt"), 1)
                ps = full(f"cT{L}")
                src = ps[:, :].rearrange("p (a b two) -> p a b two", a=4, two=2)
                kk = pairs_.rearrange("p (kv g t) -> p kv g t", kv=2, g=2)
                for par in range(2):
                    for g in range(2):
                        dst = kk[par * 64:(par + 1) * 64, :, g, :].rearrange("p kv (t c) -> p kv t c", t=2)
                        m = act.activation(dst, src[g * 64:(g + 1) * 64, :, :, par].rearrange(
                            "p (kv t) c -> p kv t c", kv=2), ACT.Copy)
                free(f"cT{L}", m)
                rows_in("nq", 4)
                act.wait_ge(ev("xc"), i + 1)
                flat = HT[0][:, :, :, :].rearrange("p a b c -> p (a b c)").rearrange("p (kv c) -> p kv c", kv=2)
                act.activation(flat[:, :, 0:608], windows_.rearrange("p (kv c) -> p kv c", kv=2),
                               ACT.Copy).then_inc(ev("xchi"), 1)
                rows_in("hi", 5)
                for kv in range(2):
                    ps = full(f"ch{L}.{kv}")
                    act.activation(chid[0:2 * NCMP, kv * 256:(kv + 1) * 256], ps[0:2 * NCMP, 0:256], ACT.Tanh,
                                   scale=0.5).then_inc(ev("cht"), 1)
                copy_out(f"chT{L}", sm("chT", 4 * 2 * NCMP).rearrange("p (j n) -> p j n", j=4),
                         lambda ps: ps[:, :].rearrange("p (j n) -> p j n", j=4)[:, :, 0:2 * NCMP])
                copy_out(f"kc{L}", sm("kc", 64)[0:2 * NCMP, :], lambda ps: ps[0:2 * NCMP, 0:64])
                for tt in range(TT):
                    ps = full(f"hg{L}.{tt}")
                    act.activation(slot(6, 1024)[:, tt * BLK:(tt + 1) * BLK], ps[:, :], ACT.Tanh,
                                   scale=0.5).then_inc(ev("hgt"), 1)
                qT = scr[:, 7 * SLOT:7 * SLOT + 2048].rearrange("p (h t) -> p h t", h=8)
                kT = slot(11, 1024).rearrange("p (h t) -> p h t", h=4)
                for tt in range(TT):
                    for g in range(3):
                        dst = qT[0:64, 4 * g:4 * g + 4] if g < 2 else kT[0:64]
                        copy_out(f"zT{L}.{tt}.{g}", dst[:, :, tt * P:(tt + 1) * P],
                                 lambda ps: ps[0:64, :].rearrange("p (h t) -> p h t", h=4))
                copy_out(f"kcT{L}", sm("kcT", 2 * NCMP)[0:64, :], lambda ps: ps[0:64, 0:2 * NCMP])

                def cmp_exps():
                    for tt in range(TT):
                        act.wait_ge(ev("cd"), 2 * i + tt + 1)
                        act.activation(sm(f"cp{tt}", 8 * NCMP), sm(f"cp{tt}", 8 * NCMP), ACT.Exp).then_inc(ev("cexp"), 1)

                soft([f"sl{L}", f"sw{L}"],
                     {0: cmp_exps,
                      2: lambda: [copy_out(f"cpT{L}.{tt}", cpT(tt)[0:8 * NCMP, :], lambda ps: ps[0:8 * NCMP, 0:P])
                                  for tt in range(TT)],
                      11: lambda: [hi(f"hr{L}.{tt}", MX[0][:, 0:4, tt * P:(tt + 1) * P]) for tt in range(TT)]})
                for tt in range(TT):
                    hi(f"nr{L}.{tt}", MX[0][:, 4:8, tt * P:(tt + 1) * P])
                norm_x(f"out{L}", f"nr{L}.1", k + 1)
                mlp_side(L, FFN_BLOCKS, 2, False)
            splits(len(units))

        @block.gpsimd
        def _(pool):
            pool.memset(powc[:, :], -0.5).then_inc(ev("powc"), 1)

            def load_gain(k):
                if k >= 2:
                    pool.wait_ge(ev("xn"), 4 * (k - 1))
                pool.dma_start(gain[:, k % 2, :], a["gains"][k, :].partition_broadcast(P)).then_inc(ev(f"gain{k % 2}"), 16)

            def rstd(src, n, width, event=None):
                chain(pool, "p_chain", pool.tensor_scalar(src, src, 1.0 / width, EPS, ALU.mult, ALU.add))
                m = pool.tensor_tensor(src, src, powc[0:src.shape[0], 0:n], ALU.pow)
                if event:
                    m.then_inc(ev(event), 1)
                else:
                    chain(pool, "p_chain", m)

            def norm(k):
                for tt in range(TT):
                    s0, s1 = sm("ssq", 4)[:, 2 * tt:2 * tt + 1], sm("ssq", 4)[:, 2 * tt + 1:2 * tt + 2]
                    pool.wait_ge(ev("ssq"), 4 * k + 2 * tt + 1)
                    chain(pool, "p_chain", pool.tensor_scalar(s0, s0, 1.0 / D, EPS, ALU.mult, ALU.add))
                    pool.wait_ge(ev("ssq"), 4 * k + 2 * tt + 2)
                    chain(pool, "p_chain", pool.tensor_scalar(s1, s1, 1.0 / D, s0, ALU.mult, ALU.add))
                    pool.tensor_tensor(s1, s1, powc[:, 0:1], ALU.pow).then_inc(ev("rstd"), 1)
                    if tt == 0 and k in NORMS_OF_X[1:]:
                        g = pool_units[NORMS_OF_X.index(k) - 1]
                        w = units[g].shape[1]
                        pool.wait_ge(split_hi, g + 1)
                        pool.tensor_tensor(wlo[:, g % NSPLIT, 0:w], raw[:, g % NRAW, 0:w],
                                           whi[:, g % NSPLIT, 0:w].bitcast(F32), ALU.subtract).then_inc(pool_lo, 1)
                    if k == 0 and tt == 0:
                        load_memory(0)
                        load_gain(1)
                if k + 2 < 10:
                    load_gain(k + 2)

            def squares(src, groups, hd, wait):
                wait()
                pool.tensor_tensor(hrow[:, :, :].rearrange("p a b -> p (a b)")[:, 0:2 * groups * hd], src, src,
                                   ALU.mult).then_inc(ev("sq"), 1)

            def stat(name, n, hd, k):
                pool.wait_ge(ev("hsum"), k + 1)
                rstd(sm(name, n), n, hd, "hrstd")

            def taken(name):
                pool.wait_ge(bank_free[fills[name].bank], fills[name].turn)

            def load_memory(s):
                for tt in range(TT):
                    pool.dma_start(slot(s + tt, 1024), a["mem"][tt * P:(tt + 1) * P, :]).then_inc(ev("memin"), 16)

            load_gain(0)
            pool.wait_ge(ev("powc"), 1)
            norm(0)
            norm(1)
            pool.wait_ge(ev("params"), 16 * 3)

            def headnorm(src, n, hd, name, k, waits):
                squares(src, n // 2, hd, waits)
                stat(name, n, hd, k)

            def scale_rows(dst, src, r, g):
                n, d = src.shape[1], src.shape[2]
                chain(pool, "p_chain", pool.tensor_tensor(dst, src, bc(r, 2, d), ALU.mult))
                return pool.tensor_tensor(dst, dst, bc(g, 1, n), ALU.mult)

            def mem_norms(i, kk):
                c = MEM[i]
                headnorm(slot(c["xq"], 1024), 8, P, "cqm", kk, lambda: (taken(f"xq{i}.0"), taken(f"xq{i}.1")))
                headnorm(slot(c["mk"], 1024), 8, P, "rk8", kk + 1,
                         lambda: (taken(f"mk{i}.0"), taken(f"mk{i}.1"), pool.wait_ge(ev("hrstd"), kk + 1)))
                pool.wait_ge(ev("hrstd"), kk + 2)
                g = sm("gqk", P)
                chain(pool, "p_chain", pool.tensor_tensor(g, rg(f"xaq{i}"), rg(f"xak{i}"), ALU.mult))
                v = slot(c["mk"], 1024).rearrange("p (n d) -> p n d", d=P)
                scale_rows(v, v, sm("rk8", 8), g).then_inc(ev("mkn"), 1)

            mem_norms(0, 0)
            norm(2)
            load_memory(8)

            def square_hidden(L):
                for tt in range(TT):
                    taken(f"h{L}.0.{tt}")
                    pool.tensor_tensor(hrow[:, tt, :], hrow[:, tt, :], hrow[:, tt, :], ALU.mult).then_inc(ev("act"), 1)
                flat = hrow[:, :, :].rearrange("p a b -> p (a b)")
                for j in range(1, MLP_BLOCKS):
                    for f in range(4):
                        taken(f"h{L}.{j}.{f}")
                    pool.tensor_tensor(flat, flat, flat, ALU.mult).then_inc(ev("squared"), 1)

            square_hidden(0)
            norm(3)
            norm(4)
            pool.wait_ge(ev("tables"), 32)
            headnorm(slot(0, 1024), 16, 64, "rq16", 2, lambda: (taken("q.0"), taken("q.1")))
            headnorm(slot(1, 1024), 16, 64, "rk16", 3, lambda: (taken("k.0"), taken("k.1"), pool.wait_ge(ev("hrstd"), 3)))
            pool.wait_ge(ev("hrstd"), 4)
            g = sm("gqk", P)
            chain(pool, "p_chain", pool.tensor_tensor(g[:, 0:64], rg("foxq"), rg("foxk"), ALU.mult))
            ka = slot(7, 1040).rearrange("p (n d) -> p n d", d=65)
            qa = slot(4, 1040).rearrange("p (n d) -> p n d", d=65)
            q = slot(0, 1024).rearrange("p (n d) -> p n d", d=64)
            k = slot(1, 1024).rearrange("p (n d) -> p n d", d=64)
            pool.memset(qa[:, :, 64:65], 1.0)
            chain(pool, "p_chain", pool.tensor_scalar(sm("rq16", 16), sm("rq16", 16), 0.125, None, ALU.mult))
            pool.tensor_tensor(qa[:, :, 0:64], q, bc(sm("rq16", 16), 2, 64), ALU.mult).then_inc(ev("qaug"), 1)
            scale_rows(ka[:, :, 0:64], k, sm("rk16", 16), g[:, 0:64]).then_inc(ev("kaug"), 1)
            mem_norms(1, 4)
            norm(5)
            square_hidden(1)
            for L in (2, 3):
                i = L - 2
                norm(6 + 2 * i)
                F, S = slot(0, 1024), slot(7, 1024)
                pool.wait_ge(ev("hfk"), i + 1)
                pool.memset(S, 1.0).then_inc(ev("lev"), 1)
                f = fills[f"n{6 + 2 * i}.1.1"]
                pool.wait_ge(bank_full[f.bank], f.turn)
                chain(pool, "p_chain", pool.memset(windows_, 0.0))
                k0 = 6 + 5 * i

                def square_rows(src, dst):
                    pool.tensor_tensor(dst, src, src, ALU.mult).then_inc(ev("sq"), 1)

                def key_squares(s, lo, row):
                    taken(row)
                    square_rows(slot(s, 1024).rearrange("p (t c) -> p t c", t=2)[:, :, lo:lo + P],
                                hrow[:, 0, 0:256].rearrange("p (t c) -> p t c", t=2))

                def windows_in():
                    kk = pairs_.rearrange("p (kv g t) -> p kv g t", kv=2, g=2)
                    X = windows_.rearrange("p (kv c) -> p kv c", kv=2)
                    taken(f"cT{L}")
                    for kv in range(2):
                        for g_ in range(2):
                            dst = X[:, kv, 0:512].rearrange("p (j c) -> p j c", j=16)[:, :, g_ * NCMP:(g_ + 1) * NCMP]
                            lowj = kk[:, kv, g_, 0:8 * NCMP].rearrange("p (n j) -> p j n", j=8)
                            hij = kk[:, kv, g_, 8:8 + 8 * NCMP].rearrange("p (n j) -> p j n", j=8)
                            pe_ = cg(f"pe{L}", 16 * kv, 16)
                            pool.tensor_tensor(dst[:, 0:8], lowj, bc(pe_[:, 0:8], 2, NCMP), ALU.add)
                            m = pool.tensor_tensor(dst[:, 8:16], hij, bc(pe_[:, 8:16], 2, NCMP), ALU.add)
                    m.then_inc(ev("xc"), 1)

                for l in range(1, LEVELS):
                    m_ = 1 << (l - 1)
                    Fv = F.rearrange("p (n two m) -> p n two m", two=2, m=m_)
                    Sv = S.rearrange("p (n two m) -> p n two m", two=2, m=m_)
                    tot = Fv[:, :, 1, m_ - 1]
                    lastf = Fv[:, :, 0, m_ - 1]
                    pool.wait_ge(ev("xlev"), 8 * i + l)
                    chain(pool, "p_chain", pool.tensor_tensor(Sv[:, :, 0, :], Sv[:, :, 0, :], bc(tot, 2, m_), ALU.mult))
                    pool.tensor_tensor(Fv[:, :, 1, :], Fv[:, :, 1, :], bc(lastf, 2, m_), ALU.mult).then_inc(ev("lev"), 1)
                    if l == 3:
                        windows_in()
                    if l == 4:
                        key_squares(2, 256, f"A{L}.1")
                    if l == 5:
                        stat("rks", 4, 64, k0)
                        key_squares(3, 0, f"B{L}.1")
                    if l == 6:
                        stat("rkw", 4, 64, k0 + 1)
                        taken(f"nq{L}.1")
                        square_rows(slot(4, 1024), hrow[:, :, :].rearrange("p a b -> p (a b)"))
                    if l == 7:
                        stat("rq16", 16, 64, k0 + 2)
                pool.wait_ge(ev("hrstd"), k0 + 3)
                pool.wait_ge(ev("xlev"), 8 * i + LEVELS)
                Z = Z_rows.rearrange("p (t g d) -> p t g d", t=2, g=12)
                for tt in range(TT):
                    qv = slot(4, 1024)[:, tt * BLK:(tt + 1) * BLK].rearrange("p (g d) -> p g d", d=64)
                    pool.tensor_tensor(Z[:, tt, 0:8, :], qv, bc(rg(f"q{L}"), 1, 8), ALU.mult)
                    for n_, (s, lo, nm) in enumerate(((2, 256, "rks"), (3, 0, "rkw"))):
                        kv_ = slot(s, 1024)[:, tt * BLK + lo:tt * BLK + lo + P].rearrange("p (g d) -> p g d", d=64)
                        m = scale_rows(Z[:, tt, 8 + 2 * n_:10 + 2 * n_, :], kv_, sm(nm, 4)[:, 2 * tt:2 * tt + 2],
                                       rg(f"k{L}", 64 * (n_ + 1), 64))
                m.then_inc(ev("zrow"), 1)
                pool.wait_ge(ev("zrow"), i + 1)
                Zr = Z_turned.rearrange("p (t g d) -> p t g d", t=2, g=12)
                tmp = hrow[:, :, :].rearrange("p a b -> p (a b)")[:, 0:768].rearrange("p (t g d) -> p t g d", t=2, g=12)
                cosb = bc(cst("cos").rearrange("p (t d) -> p t d", t=2), 2, 12)
                sinb = bc(cst("sin").rearrange("p (t d) -> p t d", t=2), 2, 12)
                pool.tensor_tensor(Zr[:, :, :, 32:64], Z[:, :, :, 32:64], cosb, ALU.mult)
                chain(pool, "p_chain", pool.tensor_tensor(tmp, Z[:, :, :, 0:32], sinb, ALU.mult))
                pool.tensor_tensor(Zr[:, :, :, 32:64], Zr[:, :, :, 32:64], tmp, ALU.add).then_inc(ev("ropeP"), 1)
                taken(f"kc{L}")
                n30 = 2 * NCMP
                kc, kt_ = sm("kc", 64), sm("kct", 64)
                pool.tensor_tensor(kt_[0:n30, :], kc[0:n30, :], kc[0:n30, :], ALU.mult).then_inc(ev("sq"), 1)
                pool.wait_ge(ev("hsum"), k0 + 4)
                rstd(sm("rkc", 1)[0:n30, :], 1, 64, "hrstd")
                pool.wait_ge(ev("hrstd"), k0 + 4)
                chain(pool, "p_chain", pool.tensor_scalar(kc[0:n30, :], kc[0:n30, :], sm("rkc", 1)[0:n30, :], None, ALU.mult))
                chain(pool, "p_chain", pool.tensor_tensor(kc[0:n30, :], kc[0:n30, :], rg(f"k{L}", 0, 64)[0:n30, :], ALU.mult))
                c_, s_ = cst("ccos")[0:n30, :], cst("csin")[0:n30, :]
                kr = sm("kcr", 64)
                x1, x2 = kc[0:n30, 0:32], kc[0:n30, 32:64]
                pool.tensor_tensor(kr[0:n30, 0:32], x1, c_, ALU.mult)
                pool.tensor_tensor(kt_[0:n30, 0:32], x2, s_, ALU.mult)
                pool.tensor_tensor(kr[0:n30, 32:64], x2, c_, ALU.mult)
                chain(pool, "p_chain", pool.tensor_tensor(kt_[0:n30, 32:64], x1, s_, ALU.mult))
                pool.tensor_tensor(kr[0:n30, 0:32], kr[0:n30, 0:32], kt_[0:n30, 0:32], ALU.subtract)
                pool.tensor_tensor(kr[0:n30, 32:64], kr[0:n30, 32:64], kt_[0:n30, 32:64], ALU.add).then_inc(ev("kcr"), 1)
                pool.wait_ge(ev("ropeP"), i + 1)
                ho = slot(9, 1024)
                for tt in range(TT):
                    taken(f"ho{L}.{tt}")
                square_rows(ho, hrow[:, :, :].rearrange("p a b -> p (a b)"))
                pool.wait_ge(ev("hsum"), k0 + 5)
                rstd(sm("rho", 8), 8, P, "hrstd")
                pool.wait_ge(ev("hrstd"), k0 + 5)
                for tt in range(TT):
                    o = ho[:, tt * BLK:(tt + 1) * BLK].rearrange("p (n d) -> p n d", d=P)
                    scale_rows(o, o, sm("rho", 8)[:, 4 * tt:4 * tt + 4], rg(f"gn{L}")).then_inc(ev("hon"), 1)
                norm(7 + 2 * i)

        @block.vector
        def _(dve):
            st = {"g": 0, "hi": 0}

            def splits(n):
                while st["g"] < min(n, len(units)):
                    g = st["g"]
                    st["g"] += 1
                    if g in pool_units:
                        continue
                    w = units[g].shape[1]
                    dve.wait_ge(split_hi, g + 1)
                    dve.tensor_tensor(wlo[:, g % NSPLIT, 0:w], raw[:, g % NRAW, 0:w],
                                      whi[:, g % NSPLIT, 0:w].bitcast(F32), ALU.subtract).then_inc(split_lo, 1)

            def full(name, further=NSPLIT):
                f = fills[name]
                splits(min(f.pos + AHEAD, f.need + further))
                dve.wait_ge(bank_full[f.bank], f.turn)
                return PS[f.bank]

            def free(name, ins, wait=False):
                ins.then_inc(bank_free[fills[name].bank], 1)
                if wait:
                    dve.wait_ge(bank_free[fills[name].bank], fills[name].turn)

            def lo(name, pair, sl, n=4, further=NSPLIT):
                st["hi"] += 1
                ps = full(name, further)
                dve.wait_ge(turn_hi, st["hi"])
                src = ps[:, 0:n * P].rearrange("p (k t) -> p k t", k=n)
                free(name, dve.tensor_tensor(sl(pair[1]), src, sl(pair[0]).bitcast(F32), ALU.subtract))

            def norm_rows(k, tt, src):
                dve.wait_ge(ev("rstd"), 2 * k + tt + 1)
                dve.wait_ge(ev(f"gain{k % 2}"), 16 * (k // 2 + 1))
                for h in range(2):
                    at = slice(h * BLK, (h + 1) * BLK)
                    dve.scalar_tensor_tensor(xn[:, tt, at], src[:, at], sm("ssq", 4)[:, 2 * tt + 1:2 * tt + 2],
                                             gain[:, k % 2, at], ALU.mult, ALU.mult).then_inc(ev("xn"), 1)

            def norm_lo(k, tt, pair, further=NSPLIT):
                for h in range(2):
                    lo(f"n{k}.{tt}.{h}", pair, lambda t: t[:, 4 * h:4 * h + 4, tt * P:(tt + 1) * P], 4, further)

            def residual(rows, tt, further=NSPLIT):
                for nb in range(2):
                    name = f"{rows}.{nb}.{tt}"
                    ps = full(name, further)
                    free(name, dve.tensor_tensor(x[:, tt, nb * BLK:(nb + 1) * BLK], ps[:, :],
                                                 x[:, tt, nb * BLK:(nb + 1) * BLK], ALU.add))

            def norm_x(rows, k):
                residual(rows, 0, 1)
                norm_rows(k, 0, x[:, 0, :])
                norm_lo(k, 0, XT, 1)
                residual(rows, 1, 1)
                splits(fills[f"{rows}.1.1"].need + 3)
                norm_rows(k, 1, x[:, 1, :])
                norm_lo(k, 1, XT)

            def hsums(dst, src, after=None):
                if after:
                    splits(fills[after].pos + AHEAD)
                st["hs"] = st.get("hs", 0) + 1
                dve.wait_ge(ev("sq"), st["hs"])
                dve.tensor_reduce(dst, src, AX.X, ALU.add).then_inc(ev("hsum"), 1)

            def hq(n, hd):
                return hrow[:, :, :].rearrange("p a b -> p (a b)")[:, 0:n * hd].rearrange("p (n d) -> p n d", d=hd)

            def soft(tags, between):
                steps = steps_of(tags)
                base = cnt["p"]
                for n, (tag, i, tt, h0, nh, klen, which) in enumerate(steps):
                    H, causal, scaled = ATTENTION[tag]
                    ps = full(f"{tag}.s{i}")
                    c = tt * H + h0
                    mx = sm("mx", 16)[:, c:c + nh]
                    if causal:
                        if n >= 2:
                            dve.wait_ge(ev("probs"), base + probs_after(steps, n - 1))
                        for j in range(nh):
                            m = dve.tensor_tensor_reduce(masked(tag, n)[:, j * klen:(j + 1) * klen],
                                                         ps[:, j * klen:(j + 1) * klen],
                                                         cst("mask", 256 - klen if tt == 0 else 0, klen), 1.0, -3.0e38,
                                                         ALU.add, ALU.max, mx[:, j:j + 1])
                        free(f"{tag}.s{i}", m, True)
                    else:
                        chain(dve, "v_chain", dve.tensor_reduce(
                            mx, ps[:, 0:nh * klen].rearrange("p (h k) -> p h k", h=nh), AX.X, ALU.max))
                    nm = sm(f"nmax{which}", 16)[:, c:c + nh]
                    if scaled:
                        m = dve.scalar_tensor_tensor(nm, mx, -1.0, sm("cq", 16)[:, c:c + nh], ALU.mult, ALU.mult)
                    else:
                        m = dve.tensor_scalar(nm, mx, -1.0, None, ALU.mult)
                    m.then_inc(ev("maxed"), 1)
                    if n in between:
                        between[n]()
                cnt["p"] += probs_after(steps, len(steps))

            def weights_of(tags, tag, tt, base, gate=None):
                steps = steps_of(tags)
                last = max(n for n, s_ in enumerate(steps) if s_[0] == tag and s_[2] == tt)
                H, causal, _ = ATTENTION[tag]
                if causal:
                    dve.wait_ge(ev("probs"), base + probs_after(steps, last + 1))
                else:
                    f = fills[f"{tag}.s{steps[last][1]}"]
                    dve.wait_ge(bank_free[f.bank], f.turn)
                r = sm("rinv", 16)[:, tt * H:(tt + 1) * H]
                chain(dve, "v_chain", dve.reciprocal(r, sm(f"rsum{steps[last][6]}", 16)[:, tt * H:(tt + 1) * H]))
                if gate is not None:
                    chain(dve, "v_chain", dve.tensor_tensor(r, r, gate, ALU.mult))
                return r

            def step(ins):
                chain(dve, "v_chain", ins)

            cnt = {"p": 0}

            def rows_out(tags, tag, tt, base, dst):
                H = ATTENTION[tag][0]
                ps = full(f"{tag}.o{tt}")
                r = weights_of(tags, tag, tt, base)
                free(f"{tag}.o{tt}", dve.tensor_tensor(dst.rearrange("p (h d) -> p h d", h=H),
                                                       ps[:, :].rearrange("p (h d) -> p h d", h=H),
                                                       bc(r, 2, BLK // H), ALU.mult))

            def mem_scale(i):
                dve.wait_ge(ev("hrstd"), (1, 5)[i])
                chain(dve, "v_chain", dve.tensor_scalar(sm("cq", 16)[:, 0:8], sm("cqm", 8), P ** -0.5, None, ALU.mult))

            def mlp_side(L, blocks, kts, squared, acts):
                def silu(g2, dst, gate, up, gate_bank, up_bank):
                    acts["t"] += 1
                    dve.wait_ge(ev("tanh"), acts["t"])
                    m = dve.scalar_tensor_tensor(g2, g2, 1.0, gate, ALU.add, ALU.mult)
                    if gate_bank == up_bank:
                        step(m)
                    else:
                        free(gate_bank, m, True)
                    free(up_bank, dve.scalar_tensor_tensor(dst, g2, 0.5, up, ALU.mult, ALU.mult))

                if not squared:
                    for tt in range(TT):
                        name = f"h{L}.0.{tt}"
                        ps = full(name)
                        silu(hrow[:, tt, 256:512], hrow[:, tt, 0:256], ps[:, 0:256], ps[:, 256:512], name, name)
                for tt in range(TT):
                    lo(f"ht{L}.0.{tt}", HT, lambda t: t[:, 0, 0:kts, tt * P:(tt + 1) * P], kts)
                flat = hrow[:, :, :].rearrange("p a b -> p (a b)")
                for j in range(1, blocks):
                    if not squared:
                        if j > 1:
                            dve.wait_ge(ev("hid"), acts["hid"] + j - 1)
                        for f in range(2):
                            gate, up = full(f"h{L}.{j}.{f}"), full(f"h{L}.{j}.{2 + f}")
                            silu(flat[:, f * T:(f + 1) * T], flat[:, (2 + f) * T:(3 + f) * T], gate[:, 0:T], up[:, 0:T],
                                 f"h{L}.{j}.{f}", f"h{L}.{j}.{2 + f}")
                        for f in range(2):
                            dve.wait_ge(bank_free[fills[f"h{L}.{j}.{2 + f}"].bank], fills[f"h{L}.{j}.{2 + f}"].turn)
                    splits(fills[f"h{L}.{j}.3"].pos + AHEAD)
                    st["hi"] += 1
                    dve.wait_ge(turn_hi, st["hi"])
                    at = 0 if squared else 2 * T
                    dve.tensor_tensor(HT[1][:, j % 2, 0:kts, :].rearrange("p f t -> p (f t)"), flat[:, at:at + kts * T],
                                      HT[0][:, j % 2, 0:kts, :].rearrange("p f t -> p (f t)").bitcast(F32),
                                      ALU.subtract).then_inc(ev("hid"), 1)
                acts["hid"] += blocks - 1

            def log1p(dst, z, w, t):
                chain(dve, "v_chain", dve.tensor_scalar(t, z, 2.0, None, ALU.add))
                chain(dve, "v_chain", dve.reciprocal(t, t))
                chain(dve, "v_chain", dve.tensor_tensor(w, z, t, ALU.mult))
                chain(dve, "v_chain", dve.tensor_tensor(t, w, w, ALU.mult))
                chain(dve, "v_chain", dve.tensor_scalar(dst, t, 1.0 / 15, None, ALU.mult))
                for n in (13, 11, 9, 7, 5, 3):
                    chain(dve, "v_chain", dve.scalar_tensor_tensor(dst, dst, 1.0 / n, t, ALU.add, ALU.mult))
                chain(dve, "v_chain", dve.scalar_tensor_tensor(dst, dst, 1.0, w, ALU.add, ALU.mult))
                chain(dve, "v_chain", dve.tensor_scalar(dst, dst, 2.0, None, ALU.mult))

            for tt in range(TT):
                norm_rows(0, tt, x[:, tt, :])
                norm_lo(0, tt, XT)
            splits(fills["u.1"].pos + AHEAD)
            for tt in range(TT):
                norm_rows(1, tt, slot(tt, 1024))
            dve.wait_ge(ev("params"), 16 * 3)
            lam = cg("lam")
            z, w4, t4, l4 = sm("z4", 4), sm("w4", 4), sm("t4", 4), sm("l4", 4)
            step(dve.tensor_scalar(z, lam, -1.0, None, ALU.mult))
            dve.tensor_tensor(z, z, lam, ALU.max).then_inc(ev("lamz"), 1)
            for tt in range(TT):
                norm_lo(1, tt, MX)
            xq, conv_splits = fills["xq0.1"].pos, 0
            u_, uc = slot(7, 1024), slot(0, 1024)
            cw, cb = cg("cw"), cg("cb")
            for tt in range(TT):
                dve.wait_ge(bank_free[fills[f"uT.{tt}"].bank], fills[f"uT.{tt}"].turn)
            for f in range(4):
                step(dve.tensor_scalar(uc[:, f * T:(f + 1) * T], u_[:, f * T:(f + 1) * T],
                                       cw[:, 4 * f + 3:4 * f + 4], cb[:, f:f + 1], ALU.mult, ALU.add))
            for s in (1, 2, 3):
                for f in range(4):
                    m = dve.scalar_tensor_tensor(uc[:, f * T + s:(f + 1) * T], u_[:, f * T:(f + 1) * T - s],
                                                 cw[:, 4 * f + 3 - s:4 * f + 4 - s], uc[:, f * T + s:(f + 1) * T],
                                                 ALU.mult, ALU.add)
                    if s < 3 or f < 3:
                        step(m)
                    if f % 2 == 1:
                        conv_splits += 1
                        splits(min(xq - 1 + conv_splits, xq + AHEAD))
            m.then_inc(ev("conv"), 1)
            dve.wait_ge(ev("conv"), 1)
            splits(fills["mk0.0"].pos)
            dve.wait_ge(ev("lamexp"), 1)
            log1p(l4, z, w4, t4)
            step(dve.tensor_scalar(t4, lam, -1.0, 0.0, ALU.mult, ALU.max))
            step(dve.tensor_tensor(l4, l4, t4, ALU.add))
            step(dve.tensor_scalar(sm("lc", 4), l4, -8.0, None, ALU.mult))
            step(dve.tensor_scalar(sm("lh", 4), l4, -4.0, None, ALU.mult))
            dve.tensor_scalar(sm("hb", 8)[:, 0:8], cg("br", 0, 8), 0.5, None, ALU.mult).then_inc(ev("lru_c"), 1)
            splits(fills["mk0.0"].pos + AHEAD)
            hsums(sm("cqm", 8), hq(8, P), "xq0.1")
            hsums(sm("rk8", 8), hq(8, P), "mk0.1")
            r, ig, s8, om = slot(1, 1024), slot(2, 1024), slot(8, 1024), slot(7, 1024)
            for g in range(2):
                for half in range(2):
                    nm = fills[f"rg{g}.{half}"]
                    splits(nm.pos + AHEAD)
                    dve.wait_ge(bank_free[nm.bank], nm.turn)
            dve.tensor_scalar(r, r, 0.5, 0.5, ALU.mult, ALU.add).then_inc(ev("rgate"), 1)
            step(dve.tensor_scalar(ig, ig, 0.5, 0.5, ALU.mult, ALU.add))
            dve.tensor_tensor(uc, uc, ig, ALU.mult).then_inc(ev("gated_in"), 1)
            dve.wait_ge(ev("gated_in"), 1)
            gated = fills["gate.0"].pos
            splits(gated)
            dve.wait_ge(ev("decay"), 1)
            decay, th = ig, slot(11, 1024)
            step(dve.scalar_tensor_tensor(om, decay, 1.0, th, ALU.add, ALU.mult))
            dve.scalar_tensor_tensor(s8, decay, 1.0, om, ALU.add, ALU.mult).then_inc(ev("b2"), 1)
            splits(gated + AHEAD)
            dve.wait_ge(ev("bsq"), 1)
            step(dve.tensor_tensor(uc, uc, s8, ALU.mult))
            for tt in range(TT):
                splits(fills[f"gateT.{tt}"].pos + AHEAD)
                dve.wait_ge(bank_free[fills[f"gateT.{tt}"].bank], fills[f"gateT.{tt}"].turn)
            gt = slot(10, 1024)
            step(dve.tensor_tensor(s8, gt, gt, ALU.mult))
            step(dve.tensor_scalar(s8, s8, 0.044715 * 0.7978845608028654, 0.7978845608028654, ALU.mult, ALU.add))
            dve.tensor_tensor(s8, s8, gt, ALU.mult).then_inc(ev("gcub"), 1)
            splits(fills["mv0.0"].pos)
            for f in range(4):
                step(dve.tensor_tensor_scan(om[:, f * T:(f + 1) * T], decay[:, f * T:(f + 1) * T],
                                            uc[:, f * T:(f + 1) * T], 0.0, ALU.mult, ALU.add))
            splits(fills["mv0.1"].pos + AHEAD)
            dve.wait_ge(ev("gtanh"), 1)
            step(dve.scalar_tensor_tensor(gt, s8, 1.0, gt, ALU.add, ALU.mult))
            dve.scalar_tensor_tensor(om, om, 0.5, gt, ALU.mult, ALU.mult).then_inc(ev("yrow"), 1)
            mem_scale(0)
            dve.wait_ge(ev("yhi"), 1)
            dve.tensor_tensor(MX[1][:, 0:4, :].rearrange("p f t -> p (f t)"), om,
                              MX[0][:, 0:4, :].rearrange("p f t -> p (f t)").bitcast(F32), ALU.subtract).then_inc(ev("ylo"), 1)
            soft(["ma0"], {})
            for tt in range(TT):
                rows_out(["ma0"], "ma0", tt, 0, xn[:, tt, 512:1024])
            for tt in range(TT):
                lo(f"mo0.{tt}", MX, lambda t: t[:, 4:8, tt * P:(tt + 1) * P])
            norm_x("out0", 2)
            acts = {"t": 0, "hid": 0}
            mlp_side(0, MLP_BLOCKS, 4, True, acts)
            norm_x("y0", 3)
            for tt in range(TT):
                norm_rows(4, tt, slot(8 + tt, 1024))
            for tt in range(TT):
                norm_lo(4, tt, MX)
            dve.wait_ge(ev("tables"), 32)
            fz, lz, lf = sm("fz", 16), sm("lz", 16), sm("lf", 16)
            for tt in range(TT):
                ps = full(f"f.{tt}")
                free(f"f.{tt}", dve.tensor_tensor(fz[:, 8 * tt:8 * tt + 8], ps[:, 0:8], rg("bf"), ALU.add))
            dve.wait_ge(bank_free[fills["f.1"].bank], fills["f.1"].turn)
            step(dve.tensor_scalar(lz, fz, -1.0, None, ALU.mult))
            dve.tensor_tensor(lz, lz, fz, ALU.max).then_inc(ev("absf"), 1)
            dve.wait_ge(ev("expf"), 1)
            w16, t16 = sm("w16", 16), sm("t16", 16)
            log1p(lf, lz, w16, t16)
            step(dve.tensor_scalar(t16, fz, 0.0, None, ALU.min))
            dve.tensor_tensor(lf, t16, lf, ALU.subtract).then_inc(ev("logf"), 1)
            ka = slot(7, 1040).rearrange("p (n d) -> p n d", d=65)
            ps = full("c")
            free("c", dve.tensor_scalar(ka[:, :, 64], ps[:, 0:16], -1.0, None, ALU.mult))
            hsums(sm("rq16", 16), hq(16, 64), "q.1")
            hsums(sm("rk16", 16), hq(16, 64), "k.1")
            x1, base = ["fa", "ma1"], cnt["p"]
            soft(x1, {1: lambda: hsums(sm("cqm", 8), hq(8, P)),
                      3: lambda: (hsums(sm("rk8", 8), hq(8, P)), rows_out(x1, "fa", 0, base, xn[:, 0, 0:512])),
                      5: lambda: mem_scale(1),
                      8: lambda: rows_out(x1, "fa", 1, base, xn[:, 1, 0:512]),
                      9: lambda: [lo(f"fo.{tt}", MX, lambda t: t[:, 0:4, tt * P:(tt + 1) * P]) for tt in range(TT)]})
            for tt in range(TT):
                rows_out(x1, "ma1", tt, base, xn[:, tt, 512:1024])
            for tt in range(TT):
                lo(f"mo1.{tt}", MX, lambda t: t[:, 4:8, tt * P:(tt + 1) * P])
            norm_x("out1", 5)
            mlp_side(1, MLP_BLOCKS, 4, True, acts)
            for L in (2, 3):
                i = L - 2
                k = 6 + 2 * i
                norm_x(f"y{L - 1}", k)
                A4, B4 = sm("A4", 4), sm("B4", 4)
                if L == 2:
                    dve.memset(A4, 0.5)
                    step(dve.memset(B4, 0.5))
                else:
                    dve.tensor_tensor(A4, cg("lb", 4, 4), cg("lb", 0, 4), ALU.subtract).then_inc(ev("lbd"), 1)
                    dve.wait_ge(ev("lbt"), 1)
                    step(dve.tensor_scalar(A4, A4, 0.5, 0.5, ALU.mult, ALU.add))
                    step(dve.tensor_scalar(B4, A4, -0.5, 0.5, ALU.mult, ALU.add))
                    step(dve.tensor_tensor(A4, A4, B4, ALU.add))
                F, K, S, Q, X = slot(0, 1024), slot(1, 1024), slot(7, 1024), slot(8, 1024), slot(9, 1024)
                for tt in range(TT):
                    splits(fills[f"hf{L}T.{tt}"].pos + AHEAD)
                    dve.wait_ge(bank_free[fills[f"hf{L}T.{tt}"].bank], fills[f"hf{L}T.{tt}"].turn)
                    dve.wait_ge(bank_full[fills[f"hq{L}T.{tt}"].bank], fills[f"hq{L}T.{tt}"].turn)
                for h in range(4):
                    dve.tensor_scalar(F[:, h * T:(h + 1) * T], S[:, h * T:(h + 1) * T], B4[:, h:h + 1], A4[:, h:h + 1],
                                      ALU.mult, ALU.add)
                step(dve.tensor_scalar(sm("Bn", 4), B4, -1.0, None, ALU.mult))
                for h in range(4):
                    m = dve.tensor_scalar(K[:, h * T:(h + 1) * T], S[:, h * T:(h + 1) * T],
                                          sm("Bn", 4)[:, h:h + 1], B4[:, h:h + 1], ALU.mult, ALU.add)
                m.then_inc(ev("hfk"), 1)
                dve.wait_ge(ev("hfk"), i + 1)
                for tt in range(TT):
                    ps = full(f"hq{L}T.{tt}")
                    dve.wait_ge(ev("hqt"), 2 * i + tt + 1)
                    q = Q.rearrange("p (f t) -> p f t", f=4)[:, :, tt * P:(tt + 1) * P]
                    step(dve.tensor_scalar(q, q, 0.5, 0.5, ALU.mult, ALU.add))
                    free(f"hq{L}T.{tt}", dve.tensor_tensor(q, ps[:, :].rearrange("p (f t) -> p f t", f=4), q, ALU.mult))
                dve.wait_ge(bank_free[fills[f"hq{L}T.1"].bank], fills[f"hq{L}T.1"].turn)

                AT = slot(10, 1024).rearrange("p (g q) -> p g q", g=8)

                def take(l):
                    if l == 0:
                        for tt in range(TT):
                            ps = full(f"lev{L}.0.{tt}")
                            free(f"lev{L}.0.{tt}", dve.tensor_tensor(
                                AT[:, 4 * tt:4 * tt + 4, :], ps[:, :].rearrange("p (h q) -> p h q", h=4),
                                bc(ident, 1, 4), ALU.mult))
                        return
                    ps = full(f"lev{L}.{l}")
                    f = fills[f"lev{L}.{l - 1}" if l > 1 else f"lev{L}.0.1"]
                    dve.wait_ge(bank_free[f.bank], f.turn)
                    if l == LEVELS:
                        free(f"lev{L}.{l}", dve.tensor_copy(slot(11, 512), ps[:, :]))
                        return
                    m_ = 1 << (l - 1)
                    nb = 64 // m_
                    out = AT.rearrange("p g (n two m) -> p g n two m", two=2, m=m_)[:, :, :, 1, :]
                    msk = bc(cst("hmask", 64 * (l - 1), 64).bitcast(U32).rearrange("p (n m) -> p n m", m=m_), 1, 8)
                    data = ps[:, :].rearrange("p (g n m) -> p g n m", g=8, m=m_)
                    free(f"lev{L}.{l}", dve.copy_predicated(out, msk, data))

                for l in range(1, LEVELS + 1):
                    m_ = 1 << (l - 1)
                    v = lambda t: t.rearrange("p (n two m) -> p n two m", two=2, m=m_)
                    f = fills[f"lev{L}.{l - 1}" if l > 1 else f"lev{L}.0.1"]
                    splits(f.pos + AHEAD)
                    dve.wait_ge(bank_full[f.bank], f.turn)
                    dve.wait_ge(ev("lev"), 8 * i + l)
                    dve.tensor_tensor(v(X)[:, :, 0, :], v(K)[:, :, 0, :], v(S)[:, :, 0, :], ALU.mult)
                    dve.tensor_tensor(v(X)[:, :, 1, :], v(Q)[:, :, 1, :], v(F)[:, :, 1, :], ALU.mult).then_inc(ev("xlev"), 1)
                    take(l - 1)
                    if l == 5:
                        hsums(sm("rks", 4), hq(4, 64))
                    if l == 6:
                        dve.wait_ge(ev("xchi"), i + 1)
                        fl = [h[:, :, :, :].rearrange("p a b c -> p (a b c)").rearrange("p (kv c) -> p kv c", kv=2)[:, :, 0:608]
                              for h in HT]
                        dve.tensor_tensor(fl[1], windows_.rearrange("p (kv c) -> p kv c", kv=2),
                                          fl[0].bitcast(F32), ALU.subtract).then_inc(ev("xclo"), 1)
                        hsums(sm("rkw", 4), hq(4, 64))
                    if l == 7:
                        hsums(sm("rq16", 16), hq(16, 64))

                n30 = 2 * NCMP

                def ch_silu(kv):
                    ps = full(f"ch{L}.{kv}")
                    dve.wait_ge(ev("cht"), 2 * i + kv + 1)
                    c_ = chid[0:n30, kv * 256:(kv + 1) * 256]
                    step(dve.tensor_scalar(c_, c_, 0.5, 0.5, ALU.mult, ALU.add))
                    free(f"ch{L}.{kv}", dve.tensor_tensor(c_, ps[0:n30, 0:256], c_, ALU.mult))

                ch_silu(0)
                take(LEVELS)
                k0 = 6 + 5 * i
                dve.wait_ge(ev("hrstd"), k0 + 3)
                step(dve.tensor_scalar(sm("cq", 16), sm("rq16", 16), 0.125, None, ALU.mult))
                ch_silu(1)
                Z = Z_rows.rearrange("p (t g d) -> p t g d", t=2, g=12)
                Zr = Z_turned.rearrange("p (t g d) -> p t g d", t=2, g=12)
                tmp = slot(9, 768).rearrange("p (t g d) -> p t g d", t=2, g=12)
                cosb = bc(cst("cos").rearrange("p (t d) -> p t d", t=2), 2, 12)
                sinb = bc(cst("sin").rearrange("p (t d) -> p t d", t=2), 2, 12)
                dve.wait_ge(ev("zrow"), i + 1)
                dve.tensor_tensor(Zr[:, :, :, 0:32], Z[:, :, :, 0:32], cosb, ALU.mult)
                step(dve.tensor_tensor(tmp, Z[:, :, :, 32:64], sinb, ALU.mult))
                dve.tensor_tensor(Zr[:, :, :, 0:32], Zr[:, :, :, 0:32], tmp, ALU.subtract).then_inc(ev("ropeD"), 1)
                splits(fills[f"chT{L}"].pos + AHEAD)
                dve.wait_ge(bank_free[fills[f"chT{L}"].bank], fills[f"chT{L}"].turn)
                chT = sm("chT", 4 * n30).rearrange("p (j g n) -> p j g n", j=4, g=2)
                rep_ = chrep.rearrange("p (m g r n) -> p m g r n", m=2, g=2, r=4)
                for m_ in range(2):
                    m = dve.tensor_copy(rep_[:, m_], bc(chT[:, 2 + m_], 2, 4))
                m.then_inc(ev("chrep"), 1)
                hsums(sm("rkc", 1)[0:n30, :], sm("kct", 64)[0:n30, :], f"kc{L}")
                sg = slot(6, 1024)
                for tt in range(TT):
                    ps = full(f"hg{L}.{tt}")
                    dve.wait_ge(ev("hgt"), 2 * i + tt + 1)
                    g_ = sg[:, tt * BLK:(tt + 1) * BLK]
                    step(dve.tensor_scalar(g_, g_, 0.5, 0.5, ALU.mult, ALU.add))
                    free(f"hg{L}.{tt}", dve.tensor_tensor(g_, ps[:, :], g_, ALU.mult))
                dve.wait_ge(ev("ngt"), i + 1)
                step(dve.tensor_scalar(sm("ng", 48), sm("ng", 48), 0.5, 0.5, ALU.mult, ALU.add))
                for tt in range(TT):
                    ps = full(f"ho{L}.{tt}")
                    free(f"ho{L}.{tt}", dve.tensor_copy(slot(9, 1024)[:, tt * BLK:(tt + 1) * BLK], ps[:, :]))

                n120 = 8 * NCMP
                ps = full(f"vc{L}")
                free(f"vc{L}", dve.tensor_tensor(cvals()[0:n120, :].rearrange("p (h d) -> p h d", h=8),
                                                 bc(ps[0:n120, 0:64], 1, 8), bc(cst("bd")[0:n120, :], 2, 64), ALU.mult))

                def cmp_scores():
                    for tt in range(TT):
                        ps = full(f"cs{L}.{tt}")
                        cp = sm(f"cp{tt}", n120)
                        cv = cp.rearrange("p (h n) -> p h n", h=8)
                        free(f"cs{L}.{tt}", dve.tensor_tensor(cv, ps[:, 0:n120].rearrange("p (h n) -> p h n", h=8),
                                                              bc(cst("cadd", NCMP * tt, NCMP), 1, 8), ALU.add), True)
                        m8 = sm(f"cmax{tt}", 8)
                        step(dve.tensor_reduce(m8, cv, AX.X, ALU.max))
                        step(dve.tensor_tensor(cv, cv, bc(m8, 2, NCMP), ALU.subtract))
                        dve.tensor_tensor(cv, cv, bc(sm("cq", 16)[:, 8 * tt:8 * tt + 8], 2, NCMP), ALU.mult).then_inc(ev("cd"), 1)

                ng = sm("ng", 48).rearrange("p (t h b) -> p t h b", t=2, b=3)

                def hgrn_rows():
                    for tt in range(TT):
                        dve.wait_ge(ev("hon"), 2 * i + tt + 1)
                        dve.tensor_tensor(xn[:, tt, 0:512], slot(9, 1024)[:, tt * BLK:(tt + 1) * BLK],
                                          sg[:, tt * BLK:(tt + 1) * BLK], ALU.mult).then_inc(ev("hrow"), 1)
                    dve.wait_ge(ev("hrow"), 2 * i + 2)

                def cmp_probs():
                    for tt in range(TT):
                        dve.wait_ge(ev("cexp"), 2 * i + tt + 1)
                        cv = sm(f"cp{tt}", n120).rearrange("p (h n) -> p h n", h=8)
                        m8 = sm(f"cinv{tt}", 8)
                        step(dve.tensor_reduce(m8, cv, AX.X, ALU.add))
                        step(dve.reciprocal(m8, m8))
                        step(dve.tensor_tensor(m8, m8, ng[:, tt, :, 0], ALU.mult))
                        step(dve.tensor_tensor(cv, cv, bc(cst("cmul", NCMP * tt, NCMP), 1, 8), ALU.mult))
                        dve.tensor_tensor(cv, cv, bc(m8, 2, NCMP), ALU.mult).then_inc(ev("cprobs"), 1)

                tags, base = [f"sl{L}", f"sw{L}"], cnt["p"]

                def branch(b, tt):
                    tag = tags[b - 1]
                    ps = full(f"{tag}.o{tt}")
                    r = weights_of(tags, tag, tt, base, ng[:, tt, :, b])
                    dst = xn[:, tt, 512:1024]
                    t_ = dst if b == 1 else hrow[:, tt, :]
                    free(f"{tag}.o{tt}", dve.tensor_tensor(t_.rearrange("p (h d) -> p h d", h=8),
                                                           ps[:, :].rearrange("p (h d) -> p h d", h=8),
                                                           bc(r, 2, 64), ALU.mult), True)
                    if b == 1:
                        ps = full(f"co{L}.{tt}")
                        free(f"co{L}.{tt}", dve.tensor_tensor(dst, ps[:, :], dst, ALU.add), True)
                    else:
                        dve.tensor_tensor(dst, dst, t_, ALU.add).then_inc(ev("nrow"), 1)

                soft(tags, {0: cmp_scores, 1: cmp_probs, 2: lambda: hsums(sm("rho", 8), hq(8, P)),
                            4: lambda: branch(1, 0), 6: hgrn_rows, 8: lambda: branch(1, 1),
                            10: lambda: branch(2, 0),
                            11: lambda: [lo(f"hr{L}.{tt}", MX, lambda t: t[:, 0:4, tt * P:(tt + 1) * P])
                                         for tt in range(TT)]})
                branch(2, 1)
                for tt in range(TT):
                    lo(f"nr{L}.{tt}", MX, lambda t: t[:, 4:8, tt * P:(tt + 1) * P])
                norm_x(f"out{L}", k + 1)
                mlp_side(L, FFN_BLOCKS, 2, False, acts)
            for tt in range(TT):
                residual("y3", tt)


def _units(w, nk):
    k, n = w.shape
    b = min(n, BLK)
    return np.ascontiguousarray(
        w.reshape(k // (nk * P), nk, P, n // b, b).transpose(3, 0, 2, 1, 4).reshape(-1, P, nk * b))


def _constants():
    c = np.zeros((P, NCONST), np.float32)

    def put(name, v):
        at, w = CONST[name]
        v = np.asarray(v, np.float32).reshape(len(v), -1)
        c[:v.shape[0], at:at + w] = v

    s, t = np.arange(P)[:, None], np.arange(P)[None, :]
    put("ident", s == t)
    put("mask", np.concatenate([np.zeros((P, P)), np.where(t <= s, 0.0, NEG)], 1))
    put("tri", s <= t)
    put("ones", np.ones((P, P)))
    half = 32
    freqs = (np.float32(10000.0) ** (-np.arange(half, dtype=np.float32) / np.float32(half))).astype(np.float32)

    def angles(pos):
        return (pos.astype(np.float32)[:, None] * freqs[None, :]).astype(np.float32)

    ang = angles(np.arange(T)).reshape(TT, P, half).transpose(1, 0, 2)
    put("cos", np.cos(ang).reshape(P, -1))
    put("sin", np.sin(ang).reshape(P, -1))
    cend = np.arange(NCMP) * 16 + 31
    put("ccos", np.cos(angles(np.tile(cend, 2))))
    put("csin", np.sin(angles(np.tile(cend, 2))))
    seen = (cend[None, None, :] <= np.arange(T).reshape(TT, P, 1)).transpose(1, 0, 2)
    put("cadd", np.where(seen, 0.0, NEG))
    put("cmul", seen)
    lev = np.zeros((P, 7, 64))
    for l in range(7):
        m = 1 << l
        k, q = np.arange(P)[:, None], np.arange(64)[None, :]
        lev[:, l] = (k // (2 * m) == q // m) & (k % (2 * m) < m)
    put("hmask", lev)
    put("bd", (np.arange(8 * NCMP)[:, None] // NCMP) == np.arange(8)[None, :])
    return c


def kernel(**inputs):
    import numpy as _np
    import concourse.bacc as _bacc
    from concourse import mybir as _mybir
    from concourse.bass_utils import run_bass_kernel_spmd as _run

    v = {n: _np.asarray(t) for n, t in inputs.items()}
    cat = _np.concatenate
    arr = {"x": v["x"][0], "mem": v["mem"][0], "const": _constants()}
    arr["gains"] = cat([v["norm_mix"][0:1], v["norm_mem"][0:1], v["norm_mlp"][0:1], v["norm_mix"][1:2], v["norm_mem"][1:2],
                        v["norm_mlp"][1:2], v["norm_mix_2"][0:1], v["norm_ffn_2"][0:1], v["norm_mix_2"][1:2],
                        v["norm_ffn_2"][1:2]])
    arr["rowg"] = cat([v["xa_q_gain"][0], v["xa_k_gain"][0], v["xa_q_gain"][1], v["xa_k_gain"][1], v["fox_q_gain"][0],
                       v["fox_k_gain"][0], v["b_forget"][0]]
                      + [t for i in range(2) for t in (v["hg_gnorm_2"][i], v["q_gain_2"][i], v["k_gain_2"][i].ravel())])
    col = lambda t: t.reshape(4, P).T
    arr["colg"] = cat([v["conv_w"][0].reshape(4, 4, P).transpose(2, 1, 0).reshape(P, 16), col(v["conv_b"][0]),
                       col(v["b_rgate"][0]), col(v["b_igate"][0]), col(v["lru_lambda"][0]),
                       col(v["hg_lb_logits_2"][0]), col(v["hg_lb_logits_2"][1])]
                      + [v[n][i].reshape(16, P).T for i in range(2) for n in ("cmp_pe_k_2", "cmp_pe_v_2")], axis=1)
    wg = _np.zeros((P, 8, P), _np.float32)
    for g, n in enumerate(("w_rgate", "w_igate")):
        for b in range(8):
            r = 64 * (b % 2)
            wg[r:r + 64, 4 * g + b // 2, r:r + 64] = v[n][0, b]
    arr["wgate"] = wg.reshape(P, -1)
    arr["w2c"] = _np.stack([_np.stack([v[n][i].reshape(2, P, 64) for n in ("cmp_w2_k_2", "cmp_w2_v_2")])
                            for i in range(2)]).transpose(3, 0, 1, 2, 4).reshape(P, -1)
    wa = v["w_in_a"][0]
    arr["w_a"] = _units(cat([wa[:, 0:512], wa[:, 1024:1536], wa[:, 512:1024]], axis=1), 2)
    for i in range(2):
        arr[f"w_kv{i}"] = _units(v["w_mem_kv"][i], 2)
        arr[f"w_o{i}"] = _units(v["w_out"][i], 2)
        arr[f"w_m{i}"] = _units(v["w_mlp_in"][i], 2)
        w = v["w_mlp_out"][i]
        arr[f"w_n{i}"] = cat([_units(w[j * BLK:(j + 1) * BLK], 2) for j in range(MLP_BLOCKS)])
    wb = v["w_in_b"][0]
    arr["w_b"] = _units(cat([wb[:, 0:1536], wb[:, 1544:2056]], axis=1), 2)
    arr["w_f"] = wb[:, 1536:1544].reshape(1, KT, P, 8).transpose(0, 2, 1, 3).reshape(1, P, KT * 8)
    for L in (2, 3):
        i = L - 2
        w = v["w_in_2"][i]
        arr[f"w_c{L}"] = _units(cat([w[:, 512:1024], w[:, 0:512], w[:, 2560:3072], w[:, 2048:2560], w[:, 1024:1536],
                                     w[:, 1536:2048]], axis=1), 2)
        arr[f"w_d{L}"] = _units(w[:, 3072:3352], 2)
        arr[f"w_w{L}"] = cat([_units(v["cmp_w1_k_2"][i], 4), _units(v["cmp_w1_v_2"][i], 4)])
        arr[f"w_o{L}"] = _units(v["w_out_2"][i], 2)
        g = v["w_ffn_in_2"][i].reshape(D, 2, FFN_BLOCKS, FFN_HALF).transpose(0, 2, 1, 3).reshape(D, -1)
        arr[f"w_m{L}"] = _units(g, 2)
        w = v["w_ffn_out_2"][i]
        arr[f"w_n{L}"] = cat([_units(w[j * FFN_HALF:(j + 1) * FFN_HALF], 2) for j in range(FFN_BLOCKS)])

    nc = _bacc.Bacc("TRN2", target_bir_lowering=False, num_devices=1)
    arrays, args = {}, {}
    for n, t in arr.items():
        t = _np.ascontiguousarray(t)
        arrays[f"in_{n}"] = t
        args[n] = nc.dram_tensor(f"in_{n}", t.shape, _mybir.dt.from_np(t.dtype), kind="ExternalInput").ap()
    args["out"] = nc.dram_tensor("out_0", (T, D), _mybir.dt.float32, kind="ExternalOutput").ap()
    program(nc, args)
    r = _run(nc, [arrays], core_ids=[0])
    return r.results[0]["out_0"].reshape(1, T, D)
```
